# Optimizing a Trainium2 kernel written in Bass

```python
import math
import jax, jax.numpy as jnp
from jax import lax
import numpy as np

D_MODEL = 1024
BATCH = 1
SEQ = 512
DEPTH = 1

N_META = 16
CHUNK = 64
RET_HEADS = 4
RET_DK = 256
RET_DV = 512
RET_QK = RET_HEADS * RET_DK
RET_V = RET_HEADS * RET_DV
ROPE_BASE = 10000.0
DN_HEADS = 8
DN_DK = 128
DN_DV = 128
DN_QK = DN_HEADS * DN_DK
DN_V = DN_HEADS * DN_DV
CONV_WIDTH = 5
DN_CONV_CH = 2 * DN_QK + DN_V
PEER_HEADS = 8
PEER_NKEYS = 128
PEER_DQ = 256
PEER_TOPK = 16
N_EXPERTS = PEER_NKEYS * PEER_NKEYS
IN_WIDTH = 2 * RET_QK + 2 * RET_V + 2 * DN_QK + 2 * DN_V + 4 * DN_HEADS + 2 * D_MODEL
DEEPNORM_ALPHA = (2.0 * DEPTH) ** 0.25
DEEPNORM_BETA = (8.0 * DEPTH) ** -0.25
LN_EPS = 1e-5
RMS_EPS = 1e-6

kernel_name = "hybrid_retention_gdn_peer_encoder"

def layer_norm(x, g=None, b=None):
    xf = x.astype(jnp.float32)
    mu = jnp.mean(xf, -1, keepdims=True)
    var = jnp.mean(jnp.square(xf - mu), -1, keepdims=True)
    y = (xf - mu) * lax.rsqrt(var + LN_EPS)
    if g is not None:
        y = y * g.astype(jnp.float32) + b.astype(jnp.float32)
    return y.astype(x.dtype)

def rms_norm(x, g):
    xf = x.astype(jnp.float32)
    y = xf * lax.rsqrt(jnp.mean(jnp.square(xf), -1, keepdims=True) + RMS_EPS)
    return (y * g.astype(jnp.float32)).astype(x.dtype)

def l2norm(x):
    xf = x.astype(jnp.float32)
    return (xf * lax.rsqrt(jnp.sum(jnp.square(xf), -1, keepdims=True) + RMS_EPS)).astype(x.dtype)

def rotary(x, pos):
    d = x.shape[-1]
    inv = 1.0 / (ROPE_BASE ** (jnp.arange(0, d, 2, dtype=jnp.float32) / d))
    ang = pos.astype(jnp.float32)[:, None] * inv[None, :]
    cos = jnp.cos(ang)[None, :, None, :]
    sin = jnp.sin(ang)[None, :, None, :]
    x1, x2 = jnp.split(x.astype(jnp.float32), 2, axis=-1)
    return jnp.concatenate([x1 * cos - x2 * sin, x1 * sin + x2 * cos], -1).astype(x.dtype)

def depthwise_conv(x, w):
    W = w.shape[0]
    return lax.conv_general_dilated(
        x, w[:, None, :].astype(x.dtype), (1,), [((W - 1) // 2, W // 2)],
        dimension_numbers=('NWC', 'WIO', 'NWC'), feature_group_count=x.shape[-1])

def to_chunks(t, front):
    B, L = t.shape[:2]
    pad = (-L) % CHUNK
    widths = [(0, 0), (pad, 0) if front else (0, pad)] + [(0, 0)] * (t.ndim - 2)
    t = jnp.pad(t, widths)
    n = (L + pad) // CHUNK
    t = t.reshape((B, n, CHUNK) + t.shape[2:])
    return t.transpose((1, 0, 3, 2) + tuple(range(4, t.ndim)))

def from_chunks(o, L, front):
    N, B, H, C, d = o.shape
    o = o.transpose(1, 0, 3, 2, 4).reshape(B, N * C, H, d)
    pad = N * C - L
    return o[:, pad:] if front else o[:, :L]

def chunked_retention(q, k, v, logdec, strict):
    C = q.shape[-2]
    b = jnp.cumsum(logdec, axis=-1)
    mask = jnp.tril(jnp.ones((C, C), bool), -1 if strict else 0)
    diff = b[..., :, None] - b[..., None, :]
    dmat = jnp.where(mask, jnp.exp(jnp.where(mask, diff, 0.0)), 0.0)
    scores = jnp.einsum('nbhid,nbhjd->nbhij', q, k) * dmat
    o_intra = jnp.einsum('nbhij,nbhjv->nbhiv', scores, v)
    q_dec = q * jnp.exp(b)[..., None]
    k_dec = k * jnp.exp(b[..., -1:] - b)[..., None]
    chunk_dec = jnp.exp(b[..., -1])

    def step(S, inp):
        qd, kd, vc, cd = inp
        o = jnp.einsum('bhid,bhdv->bhiv', qd, S)
        S = S * cd[..., None, None] + jnp.einsum('bhjd,bhjv->bhdv', kd, vc)
        return S, o

    S0 = jnp.zeros(q.shape[1:3] + (q.shape[-1], v.shape[-1]), q.dtype)
    _, o_inter = lax.scan(step, S0, (q_dec, k_dec, v, chunk_dec))
    return o_intra + o_inter

def chunked_gated_delta(q, k, v, g, beta):
    C = q.shape[-2]
    dv = v.shape[-1]
    b = jnp.cumsum(g, axis=-1)
    incl = jnp.tril(jnp.ones((C, C), bool), 0)
    strict = jnp.tril(jnp.ones((C, C), bool), -1)
    diff = b[..., :, None] - b[..., None, :]
    dec = jnp.where(incl, jnp.exp(jnp.where(incl, diff, 0.0)), 0.0)
    k_beta = k * beta[..., None]
    A = jnp.where(strict, jnp.einsum('nbhid,nbhjd->nbhij', k_beta, k) * dec, 0.0)
    lhs = A + jnp.eye(C, dtype=A.dtype)
    rhs = jnp.concatenate([v * beta[..., None], k_beta * jnp.exp(b)[..., None]], -1)
    sol = lax.linalg.triangular_solve(lhs.astype(jnp.float32), rhs.astype(jnp.float32),
                                      left_side=True, lower=True, unit_diagonal=True).astype(q.dtype)
    u, w = sol[..., :dv], sol[..., dv:]
    attn = jnp.einsum('nbhid,nbhjd->nbhij', q, k) * dec
    q_dec = q * jnp.exp(b)[..., None]
    k_dec = k * jnp.exp(b[..., -1:] - b)[..., None]
    chunk_dec = jnp.exp(b[..., -1])

    def step(S, inp):
        qd, kd, ac, uc, wc, cd = inp
        v_new = uc - jnp.einsum('bhid,bhdv->bhiv', wc, S)
        o = jnp.einsum('bhid,bhdv->bhiv', qd, S) + jnp.einsum('bhij,bhjv->bhiv', ac, v_new)
        S = S * cd[..., None, None] + jnp.einsum('bhjd,bhjv->bhdv', kd, v_new)
        return S, o

    S0 = jnp.zeros(q.shape[1:3] + (q.shape[-1], dv), q.dtype)
    _, o = lax.scan(step, S0, (q_dec, k_dec, attn, u, w, chunk_dec))
    return o

def retention_branch(q, k, v, gate, pos, decay_logit):
    B, L, _ = q.shape
    q = rotary(q.reshape(B, L, RET_HEADS, RET_DK), pos)
    k = rotary(k.reshape(B, L, RET_HEADS, RET_DK), pos) * (RET_DK ** -0.5)
    v = v.reshape(B, L, RET_HEADS, RET_DV)
    logdec = jax.nn.log_sigmoid(decay_logit.astype(jnp.float32)).astype(q.dtype)
    out = jnp.zeros_like(v)
    for d in range(2):
        bwd = d == 1
        seq = (lambda t: jnp.flip(t, 1)) if bwd else (lambda t: t)
        ld = jnp.broadcast_to(logdec[d], (B, L, RET_HEADS))
        o = chunked_retention(to_chunks(seq(q), not bwd), to_chunks(seq(k), not bwd),
                              to_chunks(seq(v), not bwd), to_chunks(ld, not bwd), strict=bwd)
        out = out + seq(from_chunks(o, L, not bwd))
    o = layer_norm(out).reshape(B, L, RET_V)
    return o * jax.nn.silu(gate)

def deltanet_branch(q, k, v, z, a, bgate, conv_w, a_log, dt_bias, norm_g):
    B, L, _ = q.shape
    qkv = jax.nn.silu(depthwise_conv(jnp.concatenate([q, k, v], -1), conv_w))
    q, k, v = jnp.split(qkv, [DN_QK, 2 * DN_QK], axis=-1)
    q = l2norm(q.reshape(B, L, DN_HEADS, DN_DK)) * (DN_DK ** -0.5)
    k = l2norm(k.reshape(B, L, DN_HEADS, DN_DK))
    v = v.reshape(B, L, DN_HEADS, DN_DV)
    a = a.reshape(B, L, 2, DN_HEADS)
    bgate = bgate.reshape(B, L, 2, DN_HEADS)
    g = -jnp.exp(a_log) * jax.nn.softplus(a + dt_bias)
    beta = jax.nn.sigmoid(bgate)
    out = jnp.zeros_like(v)
    for d in range(2):
        bwd = d == 1
        seq = (lambda t: jnp.flip(t, 1)) if bwd else (lambda t: t)
        o = chunked_gated_delta(to_chunks(seq(q), not bwd), to_chunks(seq(k), not bwd),
                                to_chunks(seq(v), not bwd), to_chunks(seq(g[:, :, d]), not bwd),
                                to_chunks(seq(beta[:, :, d]), not bwd))
        out = out + seq(from_chunks(o, L, not bwd))
    o = rms_norm(out, norm_g).reshape(B, L, DN_V)
    return o * jax.nn.silu(z)

def hybrid_mixer(h, pos, w_in, ret_decay_logit, dn_conv, dn_a_log, dn_dt_bias, dn_norm_g, p_ret, p_dn, w_out):
    sizes = [RET_QK, RET_QK, RET_V, RET_V, DN_QK, DN_QK, DN_V, DN_V,
             2 * DN_HEADS, 2 * DN_HEADS, D_MODEL, D_MODEL]
    points = [int(s) for s in np.cumsum(sizes)[:-1]]
    proj = h @ w_in
    (rq, rk, rv, rg, dq, dk, dv, dz, da, db, gate_a, gate_b) = jnp.split(proj, points, axis=-1)
    y_ret = retention_branch(rq, rk, rv, rg, pos, ret_decay_logit)
    y_dn = deltanet_branch(dq, dk, dv, dz, da, db, dn_conv, dn_a_log, dn_dt_bias, dn_norm_g)
    merged = jax.nn.sigmoid(gate_a) * (y_ret @ p_ret) + jax.nn.sigmoid(gate_b) * (y_dn @ p_dn)
    return merged @ w_out

def peer_ffn(x, w_q, sub_keys, u_tab, v_tab):
    B, L, _ = x.shape
    K = PEER_TOPK
    q = (x @ w_q).reshape(B, L, PEER_HEADS, 2, PEER_DQ // 2)
    s = jnp.einsum('blhpd,hpnd->blhpn', q, sub_keys)
    s_top, i_top = lax.top_k(s, K)
    cand = (s_top[..., 0, :, None] + s_top[..., 1, None, :]).reshape(B, L, PEER_HEADS, K * K)
    best, flat = lax.top_k(cand, K)
    i1 = jnp.take_along_axis(i_top[..., 0, :], flat // K, axis=-1)
    i2 = jnp.take_along_axis(i_top[..., 1, :], flat % K, axis=-1)
    expert = i1 * PEER_NKEYS + i2
    gate = jax.nn.softmax(best.astype(jnp.float32), axis=-1).astype(x.dtype)

    def per_batch(args):
        xb, eb, gb = args

        def per_head(hargs):
            e, g = hargs
            act = jax.nn.gelu(jnp.einsum('ld,lkd->lk', xb, u_tab[e]), approximate=False)
            return jnp.einsum('lk,lkd->ld', act * g, v_tab[e])

        return jnp.sum(lax.map(per_head, (eb.transpose(1, 0, 2), gb.transpose(1, 0, 2))), axis=0)

    return lax.map(per_batch, (x, expert, gate))

def setup_inputs(seed: int = 0) -> dict:
    key = jax.random.key(seed)
    ks = jax.random.split(key, 24)
    f32 = jnp.float32

    def nrm(k, shape, scale):
        return jax.random.normal(k, shape, f32) * scale

    x = nrm(ks[0], (BATCH, SEQ, D_MODEL), 1.0)
    meta_tokens = nrm(ks[1], (N_META, D_MODEL), 1.0)
    emb_ln_g = 1.0 + nrm(ks[2], (D_MODEL,), 0.02)
    emb_ln_b = nrm(ks[3], (D_MODEL,), 0.02)
    w_in = nrm(ks[4], (DEPTH, D_MODEL, IN_WIDTH), D_MODEL ** -0.5)
    gam = 1.0 - 2.0 ** (-5.0 - jnp.arange(RET_HEADS, dtype=f32))
    ret_decay_logit = (jnp.log(gam) - jnp.log1p(-gam))[None, None, :] + nrm(ks[5], (DEPTH, 2, RET_HEADS), 0.05)
    dn_conv = nrm(ks[6], (DEPTH, CONV_WIDTH, DN_CONV_CH), CONV_WIDTH ** -0.5)
    dn_a_log = jnp.log(jax.random.uniform(ks[7], (DEPTH, 2, DN_HEADS), f32, 1.0, 16.0))
    dt = jnp.exp(jax.random.uniform(ks[8], (DEPTH, 2, DN_HEADS), f32, math.log(1e-3), math.log(1e-1)))
    dn_dt_bias = dt + jnp.log(-jnp.expm1(-dt))
    dn_norm_g = 1.0 + nrm(ks[9], (DEPTH, DN_DV), 0.02)
    p_ret = nrm(ks[10], (DEPTH, RET_V, D_MODEL), RET_V ** -0.5)
    p_dn = nrm(ks[11], (DEPTH, DN_V, D_MODEL), DN_V ** -0.5)
    w_out = nrm(ks[12], (DEPTH, D_MODEL, D_MODEL), DEEPNORM_BETA * D_MODEL ** -0.5)
    ln1_g = 1.0 + nrm(ks[13], (DEPTH, D_MODEL), 0.02)
    ln1_b = nrm(ks[14], (DEPTH, D_MODEL), 0.02)
    peer_wq = nrm(ks[15], (DEPTH, D_MODEL, PEER_HEADS * PEER_DQ), D_MODEL ** -0.5)
    peer_keys = nrm(ks[16], (DEPTH, PEER_HEADS, 2, PEER_NKEYS, PEER_DQ // 2), (PEER_DQ // 2) ** -0.5)
    peer_u = nrm(ks[17], (DEPTH, N_EXPERTS, D_MODEL), D_MODEL ** -0.5)
    peer_v = nrm(ks[18], (DEPTH, N_EXPERTS, D_MODEL), DEEPNORM_BETA)
    ln2_g = 1.0 + nrm(ks[19], (DEPTH, D_MODEL), 0.02)
    ln2_b = nrm(ks[20], (DEPTH, D_MODEL), 0.02)
    return {"x": x, "meta_tokens": meta_tokens, "emb_ln_g": emb_ln_g, "emb_ln_b": emb_ln_b,
            "w_in": w_in, "ret_decay_logit": ret_decay_logit, "dn_conv": dn_conv,
            "dn_a_log": dn_a_log, "dn_dt_bias": dn_dt_bias, "dn_norm_g": dn_norm_g,
            "p_ret": p_ret, "p_dn": p_dn, "w_out": w_out, "ln1_g": ln1_g, "ln1_b": ln1_b,
            "peer_wq": peer_wq, "peer_keys": peer_keys, "peer_u": peer_u, "peer_v": peer_v,
            "ln2_g": ln2_g, "ln2_b": ln2_b}

def reference(x, meta_tokens, emb_ln_g, emb_ln_b, w_in, ret_decay_logit, dn_conv, dn_a_log, dn_dt_bias,
              dn_norm_g, p_ret, p_dn, w_out, ln1_g, ln1_b, peer_wq, peer_keys, peer_u, peer_v, ln2_g, ln2_b):
    B = x.shape[0]
    meta = jnp.broadcast_to(meta_tokens[None].astype(x.dtype), (B, N_META, D_MODEL))
    h = layer_norm(jnp.concatenate([meta, x], axis=1), emb_ln_g, emb_ln_b)
    pos = jnp.arange(h.shape[1])
    for l in range(DEPTH):
        y = hybrid_mixer(h, pos, w_in[l], ret_decay_logit[l], dn_conv[l], dn_a_log[l], dn_dt_bias[l],
                         dn_norm_g[l], p_ret[l], p_dn[l], w_out[l])
        h = layer_norm(DEEPNORM_ALPHA * h + y, ln1_g[l], ln1_b[l])
        y = peer_ffn(h, peer_wq[l], peer_keys[l], peer_u[l], peer_v[l])
        h = layer_norm(DEEPNORM_ALPHA * h + y, ln2_g[l], ln2_b[l])
    return h[:, N_META:]


_drawn_inputs = setup_inputs


def setup_inputs(seed=0):
    import zlib

    import numpy as np

    out = dict(_drawn_inputs(seed))
    spreads = {}
    factors = {'dn_norm_g': 3.391, 'ln2_g': 2.836, 'ln2_b': 2.95}
    for name, (base, spread) in spreads.items():
        noise = np.random.default_rng([zlib.crc32(name.encode()), seed]).standard_normal(out[name].shape)
        drawn = base * np.exp(spread * noise) if base else spread * noise
        out[name] = __import__('jax').numpy.asarray(drawn.astype(out[name].dtype))
    for name, factor in factors.items():
        out[name] = (out[name] * factor).astype(out[name].dtype)
    return out
```

```python
from contextlib import ExitStack

import numpy as np

import concourse.bass as bass
from concourse import mybir
from concourse.alu_op_type import AluOpType as ALU

ACT = mybir.ActivationFunctionType
AX = mybir.AxisListType
F32 = mybir.dt.float32
BF16 = mybir.dt.bfloat16
U32 = mybir.dt.uint32

P = 128
D = 1024
KC = D // P
SEQ = 512
META = 16
TOK = SEQ + META
NT = SEQ // P
RH, RDK, RDV = 4, 256, 512
DH, DK = 8, 128
CW = 5
PH, NK, TOPK = 8, 128, 16
ALPHA = 2.0 ** 0.25
LN_EPS, RMS_EPS = 1e-5, 1e-6
STRIP = SEQ + (NT - 1) * P + META
LEVELS = 7


def tok_cols(t):
    return slice(0, META) if t == NT else slice(META + t * P, META + (t + 1) * P)


def rows(t):
    return META if t == NT else P


class Banks:

    def __init__(self, core, order, turns=1):
        self.uses, self.place = {}, {}
        self.full, self.free, self.base = core.full, core.free, list(core.products)
        for name, b in order:
            k = self.uses.get(b, 0)
            self.place[name] = (b, k)
            self.uses[b] = k + 1
        for b, n in self.uses.items():
            core.products[b] += n * turns

    def bank(self, name):
        return self.place[name][0]

    def count(self, name, turn, done):
        b, k = self.place[name]
        return turn * self.uses[b] + (self.base[b] + k + (1 if done else 0))

    def wait_free(self, eng, name, turn=0):
        eng.wait_ge(self.free[self.bank(name)], self.count(name, turn, False))

    def wait_full(self, eng, name, turn=0):
        eng.wait_ge(self.full[self.bank(name)], self.count(name, turn, True))

    def wait_used(self, eng, name, turn=0):
        eng.wait_ge(self.full[self.bank(name)], self.count(name, turn, False))

    def wait_read(self, eng, name, turn=0):
        eng.wait_ge(self.free[self.bank(name)], self.count(name, turn, True))

    def fills(self, name, ins):
        ins.then_inc(self.full[self.bank(name)], 1)

    def reads(self, name, ins):
        ins.then_inc(self.free[self.bank(name)], 1)


class Chain:

    def __init__(self, eng, sem, base=0, turn=0, per_turn=0):
        self.eng, self.sem, self.base, self.turn, self.per_turn, self.n = eng, sem, base, turn, per_turn, 0

    def __call__(self, ins):
        ins.then_inc(self.sem, 1)
        self.n += 1
        self.eng.wait_ge(self.sem, self.turn * self.per_turn + (self.base + self.n))

    def ends_turn(self):
        assert self.n == self.per_turn, self.n


class Core:

    def __init__(self, nc, ctx):
        self.nc, self.ctx = nc, ctx
        self.banks = [ctx.enter_context(nc.psum_tensor(f"bank{b}", [P, 512], F32)) for b in range(8)]
        self.full = [self.sem(f"bank{b}_full") for b in range(8)]
        self.free = [self.sem(f"bank{b}_free") for b in range(8)]
        self.products = [0] * 8

    def sem(self, name):
        return self.ctx.enter_context(self.nc.semaphore(name))


def sbuf(nc, ctx, name, shape, dtype=F32):
    return ctx.enter_context(nc.sbuf_tensor(name, shape, dtype))



def norm_stats(nc, link, src, n, width, stats, mv, eps):
    step = 512
    for j in range(width // step):
        link(nc.vector.bn_stats(stats[0:n, 6 * j:6 * j + 6], src[:, j * step:(j + 1) * step]))
    link(nc.vector.bn_aggr(mv[0:n, 0:2], stats[0:n, 0:6 * (width // step)]))
    link(nc.vector.tensor_scalar(mv[0:n, 1:2], mv[0:n, 1:2], eps, None, ALU.add))


def embed(core, a, h0, hT, ident):
    nc = core.nc
    with ExitStack() as ctx:
        hm = sbuf(nc, ctx, "embed_meta", [META, D])
        gain = sbuf(nc, ctx, "embed_gain", [P, D])
        bias = sbuf(nc, ctx, "embed_bias", [P, D])
        stats = sbuf(nc, ctx, "embed_stats", [P, NT + 1, 12])
        mv = sbuf(nc, ctx, "embed_mv", [P, NT + 1, 2])
        rstd = sbuf(nc, ctx, "embed_rstd", [P, NT + 1, 1])
        x_in, m_in, gb_in = core.sem("embed_x_in"), core.sem("embed_meta_in"), core.sem("embed_gb_in")
        id_in = core.sem("ident_in")
        chain, var_ok, std_ok, row_ok = (core.sem(f"embed_{n}") for n in ("chain", "var", "std", "row"))
        order = [(f"t{t}h{h}", (2 * t + h) % 8) for t in range(NT + 1) for h in range(2)]
        bk = Banks(core, order)

        def tile(t):
            return hm[:, :] if t == NT else h0[:, t, :]

        with nc.Block() as block:
            @block.sync
            def _(sp):
                for t in range(NT):
                    sp.dma_start(h0[:, t, :], a["x"][t * P:(t + 1) * P, :]).then_inc(x_in, 16)
                sp.dma_start(hm[:, :], a["meta"]).then_inc(m_in, 16)
                sp.dma_start(gain[:, :], a["emb_g"].partition_broadcast(P)).then_inc(gb_in, 16)
                sp.dma_start(bias[:, :], a["emb_b"].partition_broadcast(P)).then_inc(gb_in, 16)
                sp.dma_start(ident[:, :], a["ident"]).then_inc(id_in, 16)

            @block.vector
            def _(dve):
                link = Chain(dve, chain)
                dve.wait_ge(x_in, 16 * NT)
                dve.wait_ge(m_in, 16)
                for t in range(NT + 1):
                    n = rows(t)
                    norm_stats(nc, link, tile(t), n, D, stats[:, t, :], mv[:, t, :], LN_EPS)
                nc.vector.tensor_copy(rstd[0:1, 0, :], mv[0:1, 0, 1:2]).then_inc(var_ok, 1)
                dve.wait_ge(std_ok, 2)
                link(nc.vector.reciprocal(rstd[:, 0:NT, 0], rstd[:, 0:NT, 0]))
                link(nc.vector.reciprocal(rstd[0:META, NT, :], rstd[0:META, NT, :]))
                dve.wait_ge(gb_in, 32)
                for t in range(NT + 1):
                    n, row = rows(t), tile(t)
                    link(nc.vector.tensor_scalar(row, row, mv[0:n, t, 0:1], rstd[0:n, t, :],
                                                 ALU.subtract, ALU.mult))
                    link(nc.vector.tensor_tensor(row, row, gain[0:n, :], ALU.mult))
                    nc.vector.tensor_tensor(row, row, bias[0:n, :], ALU.add).then_inc(row_ok, 1)

            @block.scalar
            def _(act):
                act.wait_ge(var_ok, 1)
                nc.scalar.activation(rstd[:, 0:NT, 0], mv[:, 0:NT, 1], ACT.Sqrt).then_inc(std_ok, 1)
                nc.scalar.activation(rstd[0:META, NT, :], mv[0:META, NT, 1:2], ACT.Sqrt).then_inc(std_ok, 1)
                for t in range(NT + 1):
                    n = rows(t)
                    for h in range(2):
                        name = f"t{t}h{h}"
                        b = bk.bank(name)
                        bk.wait_full(act, name)
                        src = core.banks[b][:, :].rearrange("p (k n) -> p k n", k=4)[:, :, 0:n]
                        nc.scalar.activation(hT[:, 4 * h:4 * h + 4, tok_cols(t)], src,
                                             ACT.Copy).then_inc(bk.free[b], 1)

            @block.tensor
            def _(pe):
                pe.wait_ge(id_in, 16)
                for t in range(NT + 1):
                    n = rows(t)
                    pe.wait_ge(row_ok, t + 1)
                    for h in range(2):
                        name = f"t{t}h{h}"
                        b = bk.bank(name)
                        bk.wait_free(pe, name)
                        for k in range(4):
                            c = 4 * h + k
                            last = nc.tensor.transpose(core.banks[b][:, k * P:k * P + n],
                                                       tile(t)[:, c * P:(c + 1) * P], ident[0:n, 0:n])
                        last.then_inc(bk.full[b], 1)



def retention(core, a, hT, yT, ident):
    nc = core.nc
    with ExitStack() as ctx:
        w_qk = sbuf(nc, ctx, "ret_w_qk", [P, KC, 512])
        w_v = sbuf(nc, ctx, "ret_w_v", [P, KC, 512])
        w_g = sbuf(nc, ctx, "ret_w_g", [P, KC, 512])
        cos = sbuf(nc, ctx, "ret_cos", [P, TOK])
        sin = sbuf(nc, ctx, "ret_sin", [P, TOK])
        ahead = sbuf(nc, ctx, "ret_ahead", [P, STRIP])
        behind = sbuf(nc, ctx, "ret_behind", [P, STRIP])
        ld = sbuf(nc, ctx, "ret_logdec", [P, 2, RH])
        lw = sbuf(nc, ctx, "ret_logdec_work", [P, 2, RH])
        ldh = sbuf(nc, ctx, "ret_logdec_head", [P, 2])
        strip = sbuf(nc, ctx, "ret_strip", [P, STRIP])
        q = sbuf(nc, ctx, "ret_q", [P, 2, SEQ])
        k = sbuf(nc, ctx, "ret_k", [P, 2, TOK])
        tmp = sbuf(nc, ctx, "ret_tmp", [P, 2, SEQ])
        v = sbuf(nc, ctx, "ret_v", [P, NT, RDV])
        vm = sbuf(nc, ctx, "ret_v_meta", [META, RDV])
        gate = sbuf(nc, ctx, "ret_gate", [P, NT, RDV])
        sd = sbuf(nc, ctx, "ret_scores", [P, NT + 1, SEQ])
        y = sbuf(nc, ctx, "ret_y", [P, NT, RDV])
        stats = sbuf(nc, ctx, "ret_stats", [P, NT, 6])
        mv = sbuf(nc, ctx, "ret_mv", [P, NT, 2])
        rstd = sbuf(nc, ctx, "ret_rstd", [P, NT, 1])
        after_wait = sbuf(nc, ctx, "ret_after_wait", [P, 1])
        tables_in, logit_in, w_qk_in, w_v_in, w_g_in = (
            core.sem("ret_" + n) for n in ("tables_in", "logit_in", "w_qk_in", "w_v_in", "w_g_in"))
        rstd_ready = core.sem("ret_rstd_ready")
        act_steps, dve_steps, logit_ready, strip_arg, strip_ready, q_ready, k_ready, var_ready, std_ready, y_ready = (
            core.sem("ret_" + n) for n in ("act_steps", "dve_steps", "logit_ready", "strip_arg", "strip_ready",
                                           "q_ready", "k_ready", "var_ready", "std_ready", "y_ready"))
        order = ([("q0", 0), ("q1", 1), ("k0", 2), ("k1", 3), ("km", 4)]
                 + [("v0", 5), ("v1", 6), ("v2", 7), ("v3", 0), ("v4", 1)]
                 + [("g0", 2), ("g1", 3), ("g2", 4), ("g3", 5)]
                 + [("s0", 6), ("s1", 7), ("s2", 0), ("s3", 1), ("s4", 2)]
                 + [("o0", 3), ("o1", 4), ("o2", 5), ("o3", 6)]
                 + [("y0", 7), ("y1", 0), ("y2", 1), ("y3", 2)])
        bk = Banks(core, order, RH)

        def out(name):
            return core.banks[bk.bank(name)]

        def weights(name, h):
            return a[name][bass.ds(h, 1)].rearrange("o p k n -> (o p) k n")

        with nc.Block() as block:
            @block.sync
            def _(sp):
                sp.dma_start(w_qk[:, :, :], weights("w_ret_qk", 0)).then_inc(w_qk_in, 16)
                sp.dma_start(w_v[:, :, :], weights("w_ret_v", 0)).then_inc(w_v_in, 16)
                sp.dma_start(w_g[:, :, :], weights("w_ret_g", 0)).then_inc(w_g_in, 16)
                sp.dma_start(ld[:, :, :].rearrange("p a b -> p (a b)"),
                             a["ret_logit"].partition_broadcast(P)).then_inc(logit_in, 16)
                for table, name in ((cos, "cos"), (sin, "sin"), (ahead, "ahead"), (behind, "behind")):
                    sp.dma_start(table[:, :], a[name]).then_inc(tables_in, 16)
                with sp.Fori(0, RH - 1) as h:
                    bk.wait_full(sp, "km", h)
                    sp.dma_start(w_qk[:, :, :], weights("w_ret_qk", h + 1)).then_inc(w_qk_in, 16)
                    bk.wait_full(sp, "v4", h)
                    sp.dma_start(w_v[:, :, :], weights("w_ret_v", h + 1)).then_inc(w_v_in, 16)
                    bk.wait_full(sp, "g3", h)
                    sp.dma_start(w_g[:, :, :], weights("w_ret_g", h + 1)).then_inc(w_g_in, 16)

            @block.tensor
            def _(pe):
                with pe.Fori(0, RH) as h:
                    pe.wait_ge(w_qk_in, 16 * h + 16)
                    for c, name in enumerate(("q0", "q1", "k0", "k1")):
                        bk.wait_free(pe, name, h)
                        for kc in range(KC):
                            last = nc.tensor.matmul(out(name)[:, :], w_qk[:, kc, c * P:(c + 1) * P],
                                                    hT[:, kc, META:TOK], start=kc == 0, stop=kc == KC - 1)
                        bk.fills(name, last)
                    bk.wait_free(pe, "km", h)
                    for c in range(2):
                        for kc in range(KC):
                            last = nc.tensor.matmul(out("km")[:, c * META:(c + 1) * META],
                                                    w_qk[:, kc, (2 + c) * P:(3 + c) * P], hT[:, kc, 0:META],
                                                    start=kc == 0, stop=kc == KC - 1)
                    bk.fills("km", last)
                    for kind, arrived, w, tiles in (("v", w_v_in, w_v, NT + 1), ("g", w_g_in, w_g, NT)):
                        pe.wait_ge(arrived, 16 * h + 16)
                        for t in range(tiles):
                            name = f"{kind}{t}"
                            bk.wait_free(pe, name, h)
                            for kc in range(KC):
                                last = nc.tensor.matmul(out(name)[0:rows(t), :], hT[:, kc, tok_cols(t)],
                                                        w[:, kc, :], start=kc == 0, stop=kc == KC - 1)
                            bk.fills(name, last)
                    pe.wait_ge(q_ready, h + 1)
                    pe.wait_ge(k_ready, 2 * h + 2)
                    for t in range(NT + 1):
                        bk.wait_free(pe, f"s{t}", h)
                        for c in range(2):
                            last = nc.tensor.matmul(out(f"s{t}")[0:rows(t), :], k[:, c, tok_cols(t)],
                                                    q[:, c, :], start=c == 0, stop=c == 1)
                        bk.fills(f"s{t}", last)
                    for t in range(NT + 1):
                        bk.wait_read(pe, f"v{t}", h)
                        bk.wait_read(pe, f"s{t}", h)
                    for i in range(NT):
                        bk.wait_free(pe, f"o{i}", h)
                        for t in range(NT + 1):
                            n = rows(t)
                            value = vm[:, :] if t == NT else v[:, t, :]
                            last = nc.tensor.matmul(out(f"o{i}")[:, :], sd[0:n, t, i * P:(i + 1) * P],
                                                    value, start=t == 0, stop=t == NT)
                        bk.fills(f"o{i}", last)
                    for i in range(NT):
                        pe.wait_ge(y_ready, NT * h + (i + 1))
                        bk.wait_free(pe, f"y{i}", h)
                        for c in range(4):
                            last = nc.tensor.transpose(out(f"y{i}")[:, c * P:(c + 1) * P],
                                                       y[:, i, c * P:(c + 1) * P], ident[:, :])
                        bk.fills(f"y{i}", last)

            @block.scalar
            def _(act):
                act.wait_ge(logit_ready, 1)
                link = Chain(act, act_steps)
                link(nc.scalar.activation(lw[:, :, :], lw[:, :, :], ACT.Exp, scale=-1.0))
                link(nc.scalar.activation(lw[:, :, :], lw[:, :, :], ACT.Ln, bias=1.0))
                with act.Fori(0, RH) as h:
                    act.wait_ge(strip_arg, h + 1)
                    nc.scalar.activation(strip[:, :], strip[:, :], ACT.Exp).then_inc(strip_ready, 1)
                    for t in range(NT + 1):
                        bk.wait_full(act, f"v{t}", h)
                        dst = vm[:, :] if t == NT else v[:, t, :]
                        bk.reads(f"v{t}", nc.scalar.activation(dst, out(f"v{t}")[0:rows(t), :], ACT.Copy))
                    for t in range(NT):
                        bk.wait_full(act, f"g{t}", h)
                        bk.reads(f"g{t}", nc.scalar.activation(gate[:, t, :], out(f"g{t}")[:, :], ACT.Silu))
                    act.wait_ge(var_ready, NT * h + NT)
                    nc.scalar.activation(rstd[:, :, 0], mv[:, :, 1], ACT.Sqrt).then_inc(std_ready, 1)
                    for i in range(NT):
                        bk.wait_full(act, f"y{i}", h)
                        bk.reads(f"y{i}", nc.scalar.activation(
                            yT[:, bass.ds(4 * h, 4), i * P:(i + 1) * P],
                            out(f"y{i}")[:, :].rearrange("p (c n) -> p c n", c=4), ACT.Copy))

            @block.vector
            def _(dve):
                link = Chain(dve, dve_steps)
                dve.wait_ge(logit_in, 16)
                link(nc.vector.tensor_scalar(lw[:, :, :], ld[:, :, :], -1.0, None, ALU.mult))
                nc.vector.tensor_tensor(lw[:, :, :], lw[:, :, :], ld[:, :, :], ALU.max).then_inc(logit_ready, 1)
                link(nc.vector.tensor_scalar(ld[:, :, :], ld[:, :, :], -1.0, 0.0, ALU.mult, ALU.max))
                dve.wait_ge(act_steps, 2)
                link(nc.vector.tensor_tensor(ld[:, :, :], ld[:, :, :], lw[:, :, :], ALU.add))
                link(nc.vector.tensor_scalar(ld[:, :, :], ld[:, :, :], -1.0, None, ALU.mult))
                dve.wait_ge(tables_in, 64)
                before = link.n
                with dve.Fori(0, RH) as h:
                    link = Chain(dve, dve_steps, before, h, 16)
                    link(nc.vector.tensor_copy(ldh[:, :], ld[:, :, bass.ds(h, 1)].rearrange("p a o -> p (a o)")))
                    link(nc.vector.tensor_scalar(strip[:, :], ahead[:, :], ldh[:, 0:1], None, ALU.mult))
                    nc.vector.scalar_tensor_tensor(out=strip[:, :], in0=behind[:, :], scalar=ldh[:, 1:2],
                                                   in1=strip[:, :], op0=ALU.mult, op1=ALU.add)\
                        .then_inc(strip_arg, 1)
                    for names, dst, col, at, n in ((("q0", "q1"), q, 0, META, SEQ), (("k0", "k1"), k, META, META, SEQ),
                                                   (("km",), k, 0, 0, META)):
                        for name in names:
                            bk.wait_full(dve, name, h)
                        if len(names) == 2:
                            x1, x2 = out(names[0])[:, :], out(names[1])[:, :]
                        else:
                            x1, x2 = out("km")[:, 0:META], out("km")[:, META:2 * META]
                        cs, sn = cos[:, at:at + n], sin[:, at:at + n]
                        nc.vector.tensor_tensor(tmp[:, 0, 0:n], x1, cs, ALU.mult)
                        link(nc.vector.tensor_tensor(tmp[:, 1, 0:n], x2, sn, ALU.mult))
                        link(nc.vector.tensor_tensor(dst[:, 0, col:col + n], tmp[:, 0, 0:n], tmp[:, 1, 0:n],
                                                     ALU.subtract))
                        ins = nc.vector.tensor_tensor(tmp[:, 0, 0:n], x1, sn, ALU.mult)
                        if len(names) == 2:
                            bk.reads(names[0], ins)
                        bk.reads(names[-1], nc.vector.tensor_tensor(tmp[:, 1, 0:n], x2, cs, ALU.mult))
                        bk.wait_read(dve, names[-1], h)
                        nc.vector.tensor_tensor(dst[:, 1, col:col + n], tmp[:, 0, 0:n], tmp[:, 1, 0:n],
                                                ALU.add).then_inc(q_ready if dst is q else k_ready, 1)
                        if dst is q:
                            dve.wait_ge(q_ready, h + 1)
                        else:
                            dve.wait_ge(k_ready, 2 * h + (1 if len(names) == 2 else 2))
                    dve.wait_ge(strip_ready, h + 1)
                    for t in range(NT + 1):
                        n = rows(t)
                        bk.wait_full(dve, f"s{t}", h)
                        x0 = (NT - 1) * P + META if t == NT else (NT - 1 - t) * P
                        bk.reads(f"s{t}", nc.vector.scalar_tensor_tensor(
                            out=sd[0:n, t, :], in0=out(f"s{t}")[0:n, :], scalar=RDK ** -0.5,
                            in1=strip[0:n, x0:x0 + SEQ], op0=ALU.mult, op1=ALU.mult))
                    for i in range(NT):
                        bk.wait_full(dve, f"o{i}", h)
                        link(nc.vector.bn_stats(stats[:, i, :], out(f"o{i}")[:, :]))
                        nc.vector.memset(after_wait[:, :], 0.0)
                        link(nc.vector.bn_aggr(mv[:, i, :], stats[:, i, :]))
                        nc.vector.tensor_scalar(mv[:, i, 1:2], mv[:, i, 1:2], LN_EPS, None, ALU.add)\
                            .then_inc(var_ready, 1)
                    dve.wait_ge(std_ready, h + 1)
                    for t in range(NT):
                        bk.wait_read(dve, f"g{t}", h)
                    nc.vector.reciprocal(rstd[:, :, 0], rstd[:, :, 0]).then_inc(rstd_ready, 1)
                    dve.wait_ge(rstd_ready, h + 1)
                    for i in range(NT):
                        bk.reads(f"o{i}", nc.vector.tensor_scalar(
                            y[:, i, :], out(f"o{i}")[:, :], mv[:, i, 0:1], rstd[:, i, :],
                            ALU.subtract, ALU.mult))
                        bk.wait_read(dve, f"o{i}", h)
                        nc.vector.tensor_tensor(y[:, i, :], y[:, i, :], gate[:, i, :], ALU.mult)\
                            .then_inc(y_ready, 1)
                    link.ends_turn()



def branch_out(core, a, phase, hT, yT, chunks, gate_name, proj_name, merged, adds):
    nc = core.nc
    with ExitStack() as ctx:
        w_gate = sbuf(nc, ctx, phase + "_w_gate", [P, KC, 512])
        w_proj = sbuf(nc, ctx, phase + "_w_proj", [P, chunks, 512])
        gate = sbuf(nc, ctx, phase + "_gate", [P, NT, 512])
        gate_in, proj_in, merged_ready, gated = (
            core.sem(f"{phase}_{n}") for n in ("gate_in", "proj_in", "merged_ready", "gated"))
        halves = D // 512
        bk = Banks(core, [(f"g{t}", t) for t in range(NT)] + [(f"p{t}", NT + t) for t in range(NT)], halves)

        def out(name):
            return core.banks[bk.bank(name)]

        def weights(name, n):
            return a[name][bass.ds(n, 1)].rearrange("o p k n -> (o p) k n")

        with nc.Block() as block:
            @block.sync
            def _(sp):
                sp.dma_start(w_gate[:, :, :], weights(gate_name, 0)).then_inc(gate_in, 16)
                sp.dma_start(w_proj[:, :, :], weights(proj_name, 0)).then_inc(proj_in, 16)
                with sp.Fori(0, halves - 1) as n:
                    bk.wait_full(sp, f"g{NT - 1}", n)
                    sp.dma_start(w_gate[:, :, :], weights(gate_name, n + 1)).then_inc(gate_in, 16)
                    bk.wait_full(sp, f"p{NT - 1}", n)
                    sp.dma_start(w_proj[:, :, :], weights(proj_name, n + 1)).then_inc(proj_in, 16)

            @block.tensor
            def _(pe):
                with pe.Fori(0, halves) as n:
                    for kind, arrived, left, w, depth in (("g", gate_in, hT, w_gate, KC),
                                                          ("p", proj_in, yT, w_proj, chunks)):
                        pe.wait_ge(arrived, 16 * n + 16)
                        for t in range(NT):
                            name = f"{kind}{t}"
                            cols = tok_cols(t) if kind == "g" else slice(t * P, (t + 1) * P)
                            bk.wait_free(pe, name, n)
                            for c in range(depth):
                                last = nc.tensor.matmul(out(name)[:, :], left[:, c, cols], w[:, c, :],
                                                        start=c == 0, stop=c == depth - 1)
                            bk.fills(name, last)

            @block.scalar
            def _(act):
                with act.Fori(0, halves) as n:
                    for t in range(NT):
                        bk.wait_full(act, f"g{t}", n)
                        act.wait_ge(gated, NT * n + 1)
                        bk.reads(f"g{t}", nc.scalar.activation(gate[:, t, :], out(f"g{t}")[:, :], ACT.Sigmoid))

            @block.vector
            def _(dve):
                nc.vector.memset(gate[0:1, 0, 0:1], 0.0).then_inc(gated, 1)
                with dve.Fori(0, halves) as n:
                    for t in range(NT):
                        bk.wait_full(dve, f"p{t}", n)
                        bk.wait_read(dve, f"g{t}", n)
                        dst = merged[:, t, bass.ds(512 * n, 512)]
                        if adds:
                            bk.reads(f"p{t}", nc.vector.tensor_tensor(gate[:, t, :], out(f"p{t}")[:, :],
                                                                      gate[:, t, :], ALU.mult))
                            bk.wait_read(dve, f"p{t}", n)
                            nc.vector.tensor_tensor(dst, dst, gate[:, t, :], ALU.add).then_inc(gated, 1)
                        else:
                            bk.reads(f"p{t}", nc.vector.tensor_tensor(dst, out(f"p{t}")[:, :],
                                                                      gate[:, t, :], ALU.mult))
                            bk.wait_read(dve, f"p{t}", n)
                            nc.vector.tensor_copy(gate[0:1, t, 0:1], gate[0:1, t, 1:2]).then_inc(gated, 1)



DIRS = ("f", "b")


def delta_net(core, a, hT, yT, ident):
    nc = core.nc
    NC5 = NT + 1
    with ExitStack() as ctx:
        w = sbuf(nc, ctx, "dn_w", [P, KC, 512])
        w_ab = sbuf(nc, ctx, "dn_w_ab", [P, KC, 32])
        upper = sbuf(nc, ctx, "dn_upper", [P, P])
        lower = sbuf(nc, ctx, "dn_lower", [P, P])
        ones = sbuf(nc, ctx, "dn_ones", [P, P])
        masks = sbuf(nc, ctx, "dn_masks", [P, 2, LEVELS, P])
        conv_w = sbuf(nc, ctx, "dn_conv_w", [P, DH, 3 * CW])
        cw = sbuf(nc, ctx, "dn_conv_head", [P, 3 * CW])
        norm_g = sbuf(nc, ctx, "dn_norm_g", [P, DK])
        dtb = sbuf(nc, ctx, "dn_dt_bias", [P, 16])
        alog = sbuf(nc, ctx, "dn_a_log", [P, 16])
        raw = sbuf(nc, ctx, "dn_raw", [P, NC5, 32])
        g = sbuf(nc, ctx, "dn_g", [P, NC5, 16])
        g2 = sbuf(nc, ctx, "dn_g_work", [P, NC5, 16])
        NEGB, BETA, NEGEXP, BETAEND, END, G = range(6)
        scal = sbuf(nc, ctx, "dn_scal", [P, 6, NC5, 16])
        hs = sbuf(nc, ctx, "dn_scal_head", [P, 6 * NC5, 2])
        eps = sbuf(nc, ctx, "dn_eps", [P, 2])
        pre = sbuf(nc, ctx, "dn_conv_in", [P, 3, TOK + CW - 1])
        cv = sbuf(nc, ctx, "dn_conv_out", [P, 3, TOK])
        sq = sbuf(nc, ctx, "dn_squares", [P, 2, TOK])
        v_tok = sbuf(nc, ctx, "dn_v_tok", [P, NC5, DK])
        k_tok = sbuf(nc, ctx, "dn_k_tok", [P, NC5, DK])
        gz = sbuf(nc, ctx, "dn_gate_z", [P, NT, DK])
        gt = sbuf(nc, ctx, "dn_g_tri", [P, 2, NT, P])
        gtm = sbuf(nc, ctx, "dn_g_tri_meta", [P, META])
        dec = sbuf(nc, ctx, "dn_decay", [P, 2, NT, P])
        decm = sbuf(nc, ctx, "dn_decay_meta", [META, META])
        qd = sbuf(nc, ctx, "dn_q_decayed", [P, 2, SEQ])
        attn = sbuf(nc, ctx, "dn_attn", [P, 2, NT, P])
        lt = sbuf(nc, ctx, "dn_l", [P, 2, NT, P])
        ltm = sbuf(nc, ctx, "dn_l_meta", [META, META])
        lm = sbuf(nc, ctx, "dn_l_levels", [P, 2, LEVELS, NT, P])
        lmm = sbuf(nc, ctx, "dn_l_levels_meta", [P, 4, P])
        x = sbuf(nc, ctx, "dn_x", [P, 2, NT, P])
        xt = sbuf(nc, ctx, "dn_xt", [P, 2, NT, P])
        yy = sbuf(nc, ctx, "dn_lx", [P, 2, NT, P])
        xm = sbuf(nc, ctx, "dn_x_meta", [P, 3, P])
        state = sbuf(nc, ctx, "dn_state", [P, 2, DK])
        rhs = sbuf(nc, ctx, "dn_rhs", [P, 2, DK])
        vn = sbuf(nc, ctx, "dn_v_new", [P, 2, DK])
        v2 = sbuf(nc, ctx, "dn_v_end", [P, 2, DK])
        ysq = sbuf(nc, ctx, "dn_y_squares", [P, NT, DK])
        y = sbuf(nc, ctx, "dn_y", [P, NT, DK])
        rstd = sbuf(nc, ctx, "dn_rstd", [P, NT])
        names = ("w_in ab_in tables_in act_steps dve_steps sp_arg sp_log g_ready exp_ready conv_ready "
                 "silu_ready sq_ready q_ready k_ready gz_ready gtri_ready expb_ready dec_ready qd_ready "
                 "attn_ready masked_ready x_start ysq_ready ms_ready std_ready y_ready").split()
        s = {n: core.sem("dn_" + n) for n in names}
        order = [("q", 0), ("k", 1), ("v", 2), ("pm", 3), ("z", 4), ("bf", 3), ("bb", 4), ("bm", 5),
                 ("nq", 5), ("nk", 6), ("nm", 7), ("tv", 0), ("tk", 1), ("tm", 2), ("kk", 6), ("qk", 7),
                 ("kkm", 0)]
        for level in range(LEVELS):
            if level:
                order += [(f"yf{level}", 1), (f"yb{level}", 4)] + ([(f"ym{level}", 7)] if level < 4 else [])
                order += [(f"zf{level}", 2), (f"zb{level}", 5)] + ([(f"zm{level}", 7)] if level < 4 else [])
            if level < LEVELS - 1:
                order += [(f"xf{level}", 3), (f"xb{level}", 6)] + ([(f"xm{level}", 7)] if level < 3 else [])
        scan = [(("f", NT), ("b", NT - 1))] + [(("f", r), ("b", NT - 2 - r)) for r in range(NT - 1)] \
            + [(("f", NT - 1),)]
        first, final = {"f": NT, "b": NT - 1}, {"f": NT - 1, "b": 0}
        for steps in scan:
            order += [(f"r{d}{c}", 1 if d == "f" else 4) for d, c in steps if c != first[d]]
            order += [(f"w{d}{c}", 2 if d == "f" else 5) for d, c in steps]
            order += [(f"s{d}{c}", 3 if d == "f" else 6) for d, c in steps if c != final[d]]
        order += [("o", 0), ("ty", 7)]
        setup_bank = Banks(core, [("ab", 0), ("sums", 1)])
        bk = Banks(core, order, DH)

        def out(name):
            return core.banks[bk.bank(name)]

        def by_chunk(ap):
            return ap.rearrange("p (c n) -> p c n", c=NT)

        def over_chunks(ap):
            return ap.unsqueeze(1).broadcast_to([ap.shape[0], NT, ap.shape[-1]])

        def masked(level):
            return 3 * level + 3 if level < 4 else 12 + 2 * (level - 3)

        def wait_xt(eng, d, level, h):
            if level == 0:
                eng.wait_ge(s["x_start"], 3 * h + 3)
            else:
                bk.wait_read(eng, f"z{d}{level}", h)

        def sc(kind, c, d):
            n = rows(c)
            return hs[0:n, kind * NC5 + c, DIRS.index(d):DIRS.index(d) + 1]

        with nc.Block() as block:
            @block.sync
            def _(sp):
                sp.dma_start(w_ab[:, :, :], a["w_dn_ab"]).then_inc(s["ab_in"], 16)
                loads = ((upper[:, :], a["upper"]), (lower[:, :], a["lower"]),
                         (masks[:, :, :, :], a["masks"]), (conv_w[:, :, :], a["dn_conv"]),
                         (norm_g[:, :], a["dn_norm_g"].partition_broadcast(P)),
                         (dtb[:, :], a["dn_dt_bias"].partition_broadcast(P)),
                         (alog[:, :], a["dn_a_log"].partition_broadcast(P)))
                for dst, src in loads:
                    sp.dma_start(dst, src).then_inc(s["tables_in"], 16)
                sp.dma_start(w[:, :, :], a["w_dn"][0]).then_inc(s["w_in"], 16)
                with sp.Fori(0, DH - 1) as h:
                    bk.wait_full(sp, "z", h)
                    sp.dma_start(w[:, :, :], a["w_dn"][bass.ds(h + 1, 1)]
                                 .rearrange("o p k n -> (o p) k n")).then_inc(s["w_in"], 16)

            @block.tensor
            def _(pe):
                pe.wait_ge(s["ab_in"], 16)
                for t in range(NC5):
                    for kc in range(KC):
                        last = nc.tensor.matmul(core.banks[0][0:rows(t), 32 * t:32 * t + 32],
                                                hT[:, kc, tok_cols(t)], w_ab[:, kc, :],
                                                start=kc == 0, stop=kc == KC - 1)
                setup_bank.fills("ab", last)
                pe.wait_ge(s["tables_in"], 16 * 7)
                pe.wait_ge(s["g_ready"], 1)
                sums = core.banks[1]
                nc.tensor.matmul(sums[:, 0:32], upper[:, :], g[:, 0:NT, 0:8], start=True, stop=True)
                nc.tensor.matmul(sums[:, 32:64], lower[:, :], g[:, 0:NT, 8:16], start=True, stop=True)
                nc.tensor.matmul(sums[0:META, 64:72], upper[0:META, 0:META], g[0:META, NT, 0:8],
                                 start=True, stop=True)
                nc.tensor.matmul(sums[:, 128:192], ones[:, :], g[:, 0:NT, :], start=True, stop=True)
                setup_bank.fills("sums", nc.tensor.matmul(
                    sums[0:META, 200:208], ones[0:META, 0:META], g[0:META, NT, 0:8], start=True, stop=True))

                setup_bank.wait_read(pe, "sums")
                with pe.Fori(0, DH) as h:
                    pe.wait_ge(s["w_in"], 16 * h + 16)
                    for i, name in enumerate("qkv"):
                        bk.wait_free(pe, name, h)
                        for kc in range(KC):
                            last = nc.tensor.matmul(out(name)[:, :], w[:, kc, i * P:(i + 1) * P],
                                                    hT[:, kc, META:TOK], start=kc == 0, stop=kc == KC - 1)
                        bk.fills(name, last)
                    bk.wait_free(pe, "pm", h)
                    for i in range(3):
                        for kc in range(KC):
                            last = nc.tensor.matmul(out("pm")[:, i * META:(i + 1) * META],
                                                    w[:, kc, i * P:(i + 1) * P], hT[:, kc, 0:META],
                                                    start=kc == 0, stop=kc == KC - 1)
                    bk.fills("pm", last)
                    bk.wait_free(pe, "z", h)
                    for t in range(NT):
                        for kc in range(KC):
                            last = nc.tensor.matmul(out("z")[:, t * P:(t + 1) * P], hT[:, kc, tok_cols(t)],
                                                    w[:, kc, 3 * P:4 * P], start=kc == 0, stop=kc == KC - 1)
                    bk.fills("z", last)
                    pe.wait_ge(s["gtri_ready"], 3 * h + 3)
                    for i, d in enumerate(DIRS):
                        bk.wait_free(pe, "b" + d, h)
                        bk.fills("b" + d, nc.tensor.matmul(out("b" + d)[:, :], ones[:, :],
                                                           gt[:, i, :, :], start=True, stop=True))
                    bk.wait_free(pe, "bm", h)
                    bk.fills("bm", nc.tensor.matmul(out("bm")[:, 0:META], ones[:, :], gtm[:, :],
                                                    start=True, stop=True))
                    pe.wait_ge(s["sq_ready"], 2 * h + 2)
                    for name, i, c0, n in (("nq", 0, META, SEQ), ("nk", 1, META, SEQ), ("nm", 1, 0, META)):
                        bk.wait_free(pe, name, h)
                        bk.fills(name, nc.tensor.matmul(out(name)[:, 0:n], ones[:, :], sq[:, i, c0:c0 + n],
                                                        start=True, stop=True))
                    pe.wait_ge(s["silu_ready"], 3 * h + 3)
                    pe.wait_ge(s["k_ready"], h + 1)
                    for name, i in (("tv", 2), ("tk", 1)):
                        bk.wait_free(pe, name, h)
                        for t in range(NT):
                            last = nc.tensor.transpose(out(name)[:, t * P:(t + 1) * P], cv[:, i, tok_cols(t)],
                                                       ident[:, :])
                        bk.fills(name, last)
                    bk.wait_free(pe, "tm", h)
                    nc.tensor.transpose(out("tm")[0:META, 0:P], cv[:, 2, 0:META], ident[:, :])
                    bk.fills("tm", nc.tensor.transpose(out("tm")[0:META, P:2 * P], cv[:, 1, 0:META],
                                                       ident[:, :]))
                    pe.wait_ge(s["q_ready"], h + 1)
                    for name, i in (("kk", 1), ("qk", 0)):
                        bk.wait_free(pe, name, h)
                        for t in range(NT):
                            last = nc.tensor.matmul(out(name)[:, t * P:(t + 1) * P], cv[:, 1, tok_cols(t)],
                                                    cv[:, i, tok_cols(t)], start=True, stop=True)
                        bk.fills(name, last)
                    bk.wait_free(pe, "kkm", h)
                    bk.fills("kkm", nc.tensor.matmul(out("kkm")[0:META, 0:META], cv[:, 1, 0:META],
                                                     cv[:, 1, 0:META], start=True, stop=True))
                    for level in range(LEVELS):
                        parts = [("f", 0), ("b", 1)] + ([("m", 2)] if level < 4 else [])
                        if level:
                            pe.wait_ge(s["masked_ready"], 18 * h + masked(level))
                            for d, i in parts:
                                bk.wait_read(pe, f"x{d}{level - 1}", h)
                                bk.wait_free(pe, f"y{d}{level}", h)
                                if d == "m":
                                    last = nc.tensor.matmul(out("ym1")[:, 0:META], lmm[:, level, :],
                                                            xm[:, 0, 0:META], start=True, stop=True)
                                else:
                                    for t in range(NT):
                                        last = nc.tensor.matmul(out(f"y{d}{level}")[:, t * P:(t + 1) * P],
                                                                lm[:, i, level, t, :], x[:, i, t, :],
                                                                start=True, stop=True)
                                bk.fills(f"y{d}{level}", last)
                            for d, i in parts:
                                bk.wait_read(pe, f"y{d}{level}", h)
                                bk.wait_free(pe, f"z{d}{level}", h)
                                if d == "m":
                                    last = nc.tensor.matmul(out("ym1")[:, 0:META], xm[:, 2, :],
                                                            xm[:, 1, 0:META], start=True, stop=True)
                                else:
                                    for t in range(NT):
                                        last = nc.tensor.matmul(out(f"z{d}{level}")[:, t * P:(t + 1) * P],
                                                                yy[:, i, t, :], xt[:, i, t, :],
                                                                start=True, stop=True)
                                bk.fills(f"z{d}{level}", last)
                        if level < LEVELS - 1:
                            for d, i in parts:
                                if d == "m" and level == 3:
                                    continue
                                wait_xt(pe, d, level, h)
                                bk.wait_free(pe, f"x{d}{level}", h)
                                if d == "m":
                                    last = nc.tensor.transpose(out("ym1")[:, 0:P], xm[:, 1, :], ident[:, :])
                                else:
                                    for t in range(NT):
                                        last = nc.tensor.transpose(out(f"x{d}{level}")[:, t * P:(t + 1) * P],
                                                                   xt[:, i, t, :], ident[:, :])
                                bk.fills(f"x{d}{level}", last)
                    pe.wait_ge(s["qd_ready"], 2 * h + 2)
                    pe.wait_ge(s["attn_ready"], 2 * h + 2)
                    for name in ("tv", "tk", "tm"):
                        bk.wait_read(pe, name, h)
                    for d, level in (("f", LEVELS - 1), ("b", LEVELS - 1), ("m", 3)):
                        wait_xt(pe, d, level, h)
                    bk.wait_free(pe, "o", h)
                    opened = False
                    for steps in scan:
                        for d, c in steps:
                            i, n = DIRS.index(d), rows(c)
                            if c != first[d]:
                                previous = {"f": NT if c == 0 else c - 1, "b": c + 1}[d]
                                bk.wait_read(pe, f"s{d}{previous}", h)
                                bk.wait_free(pe, f"r{d}{c}", h)
                                bk.fills(f"r{d}{c}", nc.tensor.matmul(out(f"r{d}{c}")[0:n, 0:DK],
                                                                      cv[:, 1, tok_cols(c)], state[:, i, :],
                                                                      start=True, stop=True))
                                nc.tensor.matmul(out("o")[:, c * P:(c + 1) * P], qd[:, i, c * P:(c + 1) * P],
                                                 state[:, i, :], start=not opened, stop=False,
                                                 skip_group_check=True)
                                opened = True
                        for d, c in steps:
                            i, n = DIRS.index(d), rows(c)
                            left = xm[:, 1, :] if c == NT else xt[:, i, c, :]
                            right = v_tok[:, c, :]
                            if c != first[d]:
                                bk.wait_read(pe, f"r{d}{c}", h)
                                right = rhs[:, i, :]
                            bk.wait_free(pe, f"w{d}{c}", h)
                            bk.fills(f"w{d}{c}", nc.tensor.matmul(out(f"w{d}{c}")[:, 0:DK], left, right,
                                                                  start=True, stop=True))
                        for d, c in steps:
                            i, n = DIRS.index(d), rows(c)
                            bk.wait_read(pe, f"w{d}{c}", h)
                            if c != final[d]:
                                bk.wait_free(pe, f"s{d}{c}", h)
                                bk.fills(f"s{d}{c}", nc.tensor.matmul(out(f"s{d}{c}")[:, 0:DK],
                                                                      k_tok[0:n, c, :], v2[0:n, i, :],
                                                                      start=True, stop=True))
                            if c != NT:
                                last = nc.tensor.matmul(out("o")[:, c * P:(c + 1) * P], attn[:, i, c, :],
                                                        vn[:, i, :], start=not opened, stop=steps is scan[-1],
                                                        skip_group_check=True)
                                opened = True
                    bk.fills("o", last)
                    pe.wait_ge(s["y_ready"], h + 1)
                    bk.wait_free(pe, "ty", h)
                    for t in range(NT):
                        last = nc.tensor.transpose(out("ty")[:, t * P:(t + 1) * P], y[:, t, :], ident[:, :])
                    bk.fills("ty", last)

            @block.scalar
            def _(act):
                link = Chain(act, s["act_steps"])
                act.wait_ge(s["sp_arg"], 1)
                link(nc.scalar.activation(g2[:, :, :], g2[:, :, :], ACT.Exp))
                link(nc.scalar.activation(g2[:, :, :], g2[:, :, :], ACT.Ln, bias=1.0))
                link(nc.scalar.activation(alog[:, :], alog[:, :], ACT.Exp))
                nc.scalar.activation(scal[:, BETA, :, :], raw[:, :, 16:32], ACT.Sigmoid)\
                    .then_inc(s["sp_log"], 1)
                setup_bank.wait_read(act, "sums")
                nc.scalar.activation(scal[:, NEGEXP, :, :], scal[:, NEGB, :, :], ACT.Exp, scale=-1.0)
                nc.scalar.activation(scal[:, BETAEND, :, :], scal[:, BETAEND, :, :], ACT.Exp)
                nc.scalar.activation(scal[:, END, :, :], scal[:, END, :, :], ACT.Exp)\
                    .then_inc(s["exp_ready"], 1)
                with act.Fori(0, DH) as h:
                    for i, name in enumerate("qkv"):
                        bk.wait_full(act, name, h)
                        bk.reads(name, nc.scalar.activation(pre[:, i, 2 + META:2 + TOK], out(name)[:, :],
                                                            ACT.Copy))
                    bk.wait_full(act, "pm", h)
                    bk.reads("pm", nc.scalar.activation(
                        pre[:, :, 2:2 + META], out("pm")[:, 0:3 * META].rearrange("p (i n) -> p i n", i=3),
                        ACT.Copy))
                    bk.wait_full(act, "z", h)
                    bk.reads("z", nc.scalar.activation(gz[:, :, :], by_chunk(out("z")[:, :]), ACT.Silu))
                    for i, d in enumerate(DIRS):
                        bk.wait_full(act, "b" + d, h)
                        nc.scalar.activation(qd[:, i, :], out("b" + d)[:, :], ACT.Exp)\
                            .then_inc(s["expb_ready"], 1)
                    for name in ("bf", "bb", "bm"):
                        bk.wait_read(act, name, h)
                    nc.scalar.activation(dec[:, :, :, :], dec[:, :, :, :], ACT.Exp)\
                        .then_inc(s["dec_ready"], 1)
                    nc.scalar.activation(decm[:, :], decm[:, :], ACT.Exp).then_inc(s["dec_ready"], 1)
                    for i in range(3):
                        act.wait_ge(s["conv_ready"], 3 * h + (i + 1))
                        nc.scalar.activation(cv[:, i, :], cv[:, i, :], ACT.Silu).then_inc(s["silu_ready"], 1)
                        if i < 2:
                            act.wait_ge(s["silu_ready"], 3 * h + (i + 1))
                            nc.scalar.activation(sq[:, i, :], cv[:, i, :], ACT.Square)\
                                .then_inc(s["sq_ready"], 1)
                    act.wait_ge(s["sq_ready"], 2 * h + 2)
                    for name, i, c0, n in (("nq", 0, META, SEQ), ("nk", 1, META, SEQ), ("nm", 1, 0, META)):
                        bk.wait_full(act, name, h)
                        bk.reads(name, nc.scalar.activation(sq[:, i, c0:c0 + n], out(name)[:, 0:n], ACT.Sqrt,
                                                            bias=eps[:, i:i + 1],
                                                            scale=float(DK) if i == 0 else 1.0))
                    for name, dst in (("tv", v_tok), ("tk", k_tok)):
                        bk.wait_full(act, name, h)
                        bk.reads(name, nc.scalar.activation(dst[:, 0:NT, :], by_chunk(out(name)[:, :]),
                                                            ACT.Copy))
                    bk.wait_full(act, "tm", h)
                    nc.scalar.activation(v_tok[0:META, NT, :], out("tm")[0:META, 0:P], ACT.Copy)
                    bk.reads("tm", nc.scalar.activation(k_tok[0:META, NT, :], out("tm")[0:META, P:2 * P],
                                                        ACT.Copy))
                    for level in range(LEVELS):
                        parts = [("f", 0), ("b", 1)] + ([("m", 2)] if level < 4 else [])
                        if level:
                            for d, i in parts:
                                bk.wait_full(act, f"y{d}{level}", h)
                                if d == "m":
                                    ins = nc.scalar.activation(xm[0:META, 2, 0:META], out("ym1")[0:META, 0:META], ACT.Copy)
                                else:
                                    ins = nc.scalar.activation(yy[:, i, :, :], by_chunk(out(f"y{d}{level}")[:, :]),
                                                               ACT.Copy)
                                bk.reads(f"y{d}{level}", ins)
                        if level < LEVELS - 1:
                            for d, i in parts:
                                if d == "m" and level == 3:
                                    continue
                                bk.wait_full(act, f"x{d}{level}", h)
                                if d == "m":
                                    ins = nc.scalar.activation(xm[0:META, 0, 0:META], out("ym1")[0:META, 0:META], ACT.Copy)
                                else:
                                    ins = nc.scalar.activation(x[:, i, :, :], by_chunk(out(f"x{d}{level}")[:, :]),
                                                               ACT.Copy)
                                bk.reads(f"x{d}{level}", ins)
                    for d, c in (step for steps in scan for step in steps if step[0] == "b"):
                        bk.wait_full(act, f"w{d}{c}", h)
                        nc.scalar.activation(vn[:, 1, :], out(f"w{d}{c}")[:, 0:DK], ACT.Copy,
                                             scale=sc(BETA, c, d))
                        bk.reads(f"w{d}{c}", nc.scalar.activation(v2[:, 1, :], out(f"w{d}{c}")[:, 0:DK],
                                                                  ACT.Copy, scale=sc(BETAEND, c, d)))
                    bk.wait_full(act, "o", h)
                    nc.scalar.activation(ysq[:, :, :], by_chunk(out("o")[:, :]), ACT.Square)\
                        .then_inc(s["ysq_ready"], 1)
                    act.wait_ge(s["ms_ready"], h + 1)
                    nc.scalar.activation(rstd[:, :], rstd[:, :], ACT.Sqrt).then_inc(s["std_ready"], 1)
                    bk.wait_full(act, "ty", h)
                    bk.reads("ty", nc.scalar.activation(yT[:, bass.ds(h, 1), :].rearrange("p o n -> p (o n)"),
                                                        out("ty")[:, :], ACT.Copy))

            @block.gpsimd
            def _(pool):
                with pool.Fori(0, DH) as h:
                    pool.wait_ge(s["expb_ready"], 2 * h + 2)
                    pool.wait_ge(s["q_ready"], h + 1)
                    for i in range(2):
                        nc.gpsimd.tensor_tensor(qd[:, i, :], qd[:, i, :], cv[:, 0, META:TOK], ALU.mult)\
                            .then_inc(s["qd_ready"], 1)
                    bk.wait_read(pool, "kk", h)
                    bk.wait_read(pool, "kkm", h)
                    for level in range(LEVELS):
                        for i in range(2):
                            nc.gpsimd.tensor_tensor(lm[:, i, level, :, :], lt[:, i, :, :],
                                                    over_chunks(masks[:, i, level, :]), ALU.mult)\
                                .then_inc(s["masked_ready"], 1)
                        if level < 4:
                            nc.gpsimd.tensor_tensor(lmm[0:META, level, 0:META], ltm[:, :], masks[0:META, 0, level, 0:META],
                                                    ALU.mult).then_inc(s["masked_ready"], 1)
                    bk.wait_read(pool, "qk", h)
                    for i, keep in enumerate((upper, lower)):
                        nc.gpsimd.tensor_tensor(attn[:, i, :, :], attn[:, i, :, :],
                                                over_chunks(keep[:, :]), ALU.mult).then_inc(s["attn_ready"], 1)
                    bk.wait_read(pool, "z", h)
                    nc.gpsimd.tensor_tensor(gz[:, :, :], gz[:, :, :], over_chunks(norm_g[:, :]), ALU.mult)\
                        .then_inc(s["gz_ready"], 1)

            @block.vector
            def _(dve):
                link = Chain(dve, s["dve_steps"])
                nc.vector.memset(pre[:, :, :], 0.0)
                nc.vector.memset(raw[:, :, :], 0.0)
                nc.vector.memset(scal[:, :, :, :], 0.0)
                for zeroed in (gtm[:, :], lmm[:, :, :], xm[:, :, :], v_tok[:, NT, :]):
                    nc.vector.memset(zeroed, 0.0)
                nc.vector.memset(eps[:, 0:1], DK * RMS_EPS)
                nc.vector.memset(eps[:, 1:2], RMS_EPS)
                link(nc.vector.memset(ones[:, :], 1.0))
                setup_bank.wait_full(dve, "ab")
                nc.vector.tensor_copy(raw[:, 0:NT, :],
                                      core.banks[0][:, 0:NT * 32].rearrange("p (t n) -> p t n", t=NT))
                setup_bank.reads("ab", nc.vector.tensor_copy(raw[0:META, NT, :],
                                                             core.banks[0][0:META, NT * 32:NC5 * 32]))
                setup_bank.wait_read(dve, "ab")
                dve.wait_ge(s["tables_in"], 16 * 7)
                z = raw[:, :, 0:16]
                link(nc.vector.tensor_tensor(z, z, dtb[:, :].unsqueeze(1).broadcast_to([P, NC5, 16]), ALU.add))
                link(nc.vector.tensor_scalar(g2[:, :, :], z, -1.0, None, ALU.mult))
                nc.vector.tensor_tensor(g2[:, :, :], g2[:, :, :], z, ALU.min).then_inc(s["sp_arg"], 1)
                dve.wait_ge(s["sp_log"], 1)
                link(nc.vector.tensor_scalar(g[:, :, :], z, 0.0, None, ALU.max))
                link(nc.vector.tensor_tensor(g[:, :, :], g[:, :, :], g2[:, :, :], ALU.add))
                link(nc.vector.tensor_scalar(alog[:, :], alog[:, :], -1.0, None, ALU.mult))
                link(nc.vector.tensor_tensor(g[:, :, :], g[:, :, :],
                                             alog[:, :].unsqueeze(1).broadcast_to([P, NC5, 16]), ALU.mult))
                nc.vector.tensor_copy(scal[:, G, :, :], g[:, :, :]).then_inc(s["g_ready"], 1)
                setup_bank.wait_full(dve, "sums")
                dve.wait_ge(s["g_ready"], 1)
                sums = core.banks[1]
                running = ((scal[:, :, 0:NT, 0:8], sums[:, 0:32].rearrange("p (c n) -> p c n", c=NT),
                            sums[:, 128:192].rearrange("p (c n) -> p c n", c=NT)[:, :, 0:8]),
                           (scal[:, :, 0:NT, 8:16], sums[:, 32:64].rearrange("p (c n) -> p c n", c=NT),
                            sums[:, 128:192].rearrange("p (c n) -> p c n", c=NT)[:, :, 8:16]),
                           (scal[0:META, :, NT:NC5, 0:8], sums[0:META, 64:72].unsqueeze(1),
                            sums[0:META, 200:208].unsqueeze(1)))
                for dst, b, end in running:
                    link(nc.vector.tensor_scalar(dst[:, NEGB], b, -1.0, None, ALU.mult))
                    nc.vector.tensor_copy(dst[:, END], end)
                    ins = nc.vector.tensor_tensor(dst[:, BETAEND], dst[:, NEGB], end, ALU.add)
                setup_bank.reads("sums", ins)
                dve.wait_ge(s["exp_ready"], 1)
                nc.vector.tensor_tensor(scal[:, BETAEND, :, :], scal[:, BETAEND, :, :], scal[:, BETA, :, :],
                                        ALU.mult)
                link(nc.vector.tensor_scalar(scal[:, NEGEXP, :, :], scal[:, NEGEXP, :, :], -1.0, None,
                                             ALU.mult))
                before = link.n
                with dve.Fori(0, DH) as h:
                    link = Chain(dve, s["dve_steps"], before, h, 17)
                    nc.vector.tensor_copy(hs[:, :, :], scal[:, :, :, :].rearrange(
                        "p k c (d h) -> p (k c) d h", d=2)[:, :, :, bass.ds(h, 1)]
                        .rearrange("p k d o -> p k (d o)"))
                    link(nc.vector.tensor_copy(cw[:, :], conv_w[:, bass.ds(h, 1), :]
                                               .rearrange("p o n -> p (o n)")))
                    for i, (d, tri) in enumerate(zip(DIRS, (upper, lower))):
                        for c in range(NT):
                            ins = nc.vector.tensor_scalar(gt[:, i, c, :], tri[:, :], sc(G, c, d), None, ALU.mult)
                        ins.then_inc(s["gtri_ready"], 1)
                    nc.vector.tensor_scalar(gtm[0:META, :], upper[0:META, 0:META], sc(G, NT, "f"), None, ALU.mult)\
                        .then_inc(s["gtri_ready"], 1)
                    dve.wait_ge(s["expb_ready"], 2 * h + 2)
                    for i, d in enumerate(DIRS):
                        for c in range(NT):
                            ins = nc.vector.tensor_scalar(dec[:, i, c, :], out("b" + d)[:, c * P:(c + 1) * P],
                                                          sc(NEGB, c, d), 0.0, ALU.add, ALU.min)
                        bk.reads("b" + d, ins)
                    bk.wait_full(dve, "bm", h)
                    bk.wait_read(dve, "bb", h)
                    bk.reads("bm", nc.vector.tensor_scalar(decm[:, :], out("bm")[0:META, 0:META],
                                                           sc(NEGB, NT, "f"), 0.0, ALU.add, ALU.min))
                    bk.wait_read(dve, "bm", h)
                    bk.wait_read(dve, "pm", h)
                    for i in range(3):
                        link(nc.vector.tensor_scalar(cv[:, i, :], pre[:, i, 0:TOK], cw[:, CW * i:CW * i + 1],
                                                     None, ALU.mult))
                        for j in range(1, CW):
                            ins = nc.vector.scalar_tensor_tensor(
                                out=cv[:, i, :], in0=pre[:, i, j:j + TOK], scalar=cw[:, CW * i + j:CW * i + j + 1],
                                in1=cv[:, i, :], op0=ALU.mult, op1=ALU.add)
                            if j < CW - 1:
                                link(ins)
                        ins.then_inc(s["conv_ready"], 1)
                    bk.wait_read(dve, "nq", h)
                    link(nc.vector.reciprocal(sq[:, 0, META:TOK], sq[:, 0, META:TOK]))
                    nc.vector.tensor_tensor(cv[:, 0, META:TOK], cv[:, 0, META:TOK], sq[:, 0, META:TOK],
                                            ALU.mult).then_inc(s["q_ready"], 1)
                    bk.wait_read(dve, "nk", h)
                    bk.wait_read(dve, "nm", h)
                    link(nc.vector.reciprocal(sq[:, 1, :], sq[:, 1, :]))
                    nc.vector.tensor_tensor(cv[:, 1, :], cv[:, 1, :], sq[:, 1, :], ALU.mult)\
                        .then_inc(s["k_ready"], 1)
                    dve.wait_ge(s["dec_ready"], 2 * h + 2)
                    bk.wait_full(dve, "kk", h)
                    for i, d in enumerate(DIRS):
                        for c in range(NT):
                            ins = nc.vector.scalar_tensor_tensor(
                                out=lt[:, i, c, :], in0=out("kk")[:, c * P:(c + 1) * P], scalar=sc(BETA, c, d),
                                in1=dec[:, i, c, :], op0=ALU.mult, op1=ALU.mult)
                    bk.reads("kk", ins)
                    bk.wait_full(dve, "kkm", h)
                    bk.reads("kkm", nc.vector.scalar_tensor_tensor(
                        out=ltm[:, :], in0=out("kkm")[0:META, 0:META], scalar=sc(BETA, NT, "f"),
                        in1=decm[:, :], op0=ALU.mult, op1=ALU.mult))
                    bk.wait_full(dve, "qk", h)
                    for i in range(2):
                        ins = nc.vector.tensor_tensor(attn[:, i, :, :], by_chunk(out("qk")[:, :]),
                                                      dec[:, i, :, :], ALU.mult)
                    bk.reads("qk", ins)
                    dve.wait_ge(s["masked_ready"], 18 * h + masked(0))
                    for i in range(2):
                        nc.vector.tensor_tensor(xt[:, i, :, :], over_chunks(ident[:, :]), lm[:, i, 0, :, :],
                                                ALU.subtract).then_inc(s["x_start"], 1)
                    nc.vector.tensor_tensor(xm[0:META, 1, 0:META], ident[0:META, 0:META], lmm[0:META, 0, 0:META],
                                            ALU.subtract).then_inc(s["x_start"], 1)
                    for level in range(1, LEVELS):
                        for d, i in [("f", 0), ("b", 1)] + ([("m", 2)] if level < 4 else []):
                            name = f"z{d}{level}"
                            bk.wait_full(dve, name, h)
                            if d == "m":
                                bk.reads(name, nc.vector.tensor_tensor(xm[0:META, 1, 0:META], xm[0:META, 1, 0:META],
                                                                       out("ym1")[0:META, 0:META], ALU.subtract))
                            else:
                                bk.reads(name, nc.vector.tensor_tensor(xt[:, i, :, :], xt[:, i, :, :],
                                                                       by_chunk(out(name)[:, :]), ALU.subtract))
                    for steps in scan:
                        for d, c in steps:
                            if c != first[d]:
                                bk.wait_full(dve, f"r{d}{c}", h)
                                bk.reads(f"r{d}{c}", nc.vector.scalar_tensor_tensor(
                                    out=rhs[:, DIRS.index(d), :], in0=out(f"r{d}{c}")[:, 0:DK],
                                    scalar=sc(NEGEXP, c, d), in1=v_tok[:, c, :], op0=ALU.mult, op1=ALU.add))
                        for d, c in steps:
                            if d == "f":
                                n, name = rows(c), f"w{d}{c}"
                                bk.wait_full(dve, name, h)
                                nc.vector.tensor_scalar(vn[0:n, 0, :], out(name)[0:n, 0:DK], sc(BETA, c, d),
                                                        None, ALU.mult)
                                bk.reads(name, nc.vector.tensor_scalar(v2[0:n, 0, :], out(name)[0:n, 0:DK],
                                                                       sc(BETAEND, c, d), None, ALU.mult))
                        for d, c in steps:
                            if c != final[d]:
                                i, name = DIRS.index(d), f"s{d}{c}"
                                bk.wait_full(dve, name, h)
                                if c == first[d]:
                                    ins = nc.vector.tensor_copy(state[:, i, :], out(name)[:, 0:DK])
                                else:
                                    ins = nc.vector.scalar_tensor_tensor(
                                        out=state[:, i, :], in0=state[:, i, :], scalar=sc(END, c, d),
                                        in1=out(name)[:, 0:DK], op0=ALU.mult, op1=ALU.add)
                                bk.reads(name, ins)
                    dve.wait_ge(s["ysq_ready"], h + 1)
                    link(nc.vector.tensor_reduce(rstd[:, :], ysq[:, :, :], AX.X, ALU.add))
                    nc.vector.tensor_scalar(rstd[:, :], rstd[:, :], 1.0 / DK, RMS_EPS, ALU.mult, ALU.add)\
                        .then_inc(s["ms_ready"], 1)
                    dve.wait_ge(s["std_ready"], h + 1)
                    link(nc.vector.reciprocal(rstd[:, :], rstd[:, :]))
                    for c in range(NT):
                        ins = nc.vector.tensor_scalar(y[:, c, :], out("o")[:, c * P:(c + 1) * P],
                                                      rstd[:, c:c + 1], None, ALU.mult)
                    bk.reads("o", ins)
                    bk.wait_read(dve, "o", h)
                    dve.wait_ge(s["gz_ready"], h + 1)
                    nc.vector.tensor_tensor(y[:, :, :], y[:, :, :], gz[:, :, :], ALU.mult)\
                        .then_inc(s["y_ready"], 1)
                    link.ends_turn()



def mixer_out(core, a, h0, merged, h1T, ident):
    nc = core.nc
    with ExitStack() as ctx:
        w = sbuf(nc, ctx, "mix_w", [P, 2, KC, 512])
        mT = sbuf(nc, ctx, "mix_T", [P, KC, SEQ])
        gain = sbuf(nc, ctx, "mix_gain", [P, D])
        bias = sbuf(nc, ctx, "mix_bias", [P, D])
        stats = sbuf(nc, ctx, "mix_stats", [P, NT, 12])
        mv = sbuf(nc, ctx, "mix_mv", [P, NT, 2])
        rstd = sbuf(nc, ctx, "mix_rstd", [P, NT])
        w_in, gb_in, steps_done, var_ready, std_ready, row_ready = (
            core.sem("mix_" + n) for n in ("w_in", "gb_in", "steps", "var_ready", "std_ready", "row_ready"))
        order = [(f"m{t}{h}", (2 * t + h) % 8) for t in range(NT) for h in range(2)]
        order += [(f"o{t}{n}", (2 * t + n) % 8) for t in range(NT) for n in range(2)]
        order += [(f"h{t}{h}", (2 * t + h) % 8) for t in range(NT) for h in range(2)]
        bk = Banks(core, order)

        def out(name):
            return core.banks[bk.bank(name)]

        def transposed(pe, kind, src, t):
            for h in range(2):
                name = f"{kind}{t}{h}"
                bk.wait_free(pe, name)
                for c in range(4):
                    last = nc.tensor.transpose(out(name)[:, c * P:(c + 1) * P],
                                               src[:, t, (4 * h + c) * P:(4 * h + c + 1) * P], ident[:, :])
                bk.fills(name, last)

        def copied(act, kind, dst, t):
            for h in range(2):
                name = f"{kind}{t}{h}"
                bk.wait_full(act, name)
                bk.reads(name, nc.scalar.activation(dst[:, 4 * h:4 * h + 4, t * P:(t + 1) * P],
                                                    out(name)[:, :].rearrange("p (c n) -> p c n", c=4),
                                                    ACT.Copy))

        with nc.Block() as block:
            @block.sync
            def _(sp):
                for n in range(2):
                    sp.dma_start(w[:, n, :, :], a["w_out"][n]).then_inc(w_in, 16)
                sp.dma_start(gain[:, :], a["ln1_g"].partition_broadcast(P)).then_inc(gb_in, 16)
                sp.dma_start(bias[:, :], a["ln1_b"].partition_broadcast(P)).then_inc(gb_in, 16)

            @block.tensor
            def _(pe):
                for t in range(NT):
                    transposed(pe, "m", merged, t)
                pe.wait_ge(w_in, 32)
                for t in range(NT):
                    for h in range(2):
                        bk.wait_read(pe, f"m{t}{h}")
                    for n in range(2):
                        name = f"o{t}{n}"
                        bk.wait_free(pe, name)
                        for kc in range(KC):
                            last = nc.tensor.matmul(out(name)[:, :], mT[:, kc, t * P:(t + 1) * P], w[:, n, kc, :],
                                                    start=kc == 0, stop=kc == KC - 1)
                        bk.fills(name, last)
                for t in range(NT):
                    pe.wait_ge(row_ready, t + 1)
                    transposed(pe, "h", h0, t)

            @block.scalar
            def _(act):
                for t in range(NT):
                    copied(act, "m", mT, t)
                for t in range(NT):
                    act.wait_ge(var_ready, t + 1)
                    nc.scalar.activation(rstd[:, t:t + 1], mv[:, t, 1:2], ACT.Sqrt).then_inc(std_ready, 1)
                for t in range(NT):
                    copied(act, "h", h1T, t)

            @block.vector
            def _(dve):
                link = Chain(dve, steps_done)
                dve.wait_ge(gb_in, 32)
                for t in range(NT):
                    for n in range(2):
                        name = f"o{t}{n}"
                        bk.wait_full(dve, name)
                        row = h0[:, t, n * 512:(n + 1) * 512]
                        bk.reads(name, nc.vector.scalar_tensor_tensor(out=row, in0=row, scalar=ALPHA,
                                                                      in1=out(name)[:, :], op0=ALU.mult,
                                                                      op1=ALU.add))
                        bk.wait_read(dve, name)
                    for n in range(2):
                        ins = nc.vector.bn_stats(stats[:, t, 6 * n:6 * n + 6], h0[:, t, n * 512:(n + 1) * 512])
                    link(ins)
                    link(nc.vector.bn_aggr(mv[:, t, :], stats[:, t, :]))
                    nc.vector.tensor_scalar(mv[:, t, 1:2], mv[:, t, 1:2], LN_EPS, None, ALU.add)\
                        .then_inc(var_ready, 1)
                    dve.wait_ge(std_ready, t + 1)
                    link(nc.vector.reciprocal(rstd[:, t:t + 1], rstd[:, t:t + 1]))
                    row = h0[:, t, :]
                    link(nc.vector.tensor_scalar(row, row, mv[:, t, 0:1], rstd[:, t:t + 1],
                                                 ALU.subtract, ALU.mult))
                    link(nc.vector.tensor_tensor(row, row, gain[:, :], ALU.mult))
                    nc.vector.tensor_tensor(row, row, bias[:, :], ALU.add).then_inc(row_ready, 1)



def retrieve(core, a, h1T, picked, ident):
    nc = core.nc
    HP = 2 * PH
    LEAST = -3.0e38
    with ExitStack() as ctx:
        w = sbuf(nc, ctx, "top_w", [P, KC, 512])
        qT = sbuf(nc, ctx, "top_q", [P, HP, SEQ])
        keys = sbuf(nc, ctx, "top_keys", [P, HP, NK])
        iota = sbuf(nc, ctx, "top_iota", [P, TOPK])
        score = sbuf(nc, ctx, "top_score", [P, HP, NK])
        rest = sbuf(nc, ctx, "top_rest", [P, HP, NK])
        best = sbuf(nc, ctx, "top_best", [P, HP, TOPK])
        besti = sbuf(nc, ctx, "top_best_index", [P, HP, TOPK], U32)
        bestf = sbuf(nc, ctx, "top_best_index_f", [P, HP, TOPK])
        pairs = sbuf(nc, ctx, "top_pairs", [P, PH, TOPK, TOPK])
        left = sbuf(nc, ctx, "top_pairs_left", [P, PH, TOPK, TOPK])
        top = sbuf(nc, ctx, "top_of_pairs", [P, PH, TOPK])
        topi = sbuf(nc, ctx, "top_of_pairs_index", [P, PH, TOPK], U32)
        rank = sbuf(nc, ctx, "top_rank", [P, 2, PH, TOPK], U32)
        rankf = sbuf(nc, ctx, "top_rank_f", [P, 2, PH, TOPK])
        total = sbuf(nc, ctx, "top_total", [P, PH])
        after_wait = sbuf(nc, ctx, "top_after_wait", [P, 1])
        chosen = sbuf(nc, ctx, "top_chosen", [P, 3, PH, TOPK])
        w_in, keys_in, dve_steps, exp_arg, exp_ready, chosen_ready, turned = (
            core.sem("top_" + n) for n in ("w_in", "keys_in", "dve_steps", "exp_arg", "exp_ready",
                                           "chosen_ready", "turned"))
        qb = Banks(core, [(f"q{c}", c) for c in range(4)], 4)
        bk = Banks(core, [(f"s{c}", c) for c in range(4)] + [("t", 4)], NT)

        with nc.Block() as block:
            @block.sync
            def _(sp):
                sp.dma_start(w[:, :, :], a["peer_wq"][0]).then_inc(w_in, 16)
                sp.dma_start(keys[:, :, :], a["peer_keys"]).then_inc(keys_in, 16)
                sp.dma_start(iota[:, :], a["iota"][:, 0:TOPK]).then_inc(keys_in, 16)
                with sp.Fori(0, 3) as n:
                    qb.wait_full(sp, "q3", n)
                    sp.dma_start(w[:, :, :], a["peer_wq"][bass.ds(n + 1, 1)]
                                 .rearrange("o p k n -> (o p) k n")).then_inc(w_in, 16)

            @block.tensor
            def _(pe):
                with pe.Fori(0, 4) as n:
                    pe.wait_ge(w_in, 16 * n + 16)
                    for c in range(4):
                        qb.wait_free(pe, f"q{c}", n)
                        for kc in range(KC):
                            last = nc.tensor.matmul(core.banks[c][:, :], w[:, kc, c * P:(c + 1) * P],
                                                    h1T[:, kc, :], start=kc == 0, stop=kc == KC - 1)
                        qb.fills(f"q{c}", last)
                pe.wait_ge(keys_in, 32)
                for c in range(4):
                    qb.wait_read(pe, f"q{c}", 3)

                def scores(t):
                    for c in range(4):
                        bk.wait_free(pe, f"s{c}", t)
                        for j in range(4):
                            hp = 4 * c + j
                            last = nc.tensor.matmul(core.banks[c][:, j * NK:(j + 1) * NK],
                                                    qT[:, hp, t * P:(t + 1) * P], keys[:, hp, :],
                                                    start=True, stop=True)
                        bk.fills(f"s{c}", last)

                scores(0)
                for t in range(NT):
                    if t + 1 < NT:
                        scores(t + 1)
                    pe.wait_ge(chosen_ready, 3 * t + 3)
                    bk.wait_free(pe, "t", t)
                    for j in range(3):
                        last = nc.tensor.transpose(core.banks[4][:, j * P:(j + 1) * P],
                                                   chosen[:, j, :, :].rearrange("p h k -> p (h k)"), ident[:, :])
                    bk.fills("t", last)

            @block.scalar
            def _(act):
                with act.Fori(0, 4) as n:
                    for c in range(4):
                        qb.wait_full(act, f"q{c}", n)
                        qb.reads(f"q{c}", nc.scalar.activation(
                            qT[:, bass.ds(4 * n + c, 1), :].rearrange("p o n -> p (o n)"),
                            core.banks[c][:, :], ACT.Copy))
                with act.Fori(0, NT) as t:
                    for c in range(4):
                        bk.wait_full(act, f"s{c}", t)
                        act.wait_ge(exp_arg, t + 1)
                        bk.reads(f"s{c}", nc.scalar.activation(
                            score[:, 4 * c:4 * c + 4, :],
                            core.banks[c][:, :].rearrange("p (j n) -> p j n", j=4), ACT.Copy))
                    act.wait_ge(exp_arg, t + 2)
                    nc.scalar.activation(top[:, :, :], top[:, :, :], ACT.Exp).then_inc(exp_ready, 1)
                    bk.wait_full(act, "t", t)
                    bk.reads("t", nc.scalar.activation(
                        picked[:, :, bass.ds(P * t, P)],
                        core.banks[4][:, 0:3 * P].rearrange("p (j n) -> p j n", j=3), ACT.Copy))

            @block.vector
            def _(dve):
                nc.vector.memset(total[:, :], 0.0).then_inc(exp_arg, 1)
                dve.wait_ge(exp_arg, 1)
                dve.wait_ge(keys_in, 32)
                with dve.Fori(0, NT) as t:
                    link = Chain(dve, dve_steps, 0, t, 18)

                    def step(ins):
                        link(ins)
                        nc.vector.memset(after_wait[:, :], 0.0)

                    def best_of(values, reduced, n, out, index):
                        for i in range(n):
                            ins = nc.vector.max(out[:, i, 0:8], values[:, i, :])
                        step(ins)
                        for i in range(n):
                            nc.vector.max_index(index[:, i, 0:8], out[:, i, 0:8], values[:, i, :])
                            ins = nc.vector.match_replace(reduced[:, i, :], out[:, i, 0:8], values[:, i, :], LEAST)
                        step(ins)
                        for i in range(n):
                            ins = nc.vector.max(out[:, i, 8:16], reduced[:, i, :])
                        step(ins)
                        for i in range(n):
                            ins = nc.vector.max_index(index[:, i, 8:16], out[:, i, 8:16], reduced[:, i, :])
                        step(ins)

                    for c in range(4):
                        bk.wait_read(dve, f"s{c}", t)
                    nc.vector.memset(after_wait[:, :], 0.0)
                    best_of(score, rest, HP, best, besti)
                    by_head = best[:, :, :].rearrange("p (h s) k -> p h s k", s=2)
                    wide = [P, PH, TOPK, TOPK]
                    nc.vector.tensor_copy(bestf[:, :, :], besti[:, :, :])
                    step(nc.vector.tensor_tensor(pairs[:, :, :, :], by_head[:, :, 0, :].unsqueeze(3).broadcast_to(wide),
                                                 by_head[:, :, 1, :].unsqueeze(2).broadcast_to(wide), ALU.add))
                    best_of(pairs[:, :, :, :].rearrange("p h a b -> p h (a b)"),
                            left[:, :, :, :].rearrange("p h a b -> p h (a b)"), PH, top, topi)
                    nc.vector.tensor_scalar(rank[:, 0, :, :], topi[:, :, :], 4, None, ALU.logical_shift_right)
                    link(nc.vector.tensor_scalar(rank[:, 1, :, :], topi[:, :, :], 15, None, ALU.bitwise_and))
                    link(nc.vector.tensor_copy(rankf[:, :, :, :], rank[:, :, :, :]))
                    link(nc.vector.tensor_copy(total[:, :], top[:, :, 0]))
                    nc.vector.tensor_tensor(top[:, :, :], top[:, :, :],
                                            total[:, :].unsqueeze(2).broadcast_to([P, PH, TOPK]),
                                            ALU.subtract).then_inc(exp_arg, 1)
                    of_rank = bestf[:, :, :].rearrange("p (h s) k -> p h s k", s=2)
                    for side in range(2):
                        link(nc.vector.tensor_tensor(
                            left[:, :, :, :], rankf[:, side, :, :].unsqueeze(3).broadcast_to(wide),
                            iota[:, :].unsqueeze(1).unsqueeze(1).broadcast_to(wide), ALU.is_equal))
                        link(nc.vector.tensor_tensor(
                            left[:, :, :, :], left[:, :, :, :],
                            of_rank[:, :, side, :].unsqueeze(2).broadcast_to(wide), ALU.mult))
                        nc.vector.tensor_reduce(chosen[:, 1 + side, :, :], left[:, :, :, :], AX.X, ALU.add)\
                            .then_inc(chosen_ready, 1)
                        dve.wait_ge(chosen_ready, 3 * t + (side + 1))
                    dve.wait_ge(exp_ready, t + 1)
                    link(nc.vector.tensor_reduce(total[:, :], top[:, :, :], AX.X, ALU.add))
                    link(nc.vector.reciprocal(total[:, :], total[:, :]))
                    nc.vector.tensor_tensor(chosen[:, 0, :, :], top[:, :, :],
                                            total[:, :].unsqueeze(2).broadcast_to([P, PH, TOPK]),
                                            ALU.mult).then_inc(chosen_ready, 1)
                    dve.wait_ge(chosen_ready, 3 * t + 3)
                    link.ends_turn()


def spread(core, a, picked, weights_dram):
    nc = core.nc
    G = 4
    SLOTS = 4
    with ExitStack() as ctx:
        iota = sbuf(nc, ctx, "spread_iota", [P, NK])
        first = sbuf(nc, ctx, "spread_first", [P, SLOTS, G, NK])
        second = sbuf(nc, ctx, "spread_second", [P, SLOTS, G, NK])
        grid = sbuf(nc, ctx, "spread_grid", [P, NK, P])
        iota_in, first_ready, second_ready, stored = (
            core.sem("spread_" + n) for n in ("iota_in", "first_ready", "second_ready", "stored"))
        TURN = SLOTS * G
        turns = P // TURN
        bk = Banks(core, [(f"w{u}", u) for u in range(SLOTS)], SEQ // TURN)

        with nc.Block() as block:
            @block.sync
            def _(sp):
                sp.dma_start(iota[:, :], a["iota"]).then_inc(iota_in, 16)
                for t in range(NT):
                    for u in range(SLOTS):
                        bk.wait_read(sp, f"w{u}", turns * t + (turns - 1))
                    sp.dma_start(weights_dram.rearrange("b a t -> a b t")[:, :, t * P:(t + 1) * P],
                                 grid[:, :, :]).then_inc(stored, 16)
                sp.wait_ge(stored, 16 * NT)

            @block.vector
            def _(dve):
                dve.wait_ge(iota_in, 16)
                with dve.Fori(0, SEQ // TURN) as n:
                    for u in range(SLOTS):
                        bk.wait_used(dve, f"w{u}", n)
                        for j in range(G):
                            token = n * TURN + (u * G + j)
                            ins = nc.vector.tensor_scalar(
                                first[:, u, j, :], iota[:, :],
                                picked[:, 1, bass.ds(token, 1)], picked[:, 0, bass.ds(token, 1)],
                                ALU.is_equal, ALU.mult)
                        ins.then_inc(first_ready, 1)
                        for j in range(G):
                            token = n * TURN + (u * G + j)
                            ins = nc.vector.tensor_scalar(second[:, u, j, :], iota[:, :],
                                                          picked[:, 2, bass.ds(token, 1)], None,
                                                          ALU.is_equal)
                        ins.then_inc(second_ready, 1)

            @block.tensor
            def _(pe):
                with pe.Fori(0, SEQ // TURN) as n:
                    for u in range(SLOTS):
                        pe.wait_ge(first_ready, SLOTS * n + (u + 1))
                        pe.wait_ge(second_ready, SLOTS * n + (u + 1))
                        bk.wait_free(pe, f"w{u}", n)
                        for j in range(G):
                            last = nc.tensor.matmul(core.banks[u][:, j * NK:(j + 1) * NK], first[:, u, j, :],
                                                    second[:, u, j, :], start=True, stop=True)
                        bk.fills(f"w{u}", last)

            @block.scalar
            def _(act):
                for t in range(NT):
                    if t:
                        act.wait_ge(stored, 16 * t)
                    with act.Fori(0, turns) as n:
                        for u in range(SLOTS):
                            bk.wait_full(act, f"w{u}", n + t * turns)
                            bk.reads(f"w{u}", nc.scalar.activation(
                                grid[:, :, bass.ds(n * TURN + u * G, G)],
                                core.banks[u][:, :].rearrange("p (j n) -> p n j", j=G), ACT.Copy))



GROUP = 4
UNITS = 2 * NT


def experts(core, a, h1, h1T, acc, weights_dram):
    nc = core.nc
    with ExitStack() as ctx:
        xs = [sbuf(nc, ctx, f"ex_x_{n}", [P, KC, SEQ], BF16) for n in ("hi", "lo")]
        u32 = sbuf(nc, ctx, "ex_u", [P, 4, KC, P])
        v32 = sbuf(nc, ctx, "ex_v", [P, 4, D])
        wt = sbuf(nc, ctx, "ex_weights", [P, 4, SEQ])
        us = [sbuf(nc, ctx, f"ex_u_{n}", [P, 2, KC, P], BF16) for n in ("hi", "lo")]
        vs = [sbuf(nc, ctx, f"ex_v_{n}", [P, 2 * GROUP, D], BF16) for n in ("hi", "lo")]
        g32 = sbuf(nc, ctx, "ex_gated", [P, 4, SEQ])
        gs = [sbuf(nc, ctx, f"ex_gated_{n}", [P, 2 * GROUP, SEQ], BF16) for n in ("hi", "lo")]
        u_in = [core.sem(f"ex_u_in{i}") for i in range(4)]
        v_in = [core.sem(f"ex_v_in{i}") for i in range(4)]
        wt_in = [core.sem(f"ex_weights_in{i}") for i in range(4)]
        names = ("x_hi x_lo u_hi u_lo v_hi v_lo hidden gelu gated gated_hi gated_lo unit added").split()
        s = {n: core.sem("ex_" + n) for n in names}
        blocks = NK
        passes = ((0, 0), (0, 1), (1, 0))

        def split_x(act, dve):
            if act is not None:
                nc.scalar.activation(xs[0][:, :, :], h1T[:, :, :], ACT.Copy).then_inc(s["x_hi"], 1)
            if dve is not None:
                dve.wait_ge(s["x_hi"], 1)
                nc.vector.tensor_tensor(xs[1][:, :, :], h1T[:, :, :], xs[0][:, :, :], ALU.subtract)\
                    .then_inc(s["x_lo"], 1)

        def run(eng, first, step, last_units):
            for j in range(GROUP):
                step(j, j, first=True)
            with eng.Fori(0, (blocks - 2 * GROUP) // (2 * GROUP)) as turn:
                for j in range(2 * GROUP):
                    step(turn * (2 * GROUP) + (GROUP + j), GROUP + j)
            for j in range(GROUP):
                step(blocks - GROUP + j, blocks - GROUP + j, final=j == GROUP - 1)
            for j in range(GROUP):
                last_units(blocks + j, blocks + j)


        with nc.Block() as block:
            @block.sync
            def _(sp):
                def load(n, m, wait=True):
                    slot = m % 4
                    u_block, w_block, v_block = (block_of(dram, n) for dram in (a["peer_u"], weights_dram, a["peer_v"]))
                    if wait:
                        sp.wait_ge(s["u_lo"], n - 3)
                    sp.dma_start(u32[:, slot, :, :], u_block).then_inc(u_in[slot], 16)
                    if wait:
                        sp.wait_ge(s["gated"], n - 3)
                    sp.dma_start(wt[:, slot, :], w_block).then_inc(wt_in[slot], 16)
                    if wait:
                        sp.wait_ge(s["v_lo"], n - 3)
                    sp.dma_start(v32[:, slot, :], v_block).then_inc(v_in[slot], 16)

                def block_of(dram, n):
                    if isinstance(n, int):
                        return dram[n]
                    one = dram[bass.ds(n, 1)]
                    return one.rearrange("o p k n -> (o p) k n") if len(dram.shape) == 4 \
                        else one.rearrange("o p n -> (o p) n")

                for n in range(4):
                    load(n, n, wait=False)
                with sp.Fori(0, blocks // 4 - 1) as turn:
                    for j in range(4):
                        load(turn * 4 + (4 + j), j)

            @block.tensor
            def _(pe):
                def hidden(n, m):
                    bank = core.banks[m % 4]
                    pe.wait_ge(s["u_hi"], n + 1)
                    pe.wait_ge(s["u_lo"], n + 1)
                    if m >= 4:
                        pe.wait_ge(s["gelu"], n - 3)
                    for kc in range(KC):
                        for i, (l, r) in enumerate(passes):
                            last = nc.tensor.matmul(bank[:, :], us[l][:, m % 2, kc, :], xs[r][:, kc, :],
                                                    start=kc == 0 and i == 0, stop=kc == KC - 1 and i == 2)
                    last.then_inc(s["hidden"], 1)

                def units(n, m):
                    side = (m // GROUP - 1) % 2
                    for u in (2 * (m % GROUP), 2 * (m % GROUP) + 1):
                        half, t = divmod(u, NT)
                        bank = core.banks[4 + t]
                        pe.wait_ge(s["added"], 2 * n + (u - 2 * GROUP - 2 * (m % GROUP) + 1))
                        for j in range(GROUP):
                            slot = GROUP * side + j
                            for i, (l, r) in enumerate(passes):
                                last = nc.tensor.matmul(bank[:, :], gs[l][:, slot, t * P:(t + 1) * P],
                                                        vs[r][:, slot, half * 512:(half + 1) * 512],
                                                        start=j == 0 and i == 0,
                                                        stop=j == GROUP - 1 and i == 2)
                        last.then_inc(s["unit"], 1)

                def step(n, m, first=False, final=False):
                    hidden(n, m)
                    if not first:
                        if m % GROUP == 0:
                            pe.wait_ge(s["gated_hi"], n)
                            pe.wait_ge(s["gated_lo"], n)
                            pe.wait_ge(s["v_hi"], n)
                            pe.wait_ge(s["v_lo"], n)
                        units(n, m)

                def last_units(n, m):
                    if m % GROUP == 0:
                        pe.wait_ge(s["gated_hi"], n)
                        pe.wait_ge(s["gated_lo"], n)
                        pe.wait_ge(s["v_hi"], n)
                        pe.wait_ge(s["v_lo"], n)
                    units(n, m)

                pe.wait_ge(s["x_lo"], 1)
                run(pe, True, step, last_units)

            @block.scalar
            def _(act):
                def u_hi(n, m):
                    act.wait_ge(u_in[m % 4], arrived(n, m))
                    if m >= 2:
                        act.wait_ge(s["hidden"], n - 1)
                    nc.scalar.activation(us[0][:, m % 2, :, :], u32[:, m % 4, :, :], ACT.Copy)\
                        .then_inc(s["u_hi"], 1)

                def arrived(n, m):
                    return 4 * (n - m % 4) + 16

                def step(n, m, first=False, final=False):
                    if not final:
                        u_hi(n + 1, m + 1)
                    act.wait_ge(s["hidden"], n + 1)
                    if m >= 4:
                        act.wait_ge(s["gated_lo"], n - 3)
                    nc.scalar.activation(g32[:, m % 4, :], core.banks[m % 4][:, :], ACT.Gelu)\
                        .then_inc(s["gelu"], 1)
                    act.wait_ge(v_in[m % 4], arrived(n, m))
                    if m >= GROUP:
                        act.wait_ge(s["added"], 2 * n + (NT - 2 * (m % GROUP) - 2 * GROUP))
                    nc.scalar.activation(vs[0][:, m % 8, :], v32[:, m % 4, :], ACT.Copy).then_inc(s["v_hi"], 1)
                    act.wait_ge(s["gated"], n + 1)
                    nc.scalar.activation(gs[0][:, m % 8, :], g32[:, m % 4, :], ACT.Copy)\
                        .then_inc(s["gated_hi"], 1)

                split_x(act, None)
                u_hi(0, 0)
                run(act, True, step, lambda n, m: None)

            @block.vector
            def _(dve):
                def u_lo(n, m):
                    dve.wait_ge(s["u_hi"], n + 1)
                    if m >= 2:
                        dve.wait_ge(s["hidden"], n - 1)
                    nc.vector.tensor_tensor(us[1][:, m % 2, :, :], u32[:, m % 4, :, :], us[0][:, m % 2, :, :],
                                            ALU.subtract).then_inc(s["u_lo"], 1)

                def add_units(n, m):
                    for u in (2 * (m % GROUP), 2 * (m % GROUP) + 1):
                        half, t = divmod(u, NT)
                        dve.wait_ge(s["unit"], 2 * n + (u - 2 * GROUP - 2 * (m % GROUP) + 1))
                        part = acc[:, t, half * 512:(half + 1) * 512]
                        nc.vector.tensor_tensor(part, part, core.banks[4 + t][:, :], ALU.add)\
                            .then_inc(s["added"], 1)

                def step(n, m, first=False, final=False):
                    if not final:
                        u_lo(n + 1, m + 1)
                    dve.wait_ge(s["gelu"], n + 1)
                    dve.wait_ge(wt_in[m % 4], 4 * (n - m % 4) + 16)
                    nc.vector.tensor_tensor(g32[:, m % 4, :], g32[:, m % 4, :], wt[:, m % 4, :], ALU.mult)\
                        .then_inc(s["gated"], 1)
                    dve.wait_ge(s["v_hi"], n + 1)
                    nc.vector.tensor_tensor(vs[1][:, m % 8, :], v32[:, m % 4, :], vs[0][:, m % 8, :],
                                            ALU.subtract).then_inc(s["v_lo"], 1)
                    dve.wait_ge(s["gated_hi"], n + 1)
                    nc.vector.tensor_tensor(gs[1][:, m % 8, :], g32[:, m % 4, :], gs[0][:, m % 8, :],
                                            ALU.subtract).then_inc(s["gated_lo"], 1)
                    if not first:
                        add_units(n, m)

                for t in range(NT):
                    nc.vector.tensor_scalar(acc[:, t, :], h1[:, t, :], ALPHA, None, ALU.mult)\
                        .then_inc(s["added"], 1)
                dve.wait_ge(s["added"], NT)
                split_x(None, dve)
                u_lo(0, 0)
                run(dve, True, step, add_units)


def finish(core, a, acc, out):
    nc = core.nc
    with ExitStack() as ctx:
        gain = sbuf(nc, ctx, "fin_gain", [P, D])
        bias = sbuf(nc, ctx, "fin_bias", [P, D])
        stats = sbuf(nc, ctx, "fin_stats", [P, NT, 12])
        mv = sbuf(nc, ctx, "fin_mv", [P, NT, 2])
        rstd = sbuf(nc, ctx, "fin_rstd", [P, NT])
        gb_in, steps_done, var_ready, std_ready, row_ready, stored = (
            core.sem("fin_" + n) for n in ("gb_in", "steps", "var_ready", "std_ready", "row_ready", "stored"))
        with nc.Block() as block:
            @block.sync
            def _(sp):
                sp.dma_start(gain[:, :], a["ln2_g"].partition_broadcast(P)).then_inc(gb_in, 16)
                sp.dma_start(bias[:, :], a["ln2_b"].partition_broadcast(P)).then_inc(gb_in, 16)
                for t in range(NT):
                    sp.wait_ge(row_ready, t + 1)
                    sp.dma_start(out[t * P:(t + 1) * P, :], acc[:, t, :]).then_inc(stored, 16)
                sp.wait_ge(stored, 16 * NT)

            @block.scalar
            def _(act):
                act.wait_ge(var_ready, 1)
                nc.scalar.activation(rstd[:, :], mv[:, :, 1], ACT.Sqrt).then_inc(std_ready, 1)

            @block.vector
            def _(dve):
                link = Chain(dve, steps_done)
                for t in range(NT):
                    for n in range(2):
                        ins = nc.vector.bn_stats(stats[:, t, 6 * n:6 * n + 6], acc[:, t, n * 512:(n + 1) * 512])
                link(ins)
                for t in range(NT):
                    ins = nc.vector.bn_aggr(mv[:, t, :], stats[:, t, :])
                link(ins)
                nc.vector.tensor_scalar(mv[:, :, 1], mv[:, :, 1], LN_EPS, None, ALU.add).then_inc(var_ready, 1)
                dve.wait_ge(std_ready, 1)
                link(nc.vector.reciprocal(rstd[:, :], rstd[:, :]))
                dve.wait_ge(gb_in, 32)
                for t in range(NT):
                    row = acc[:, t, :]
                    link(nc.vector.tensor_scalar(row, row, mv[:, t, 0:1], rstd[:, t:t + 1],
                                                 ALU.subtract, ALU.mult))
                    link(nc.vector.tensor_tensor(row, row, gain[:, :], ALU.mult))
                    nc.vector.tensor_tensor(row, row, bias[:, :], ALU.add).then_inc(row_ready, 1)


def program(nc, a, out):
    with ExitStack() as ctx:
        core = Core(nc, ctx)
        weights_dram = nc.dram_tensor("expert_weights", [NK, NK, SEQ], F32).ap()
        ident = sbuf(nc, ctx, "ident", [P, P])
        h0 = sbuf(nc, ctx, "h0", [P, NT, D])
        hT = sbuf(nc, ctx, "hT", [P, KC, TOK])
        embed(core, a, h0, hT, ident)
        with ExitStack() as mixer:
            merged = sbuf(nc, mixer, "merged", [P, NT, D])
            with ExitStack() as part:
                yT = sbuf(nc, part, "ret_yT", [P, 4 * RH, SEQ])
                retention(core, a, hT, yT, ident)
                branch_out(core, a, "ret_out", hT, yT, 4 * RH, "w_gate_a", "p_ret", merged, False)
            with ExitStack() as part:
                yT = sbuf(nc, part, "dn_yT", [P, DH, SEQ])
                delta_net(core, a, hT, yT, ident)
                branch_out(core, a, "dn_out", hT, yT, DH, "w_gate_b", "p_dn", merged, True)
            h1T = hT[:, :, META:TOK]
            mixer_out(core, a, h0, merged, h1T, ident)
        with ExitStack() as peer:
            with ExitStack() as part:
                picked = sbuf(nc, part, "picked", [P, 3, SEQ])
                retrieve(core, a, h1T, picked, ident)
                spread(core, a, picked, weights_dram)
            acc = sbuf(nc, peer, "acc", [P, NT, D])
            experts(core, a, h0, h1T, acc, weights_dram)
            finish(core, a, acc, out)


def shape_constants():
    pos = np.arange(TOK, dtype=np.float32)
    inv = (1.0 / (np.float32(10000.0) ** (np.arange(0, RDK, 2, dtype=np.float32) / np.float32(RDK)))).astype(np.float32)
    ang = inv[:, None] * pos[None, :]
    delta = np.arange(STRIP)[None, :] - (NT - 1) * P - np.arange(P)[:, None]
    return {
        "ident": np.eye(P, dtype=np.float32),
        "cos": np.cos(ang).astype(np.float32),
        "sin": np.sin(ang).astype(np.float32),
        "ahead": np.maximum(delta, 0).astype(np.float32),
        "behind": np.maximum(-delta, 0).astype(np.float32),
        "upper": np.triu(np.ones((P, P), np.float32)),
        "lower": np.tril(np.ones((P, P), np.float32)),
        "masks": level_masks(),
        "iota": np.tile(np.arange(NK, dtype=np.float32), (P, 1)),
    }


def level_masks():
    j, i = np.arange(P)[:, None], np.arange(P)[None, :]
    out = np.zeros((P, 2, LEVELS, P), np.float32)
    for level in range(LEVELS):
        n = 2 ** level
        same = i // (2 * n) == j // (2 * n)
        out[:, 0, level] = same & (i // n > j // n)
        out[:, 1, level] = same & (i // n < j // n)
    return out


def laid_out(x, meta_tokens, emb_ln_g, emb_ln_b, w_in, ret_decay_logit, dn_conv, dn_a_log, dn_dt_bias,
             dn_norm_g, p_ret, p_dn, w_out, ln1_g, ln1_b, peer_wq, peer_keys, peer_u, peer_v, ln2_g, ln2_b):
    c = np.ascontiguousarray

    def rows_in_chunks(w):
        return w.reshape(-1, P, w.shape[-1]).transpose(1, 0, 2)

    def column_blocks(w, width):
        return c(np.stack([rows_in_chunks(w[:, n:n + width]) for n in range(0, w.shape[1], width)]))

    ends = np.cumsum([1024, 1024, 2048, 2048, 1024, 1024, 1024, 1024, 16, 16, 1024, 1024])
    rq, rk, rv, rg, dq, dk, dv, dz, da, db, ga, gb = np.split(w_in[0], ends[:-1], axis=1)
    return {
        "x": c(x[0]), "meta": c(meta_tokens), "emb_g": c(emb_ln_g), "emb_b": c(emb_ln_b),
        "ret_logit": c(ret_decay_logit[0].reshape(-1)),
        "w_ret_qk": c(np.stack([rows_in_chunks(np.concatenate([rq[:, h * RDK:(h + 1) * RDK],
                                                               rk[:, h * RDK:(h + 1) * RDK]], 1))
                                for h in range(RH)])),
        "w_ret_v": c(np.stack([rows_in_chunks(rv[:, h * RDV:(h + 1) * RDV]) for h in range(RH)])),
        "w_ret_g": c(np.stack([rows_in_chunks(rg[:, h * RDV:(h + 1) * RDV]) for h in range(RH)])),
        "w_gate_a": column_blocks(ga, 512), "w_gate_b": column_blocks(gb, 512),
        "p_ret": column_blocks(p_ret[0], 512), "p_dn": column_blocks(p_dn[0], 512),
        "w_dn": c(np.stack([rows_in_chunks(np.concatenate([m[:, h * DK:(h + 1) * DK]
                                                           for m in (dq, dk, dv, dz)], 1))
                            for h in range(DH)])),
        "w_dn_ab": c(rows_in_chunks(np.concatenate([da, db], 1))),
        "dn_conv": c(dn_conv[0].reshape(CW, 3, DH, P).transpose(3, 2, 1, 0).reshape(P, DH, 3 * CW)),
        "dn_norm_g": c(dn_norm_g[0]), "dn_dt_bias": c(dn_dt_bias[0].reshape(-1)),
        "dn_a_log": c(dn_a_log[0].reshape(-1)),
        "w_out": column_blocks(w_out[0], 512), "ln1_g": c(ln1_g[0]), "ln1_b": c(ln1_b[0]),
        "peer_wq": column_blocks(peer_wq[0], 512),
        "peer_keys": c(peer_keys[0].transpose(3, 0, 1, 2).reshape(P, 2 * PH, NK)),
        "peer_u": c(peer_u[0].reshape(NK, NK, KC, P).transpose(1, 3, 2, 0)),
        "peer_v": c(peer_v[0].reshape(NK, NK, D).transpose(1, 0, 2)),
        "ln2_g": c(ln2_g[0]), "ln2_b": c(ln2_b[0]),
        **shape_constants(),
    }


def kernel(**inputs):
    import concourse.bacc as bacc
    from concourse.bass_utils import run_bass_kernel_spmd as run

    nc = bacc.Bacc("TRN2", target_bir_lowering=False, num_devices=1)
    arrays, a = {}, {}
    for name, array in laid_out(**{n: np.asarray(v) for n, v in inputs.items()}).items():
        arrays[f"in_{name}"] = array
        a[name] = nc.dram_tensor(f"in_{name}", array.shape, mybir.dt.from_np(array.dtype),
                                 kind="ExternalInput").ap()
    out = nc.dram_tensor("out_0", (SEQ, D), F32, kind="ExternalOutput").ap()
    program(nc, a, out)
    result = run(nc, [arrays], core_ids=[0])
    return result.results[0]["out_0"].reshape(1, SEQ, D)
```

```python
from contextlib import ExitStack

import numpy as np

import concourse.bass as bass
from concourse import mybir
from concourse.alu_op_type import AluOpType as ALU

ACT = mybir.ActivationFunctionType
AX = mybir.AxisListType
F32 = mybir.dt.float32
BF16 = mybir.dt.bfloat16
U32 = mybir.dt.uint32

P = 128
D = 1024
KC = D // P
SEQ = 512
META = 16
TOK = SEQ + META
NT = SEQ // P
RH, RDK, RDV = 4, 256, 512
DH, DK = 8, 128
CW = 5
PH, NK, TOPK = 8, 128, 16
ALPHA = 2.0 ** 0.25
LN_EPS, RMS_EPS = 1e-5, 1e-6
STRIP = SEQ + (NT - 1) * P + META
LEVELS = 7


def tok_cols(t):
    return slice(0, META) if t == NT else slice(META + t * P, META + (t + 1) * P)


def rows(t):
    return META if t == NT else P


class Banks:

    def __init__(self, core, order, turns=1):
        self.uses, self.place = {}, {}
        self.full, self.free, self.base = core.full, core.free, list(core.products)
        for name, b in order:
            k = self.uses.get(b, 0)
            self.place[name] = (b, k)
            self.uses[b] = k + 1
        for b, n in self.uses.items():
            core.products[b] += n * turns

    def bank(self, name):
        return self.place[name][0]

    def count(self, name, turn, done):
        b, k = self.place[name]
        return turn * self.uses[b] + (self.base[b] + k + (1 if done else 0))

    def wait_free(self, eng, name, turn=0):
        eng.wait_ge(self.free[self.bank(name)], self.count(name, turn, False))

    def wait_full(self, eng, name, turn=0):
        eng.wait_ge(self.full[self.bank(name)], self.count(name, turn, True))

    def wait_used(self, eng, name, turn=0):
        eng.wait_ge(self.full[self.bank(name)], self.count(name, turn, False))

    def wait_read(self, eng, name, turn=0):
        eng.wait_ge(self.free[self.bank(name)], self.count(name, turn, True))

    def fills(self, name, ins):
        ins.then_inc(self.full[self.bank(name)], 1)

    def reads(self, name, ins):
        ins.then_inc(self.free[self.bank(name)], 1)


class Chain:

    def __init__(self, eng, sem, base=0, turn=0, per_turn=0):
        self.eng, self.sem, self.base, self.turn, self.per_turn, self.n = eng, sem, base, turn, per_turn, 0

    def __call__(self, ins):
        ins.then_inc(self.sem, 1)
        self.n += 1
        self.eng.wait_ge(self.sem, self.turn * self.per_turn + (self.base + self.n))

    def ends_turn(self):
        assert self.n == self.per_turn, self.n


class Core:

    def __init__(self, nc, ctx):
        self.nc, self.ctx = nc, ctx
        self.banks = [ctx.enter_context(nc.psum_tensor(f"bank{b}", [P, 512], F32)) for b in range(8)]
        self.full = [self.sem(f"bank{b}_full") for b in range(8)]
        self.free = [self.sem(f"bank{b}_free") for b in range(8)]
        self.products = [0] * 8

    def sem(self, name):
        return self.ctx.enter_context(self.nc.semaphore(name))


def sbuf(nc, ctx, name, shape, dtype=F32):
    return ctx.enter_context(nc.sbuf_tensor(name, shape, dtype))


def sbuf_pair(nc, ctx, name, shape):
    return [sbuf(nc, ctx, f"{name}_{half}", shape, BF16) for half in ("hi", "lo")]



PASSES = ((0, 0), (0, 1), (1, 0))


def pair_matmul(nc, out, left, right, start, stop):
    for i, (l, r) in enumerate(PASSES):
        last = nc.tensor.matmul(out, left[l], right[r], start=start and i == 0,
                                stop=stop and i == len(PASSES) - 1)
    return last


def view(pair, *at):
    return [half[at] for half in pair]


class Weights:

    RING = 4

    def __init__(self, core):
        self.core, self.nc, self.first = core, core.nc, 0
        self.arrived = [core.sem(f"w_slice_in{i}") for i in range(self.RING)]
        self.hi_done, self.lo_done = core.sem("w_hi_done"), core.sem("w_lo_done")

    def open(self, ctx, name, blocks, dram):
        self.raw = sbuf(self.nc, ctx, f"{name}_w_raw", [P, self.RING, KC, P])
        self.pair = sbuf_pair(self.nc, ctx, f"{name}_w", [P, blocks, 4, KC, P])
        self.dram, self.blocks = dram, blocks

    def close(self, slices):
        self.first += slices

    def load(self, sp, g, m, waits):
        source = self.dram[g] if isinstance(g, int) else \
            self.dram[bass.ds(g, 1)].rearrange("o p k n -> (o p) k n")
        if waits:
            sp.wait_ge(self.lo_done, g + (self.first - self.RING + 1))
        sp.dma_start(self.raw[:, m % self.RING, :, :], source).then_inc(self.arrived[m % self.RING], 16)

    def hi(self, act, g, m, slot):
        act.wait_ge(self.arrived[m % self.RING],
                    (16 // self.RING) * (g - m % self.RING) + ((16 // self.RING) * self.first + 16))
        self.nc.scalar.activation(self.pair[0][:, slot, m % 4, :, :], self.raw[:, m % self.RING, :, :],
                                  ACT.Copy).then_inc(self.hi_done, 1)

    def lo(self, pool, g, m, slot):
        pool.wait_ge(self.hi_done, g + (self.first + 1))
        self.nc.gpsimd.tensor_tensor(self.pair[1][:, slot, m % 4, :, :], self.raw[:, m % self.RING, :, :],
                                     self.pair[0][:, slot, m % 4, :, :], ALU.subtract).then_inc(self.lo_done, 1)

    def wait(self, pe, g):
        pe.wait_ge(self.lo_done, g + (self.first + 1))

    def columns(self, slot, c, kc):
        return view(self.pair, slice(None), slot, c, kc)

    def block(self, slot, kc):
        return view(self.pair, slice(None), slot, slice(None), kc)



def norm_stats(nc, link, src, n, width, stats, mv, eps):
    step = 512
    for j in range(width // step):
        link(nc.vector.bn_stats(stats[0:n, 6 * j:6 * j + 6], src[:, j * step:(j + 1) * step]))
    link(nc.vector.bn_aggr(mv[0:n, 0:2], stats[0:n, 0:6 * (width // step)]))
    link(nc.vector.tensor_scalar(mv[0:n, 1:2], mv[0:n, 1:2], eps, None, ALU.add))


def embed(core, a, h0, hT, ident):
    nc = core.nc
    with ExitStack() as ctx:
        hm = sbuf(nc, ctx, "embed_meta", [META, D])
        gain = sbuf(nc, ctx, "embed_gain", [P, D])
        bias = sbuf(nc, ctx, "embed_bias", [P, D])
        stats = sbuf(nc, ctx, "embed_stats", [P, NT + 1, 12])
        mv = sbuf(nc, ctx, "embed_mv", [P, NT + 1, 2])
        rstd = sbuf(nc, ctx, "embed_rstd", [P, NT + 1, 1])
        x_in, m_in, gb_in = core.sem("embed_x_in"), core.sem("embed_meta_in"), core.sem("embed_gb_in")
        id_in, hi_ready = core.sem("ident_in"), core.sem("embed_hi_ready")
        chain, var_ok, std_ok, row_ok = (core.sem(f"embed_{n}") for n in ("chain", "var", "std", "row"))
        order = [(f"t{t}h{h}", (2 * t + h) % 8) for t in range(NT + 1) for h in range(2)]
        bk = Banks(core, order)

        def tile(t):
            return hm[:, :] if t == NT else h0[:, t, :]

        with nc.Block() as block:
            @block.sync
            def _(sp):
                for t in range(NT):
                    sp.dma_start(h0[:, t, :], a["x"][t * P:(t + 1) * P, :]).then_inc(x_in, 16)
                sp.dma_start(hm[:, :], a["meta"]).then_inc(m_in, 16)
                sp.dma_start(gain[:, :], a["emb_g"].partition_broadcast(P)).then_inc(gb_in, 16)
                sp.dma_start(bias[:, :], a["emb_b"].partition_broadcast(P)).then_inc(gb_in, 16)
                sp.dma_start(ident[:, :], a["ident"]).then_inc(id_in, 16)

            @block.vector
            def _(dve):
                link = Chain(dve, chain)

                def low_halves(dve, t):
                    for h in range(2):
                        name, cols = f"t{t}h{h}", tok_cols(t)
                        dve.wait_ge(hi_ready, 2 * t + h + 1)
                        src = core.banks[bk.bank(name)][:, :].rearrange("p (k n) -> p k n", k=4)[:, :, 0:rows(t)]
                        bk.reads(name, nc.vector.tensor_tensor(hT[1][:, 4 * h:4 * h + 4, cols], src,
                                                               hT[0][:, 4 * h:4 * h + 4, cols], ALU.subtract))

                dve.wait_ge(x_in, 16 * NT)
                dve.wait_ge(m_in, 16)
                for t in range(NT + 1):
                    n = rows(t)
                    norm_stats(nc, link, tile(t), n, D, stats[:, t, :], mv[:, t, :], LN_EPS)
                nc.vector.tensor_copy(rstd[0:1, 0, :], mv[0:1, 0, 1:2]).then_inc(var_ok, 1)
                dve.wait_ge(std_ok, 2)
                link(nc.vector.reciprocal(rstd[:, 0:NT, 0], rstd[:, 0:NT, 0]))
                link(nc.vector.reciprocal(rstd[0:META, NT, :], rstd[0:META, NT, :]))
                dve.wait_ge(gb_in, 32)
                for t in range(NT + 1):
                    n, row = rows(t), tile(t)
                    link(nc.vector.tensor_scalar(row, row, mv[0:n, t, 0:1], rstd[0:n, t, :],
                                                 ALU.subtract, ALU.mult))
                    link(nc.vector.tensor_tensor(row, row, gain[0:n, :], ALU.mult))
                    nc.vector.tensor_tensor(row, row, bias[0:n, :], ALU.add).then_inc(row_ok, 1)
                    if t:
                        low_halves(dve, t - 1)
                low_halves(dve, NT)

            @block.scalar
            def _(act):
                act.wait_ge(var_ok, 1)
                nc.scalar.activation(rstd[:, 0:NT, 0], mv[:, 0:NT, 1], ACT.Sqrt).then_inc(std_ok, 1)
                nc.scalar.activation(rstd[0:META, NT, :], mv[0:META, NT, 1:2], ACT.Sqrt).then_inc(std_ok, 1)
                for t in range(NT + 1):
                    n = rows(t)
                    for h in range(2):
                        name = f"t{t}h{h}"
                        b = bk.bank(name)
                        bk.wait_full(act, name)
                        src = core.banks[b][:, :].rearrange("p (k n) -> p k n", k=4)[:, :, 0:n]
                        nc.scalar.activation(hT[0][:, 4 * h:4 * h + 4, tok_cols(t)], src,
                                             ACT.Copy).then_inc(hi_ready, 1)

            @block.tensor
            def _(pe):
                pe.wait_ge(id_in, 16)
                for t in range(NT + 1):
                    n = rows(t)
                    pe.wait_ge(row_ok, t + 1)
                    for h in range(2):
                        name = f"t{t}h{h}"
                        b = bk.bank(name)
                        bk.wait_free(pe, name)
                        for k in range(4):
                            c = 4 * h + k
                            last = nc.tensor.transpose(core.banks[b][:, k * P:k * P + n],
                                                       tile(t)[:, c * P:(c + 1) * P], ident[0:n, 0:n])
                        last.then_inc(bk.full[b], 1)



def retention(core, weights, a, hT, yT, work, ident):
    nc = core.nc
    with ExitStack() as ctx:
        cos = sbuf(nc, ctx, "ret_cos", [P, TOK])
        sin = sbuf(nc, ctx, "ret_sin", [P, TOK])
        ahead = sbuf(nc, ctx, "ret_ahead", [P, STRIP])
        behind = sbuf(nc, ctx, "ret_behind", [P, STRIP])
        ld = sbuf(nc, ctx, "ret_logdec", [P, 2, RH])
        lw = sbuf(nc, ctx, "ret_logdec_work", [P, 2, RH])
        ldh = sbuf(nc, ctx, "ret_logdec_head", [P, 2])
        strip = sbuf(nc, ctx, "ret_strip", [P, STRIP])
        q = sbuf(nc, ctx, "ret_q", [P, 2, SEQ])
        k = sbuf(nc, ctx, "ret_k", [P, 2, TOK])
        tmp = sbuf(nc, ctx, "ret_tmp", [P, 2, SEQ])
        v = sbuf(nc, ctx, "ret_v", [P, NT, RDV])
        vm = sbuf(nc, ctx, "ret_v_meta", [META, RDV])
        y, gate = work[:, :, 0:RDV], work[:, :, RDV:2 * RDV]
        sd = sbuf(nc, ctx, "ret_scores", [P, NT + 1, SEQ])
        stats = sbuf(nc, ctx, "ret_stats", [P, NT, 6])
        mv = sbuf(nc, ctx, "ret_mv", [P, NT, 2])
        rstd = sbuf(nc, ctx, "ret_rstd", [P, NT, 1])
        after_wait = sbuf(nc, ctx, "ret_after_wait", [P, 1])
        tables_in, logit_in, y_hi = (core.sem("ret_" + n) for n in ("tables_in", "logit_in", "y_hi"))
        rstd_ready = core.sem("ret_rstd_ready")
        act_steps, dve_steps, logit_ready, strip_arg, strip_ready, q_ready, k_ready, var_ready, std_ready, y_ready = (
            core.sem("ret_" + n) for n in ("act_steps", "dve_steps", "logit_ready", "strip_arg", "strip_ready",
                                           "q_ready", "k_ready", "var_ready", "std_ready", "y_ready"))
        order = ([("q0", 0), ("q1", 1), ("k0", 2), ("k1", 3), ("km", 4)]
                 + [("v0", 5), ("v1", 6), ("v2", 7), ("v3", 0), ("v4", 1)]
                 + [("g0", 2), ("g1", 3), ("g2", 4), ("g3", 5)]
                 + [("s0", 6), ("s1", 7), ("s2", 0), ("s3", 1), ("s4", 2)]
                 + [("o0", 3), ("o1", 4), ("o2", 5), ("o3", 6)]
                 + [("y0", 7), ("y1", 0), ("y2", 1), ("y3", 2)])
        bk = Banks(core, order, RH)

        def out(name):
            return core.banks[bk.bank(name)]

        blocks = (("qk", "km"), ("v", "v4"), ("g", "g3"))
        B = len(blocks)

        with nc.Block() as block:
            @block.sync
            def _(sp):
                sp.dma_start(ld[:, :, :].rearrange("p a b -> p (a b)"),
                             a["ret_logit"].partition_broadcast(P)).then_inc(logit_in, 16)
                for table, name in ((cos, "cos"), (sin, "sin"), (ahead, "ahead"), (behind, "behind")):
                    sp.dma_start(table[:, :], a[name]).then_inc(tables_in, 16)
                for g in range(4 * B):
                    weights.load(sp, g, g, g >= weights.RING)
                with sp.Fori(0, RH) as h:
                    for g in range(4 * B):
                        weights.load(sp, h * (4 * B) + (4 * B + g), g, True)

            @block.gpsimd
            def _(pool):
                with pool.Fori(0, RH + 1) as h:
                    for g in range(4 * B):
                        weights.lo(pool, h * (4 * B) + g, g, g // 4)

            @block.tensor
            def _(pe):
                with pe.Fori(0, RH) as h:
                    for c, name in enumerate(("q0", "q1", "k0", "k1")):
                        weights.wait(pe, h * (4 * B) + c)
                        bk.wait_free(pe, name, h)
                        if name == "k0":
                            bk.wait_free(pe, "km", h)
                        for kc in range(KC):
                            left, ends = weights.columns(0, c, kc), dict(start=kc == 0, stop=kc == KC - 1)
                            last = pair_matmul(nc, out(name)[:, :], left,
                                               view(hT, slice(None), kc, slice(META, TOK)), **ends)
                            if kc == KC - 1:
                                bk.fills(name, last)
                            if c >= 2:
                                last = pair_matmul(nc, out("km")[:, (c - 2) * META:(c - 1) * META], left,
                                                   view(hT, slice(None), kc, slice(0, META)), **ends)
                    bk.fills("km", last)
                    for b, kind, tiles in ((1, "v", NT + 1), (2, "g", NT)):
                        weights.wait(pe, h * (4 * B) + (4 * b + 3))
                        for t in range(tiles):
                            name = f"{kind}{t}"
                            bk.wait_free(pe, name, h)
                            for kc in range(KC):
                                last = pair_matmul(nc, out(name)[0:rows(t), :],
                                                   view(hT, slice(None), kc, tok_cols(t)),
                                                   weights.block(b, kc), kc == 0, kc == KC - 1)
                            bk.fills(name, last)
                    pe.wait_ge(q_ready, h + 1)
                    pe.wait_ge(k_ready, 2 * h + 2)
                    for t in range(NT + 1):
                        bk.wait_free(pe, f"s{t}", h)
                        for c in range(2):
                            last = nc.tensor.matmul(out(f"s{t}")[0:rows(t), :], k[:, c, tok_cols(t)],
                                                    q[:, c, :], start=c == 0, stop=c == 1)
                        bk.fills(f"s{t}", last)
                    for t in range(NT + 1):
                        bk.wait_read(pe, f"v{t}", h)
                        bk.wait_read(pe, f"s{t}", h)
                    for i in range(NT):
                        bk.wait_free(pe, f"o{i}", h)
                        for t in range(NT + 1):
                            n = rows(t)
                            value = vm[:, :] if t == NT else v[:, t, :]
                            last = nc.tensor.matmul(out(f"o{i}")[:, :], sd[0:n, t, i * P:(i + 1) * P],
                                                    value, start=t == 0, stop=t == NT)
                        bk.fills(f"o{i}", last)
                    for i in range(NT):
                        pe.wait_ge(y_ready, NT * h + (i + 1))
                        bk.wait_free(pe, f"y{i}", h)
                        for c in range(4):
                            last = nc.tensor.transpose(out(f"y{i}")[:, c * P:(c + 1) * P],
                                                       y[:, i, c * P:(c + 1) * P], ident[:, :])
                        bk.fills(f"y{i}", last)

            @block.scalar
            def _(act):
                act.wait_ge(logit_ready, 1)
                link = Chain(act, act_steps)
                link(nc.scalar.activation(lw[:, :, :], lw[:, :, :], ACT.Exp, scale=-1.0))
                link(nc.scalar.activation(lw[:, :, :], lw[:, :, :], ACT.Ln, bias=1.0))

                def following(b, h):
                    bk.wait_full(act, blocks[b][1], h)
                    for c in range(4):
                        weights.hi(act, h * (4 * B) + (4 * B + 4 * b + c), 4 * b + c, b)

                for g in range(4 * B):
                    weights.hi(act, g, g, g // 4)
                with act.Fori(0, RH) as h:
                    act.wait_ge(strip_arg, h + 1)
                    nc.scalar.activation(strip[:, :], strip[:, :], ACT.Exp).then_inc(strip_ready, 1)
                    for t in range(NT + 1):
                        bk.wait_full(act, f"v{t}", h)
                        dst = vm[:, :] if t == NT else v[:, t, :]
                        bk.reads(f"v{t}", nc.scalar.activation(dst, out(f"v{t}")[0:rows(t), :], ACT.Copy))
                    following(0, h)
                    for t in range(NT):
                        bk.wait_full(act, f"g{t}", h)
                        bk.reads(f"g{t}", nc.scalar.activation(gate[:, t, :], out(f"g{t}")[:, :], ACT.Silu))
                    following(1, h)
                    following(2, h)
                    act.wait_ge(var_ready, NT * h + NT)
                    nc.scalar.activation(rstd[:, :, 0], mv[:, :, 1], ACT.Sqrt).then_inc(std_ready, 1)
                    for i in range(NT):
                        bk.wait_full(act, f"y{i}", h)
                        nc.scalar.activation(yT[0][:, bass.ds(4 * h, 4), i * P:(i + 1) * P],
                                             out(f"y{i}")[:, :].rearrange("p (c n) -> p c n", c=4),
                                             ACT.Copy).then_inc(y_hi, 1)

            @block.vector
            def _(dve):
                link = Chain(dve, dve_steps)
                dve.wait_ge(logit_in, 16)
                link(nc.vector.tensor_scalar(lw[:, :, :], ld[:, :, :], -1.0, None, ALU.mult))
                nc.vector.tensor_tensor(lw[:, :, :], lw[:, :, :], ld[:, :, :], ALU.max).then_inc(logit_ready, 1)
                link(nc.vector.tensor_scalar(ld[:, :, :], ld[:, :, :], -1.0, 0.0, ALU.mult, ALU.max))
                dve.wait_ge(act_steps, 2)
                link(nc.vector.tensor_tensor(ld[:, :, :], ld[:, :, :], lw[:, :, :], ALU.add))
                link(nc.vector.tensor_scalar(ld[:, :, :], ld[:, :, :], -1.0, None, ALU.mult))
                dve.wait_ge(tables_in, 64)
                before = link.n
                with dve.Fori(0, RH) as h:
                    link = Chain(dve, dve_steps, before, h, 16)
                    link(nc.vector.tensor_copy(ldh[:, :], ld[:, :, bass.ds(h, 1)].rearrange("p a o -> p (a o)")))
                    link(nc.vector.tensor_scalar(strip[:, :], ahead[:, :], ldh[:, 0:1], None, ALU.mult))
                    nc.vector.scalar_tensor_tensor(out=strip[:, :], in0=behind[:, :], scalar=ldh[:, 1:2],
                                                   in1=strip[:, :], op0=ALU.mult, op1=ALU.add)\
                        .then_inc(strip_arg, 1)
                    for names, dst, col, at, n in ((("q0", "q1"), q, 0, META, SEQ), (("k0", "k1"), k, META, META, SEQ),
                                                   (("km",), k, 0, 0, META)):
                        for name in names:
                            bk.wait_full(dve, name, h)
                        if len(names) == 2:
                            x1, x2 = out(names[0])[:, :], out(names[1])[:, :]
                        else:
                            x1, x2 = out("km")[:, 0:META], out("km")[:, META:2 * META]
                        cs, sn = cos[:, at:at + n], sin[:, at:at + n]
                        nc.vector.tensor_tensor(tmp[:, 0, 0:n], x1, cs, ALU.mult)
                        link(nc.vector.tensor_tensor(tmp[:, 1, 0:n], x2, sn, ALU.mult))
                        link(nc.vector.tensor_tensor(dst[:, 0, col:col + n], tmp[:, 0, 0:n], tmp[:, 1, 0:n],
                                                     ALU.subtract))
                        ins = nc.vector.tensor_tensor(tmp[:, 0, 0:n], x1, sn, ALU.mult)
                        if len(names) == 2:
                            bk.reads(names[0], ins)
                        bk.reads(names[-1], nc.vector.tensor_tensor(tmp[:, 1, 0:n], x2, cs, ALU.mult))
                        bk.wait_read(dve, names[-1], h)
                        nc.vector.tensor_tensor(dst[:, 1, col:col + n], tmp[:, 0, 0:n], tmp[:, 1, 0:n],
                                                ALU.add).then_inc(q_ready if dst is q else k_ready, 1)
                        if dst is q:
                            dve.wait_ge(q_ready, h + 1)
                        else:
                            dve.wait_ge(k_ready, 2 * h + (1 if len(names) == 2 else 2))
                    dve.wait_ge(strip_ready, h + 1)
                    for t in range(NT + 1):
                        n = rows(t)
                        bk.wait_full(dve, f"s{t}", h)
                        x0 = (NT - 1) * P + META if t == NT else (NT - 1 - t) * P
                        bk.reads(f"s{t}", nc.vector.scalar_tensor_tensor(
                            out=sd[0:n, t, :], in0=out(f"s{t}")[0:n, :], scalar=RDK ** -0.5,
                            in1=strip[0:n, x0:x0 + SEQ], op0=ALU.mult, op1=ALU.mult))
                    for i in range(NT):
                        bk.wait_full(dve, f"o{i}", h)
                        link(nc.vector.bn_stats(stats[:, i, :], out(f"o{i}")[:, :]))
                        nc.vector.memset(after_wait[:, :], 0.0)
                        link(nc.vector.bn_aggr(mv[:, i, :], stats[:, i, :]))
                        nc.vector.tensor_scalar(mv[:, i, 1:2], mv[:, i, 1:2], LN_EPS, None, ALU.add)\
                            .then_inc(var_ready, 1)
                    dve.wait_ge(std_ready, h + 1)
                    for t in range(NT):
                        bk.wait_read(dve, f"g{t}", h)
                    nc.vector.reciprocal(rstd[:, :, 0], rstd[:, :, 0]).then_inc(rstd_ready, 1)
                    dve.wait_ge(rstd_ready, h + 1)
                    for i in range(NT):
                        bk.reads(f"o{i}", nc.vector.tensor_scalar(
                            y[:, i, :], out(f"o{i}")[:, :], mv[:, i, 0:1], rstd[:, i, :],
                            ALU.subtract, ALU.mult))
                        bk.wait_read(dve, f"o{i}", h)
                        nc.vector.tensor_tensor(y[:, i, :], y[:, i, :], gate[:, i, :], ALU.mult)\
                            .then_inc(y_ready, 1)
                    for i in range(NT):
                        dve.wait_ge(y_hi, NT * h + (i + 1))
                        part = (slice(None), bass.ds(4 * h, 4), slice(i * P, (i + 1) * P))
                        bk.reads(f"y{i}", nc.vector.tensor_tensor(
                            yT[1][part], out(f"y{i}")[:, :].rearrange("p (c n) -> p c n", c=4), yT[0][part],
                            ALU.subtract))
                    link.ends_turn()



def branch_out(core, weights, phase, hT, yT, chunks, started, merged, adds, extra=0):
    nc = core.nc
    with ExitStack() as ctx:
        gate = sbuf(nc, ctx, phase + "_gate", [P, NT, 512])
        merged_ready, gated = (core.sem(f"{phase}_{n}") for n in ("merged_ready", "gated"))
        halves = D // 512
        bk = Banks(core, [(f"g{t}", t) for t in range(NT)] + [(f"p{t}", NT + t) for t in range(NT)], halves)
        per_half = 1 + chunks // KC
        total = halves * per_half + extra

        def out(name):
            return core.banks[bk.bank(name)]

        def slot(b):
            return b % weights.blocks

        with nc.Block() as block:
            @block.sync
            def _(sp):
                for g in range(4 * started, 4 * total):
                    weights.load(sp, g, g, weights.first + g >= weights.RING)

            @block.gpsimd
            def _(pool):
                for g in range(4 * started, 4 * total):
                    weights.lo(pool, g, g, slot(g // 4))

            @block.tensor
            def _(pe):
                for n in range(halves):
                    for kind, left, b0, depth in (("g", hT, 0, KC), ("p", yT, 1, chunks)):
                        for t in range(NT):
                            name = f"{kind}{t}"
                            cols = tok_cols(t) if kind == "g" else slice(t * P, (t + 1) * P)
                            bk.wait_free(pe, name, n)
                            for c in range(depth):
                                b = per_half * n + b0 + c // KC
                                if t == 0 and c % KC == 0:
                                    weights.wait(pe, 4 * b + 3)
                                last = pair_matmul(nc, out(name)[:, :], view(left, slice(None), c, cols),
                                                   weights.block(slot(b), c % KC), c == 0, c == depth - 1)
                            bk.fills(name, last)

            @block.scalar
            def _(act):
                def split(blocks):
                    for b in blocks:
                        if b >= weights.blocks:
                            n, place = divmod(b - weights.blocks, per_half)
                            bk.wait_full(act, f"g{NT - 1}" if place == 0 else f"p{NT - 1}", n)
                        for c in range(4):
                            weights.hi(act, 4 * b + c, 4 * b + c, slot(b))

                def sigmoids(n):
                    for t in range(NT):
                        bk.wait_full(act, f"g{t}", n)
                        act.wait_ge(gated, NT * n + 1)
                        bk.reads(f"g{t}", nc.scalar.activation(gate[:, t, :], out(f"g{t}")[:, :], ACT.Sigmoid))

                split(range(started, per_half))
                sigmoids(0)
                split(range(max(started, per_half), halves * per_half))
                sigmoids(1)
                split(range(halves * per_half, total))

            @block.vector
            def _(dve):
                nc.vector.memset(gate[0:1, 0, 0:1], 0.0).then_inc(gated, 1)
                with dve.Fori(0, halves) as n:
                    for t in range(NT):
                        bk.wait_full(dve, f"p{t}", n)
                        bk.wait_read(dve, f"g{t}", n)
                        dst = merged[:, t, bass.ds(512 * n, 512)]
                        if adds:
                            bk.reads(f"p{t}", nc.vector.tensor_tensor(gate[:, t, :], out(f"p{t}")[:, :],
                                                                      gate[:, t, :], ALU.mult))
                            bk.wait_read(dve, f"p{t}", n)
                            nc.vector.tensor_tensor(dst, dst, gate[:, t, :], ALU.add).then_inc(gated, 1)
                        else:
                            bk.reads(f"p{t}", nc.vector.tensor_tensor(dst, out(f"p{t}")[:, :],
                                                                      gate[:, t, :], ALU.mult))
                            bk.wait_read(dve, f"p{t}", n)
                            nc.vector.tensor_copy(gate[0:1, t, 0:1], gate[0:1, t, 1:2]).then_inc(gated, 1)



DIRS = ("f", "b")
BANK_OF = {"f": 1, "b": 4, "m": 7}
FOLLOWING_DONE = {"GATES": 0, "CONV_0": 1, "CONV_1": 1 + (CW - 1), "CONV_2": 1 + 2 * (CW - 1),
                  "SCALES": 1 + 3 * (CW - 1)}
FOLLOWING_STEPS = 1 + 3 * (CW - 1) + 1


def delta_net(core, weights, a, hT, yT, ident):
    nc = core.nc
    NC5 = NT + 1
    with ExitStack() as ctx:
        w_ab = sbuf(nc, ctx, "dn_w_ab", [P, KC, 32])
        w_ab_pair = sbuf_pair(nc, ctx, "dn_w_ab", [P, KC, 32])
        upper = sbuf(nc, ctx, "dn_upper", [P, P])
        lower = sbuf(nc, ctx, "dn_lower", [P, P])
        ones = sbuf(nc, ctx, "dn_ones", [P, P])
        masks = sbuf(nc, ctx, "dn_masks", [P, 2, LEVELS, P])
        conv_w = sbuf(nc, ctx, "dn_conv_w", [P, DH, 3 * CW])
        cw = sbuf(nc, ctx, "dn_conv_head", [P, 3 * CW])
        norm_g = sbuf(nc, ctx, "dn_norm_g", [P, 1])
        dtb = sbuf(nc, ctx, "dn_dt_bias", [P, 16])
        alog = sbuf(nc, ctx, "dn_a_log", [P, 16])
        raw = sbuf(nc, ctx, "dn_raw", [P, NC5, 32])
        g = sbuf(nc, ctx, "dn_g", [P, NC5, 16])
        g2 = sbuf(nc, ctx, "dn_g_work", [P, NC5, 16])
        NEGB, BETA, NEGEXP, BETAEND, END, G = range(6)
        scal = sbuf(nc, ctx, "dn_scal", [P, 6, NC5, 16])
        hs = sbuf(nc, ctx, "dn_scal_head", [P, 6 * NC5, 2])
        hs_next = sbuf(nc, ctx, "dn_scal_next_head", [P, 6 * NC5, 2])
        eps = sbuf(nc, ctx, "dn_eps", [P, 2])
        pre = sbuf(nc, ctx, "dn_conv_in", [P, 3, TOK + CW - 1])
        cv = sbuf(nc, ctx, "dn_conv_out", [P, 3, TOK])
        qk = sbuf(nc, ctx, "dn_q_k", [P, 2, TOK])
        expb = sbuf(nc, ctx, "dn_exp_b", [P, 2, SEQ])
        sq_meta = sbuf(nc, ctx, "dn_squares_meta", [P, META])
        v_tok = sbuf(nc, ctx, "dn_v_tok", [P, NC5, DK])
        k_tok = sbuf(nc, ctx, "dn_k_tok", [P, NC5, DK])
        inv_len = sbuf(nc, ctx, "dn_inverse_lengths", [P, 2 * NC5])
        gz = sbuf(nc, ctx, "dn_gate_z", [P, SEQ])
        gt = sbuf(nc, ctx, "dn_g_tri", [P, 2, NT, P])
        gtm = sbuf(nc, ctx, "dn_g_tri_meta", [P, META])
        dec = sbuf(nc, ctx, "dn_decay", [P, 2, NT, P])
        decm = sbuf(nc, ctx, "dn_decay_meta", [META, META])
        qd = sbuf(nc, ctx, "dn_q_decayed", [P, 2, SEQ])
        attn = sbuf(nc, ctx, "dn_attn", [P, 2, NT, P])
        lt = sbuf(nc, ctx, "dn_l", [P, 2, NT, P])
        sq = lt[:, :, :, :]
        ltm = sbuf(nc, ctx, "dn_l_meta", [META, META])
        lm = sbuf(nc, ctx, "dn_l_levels", [P, 2, LEVELS, NT, P])
        lmm = sbuf(nc, ctx, "dn_l_levels_meta", [P, 4, P])
        x = sbuf(nc, ctx, "dn_x", [P, 2, NT, P])
        xt = sbuf(nc, ctx, "dn_xt", [P, 2, NT, P])
        yy = sbuf(nc, ctx, "dn_lx", [P, 2, NT, P])
        xm = sbuf(nc, ctx, "dn_x_meta", [P, 3, P])
        state = sbuf(nc, ctx, "dn_state", [P, 2, DK])
        rhs = sbuf(nc, ctx, "dn_rhs", [P, 2, DK])
        vn = sbuf(nc, ctx, "dn_v_new", [P, 2, DK])
        v2 = sbuf(nc, ctx, "dn_v_end", [P, 2, DK])
        ysq, y = gt[:, 0, :, :], gt[:, 1, :, :]
        rstd = sbuf(nc, ctx, "dn_rstd", [P, NT])
        names = ("ab_in ab_hi ab_lo y_hi y_lo tables_in act_steps dve_steps sp_arg sp_log g_ready exp_ready conv_ready "
                 "silu_ready sq_ready diag_ready gtri_ready expb_ready dec_ready qd_ready "
                 "attn_ready masked_ready x_start next_steps ysq_ready ms_ready std_ready").split()
        s = {n: core.sem("dn_" + n) for n in names}
        setup_bank = Banks(core, [("ab", 0), ("sums", 1)])
        early = Banks(core, [("pm", 6), ("q", 2), ("k", 3), ("v", 5), ("bf", 2), ("bb", 3), ("bm", 5),
                             ("ss", 2), ("nq", 2), ("nk", 3), ("nm", 5), ("z", 6)], DH)
        order = [("tv", 1), ("tk", 4), ("tm", 7), ("kk", 0), ("qk", 1), ("kkm", 7)]
        for level in range(LEVELS):
            parts = "fbm" if level < 4 else "fb"
            if level:
                order += [(f"y{d}{level}", BANK_OF[d]) for d in parts]
                order += [(f"z{d}{level}", BANK_OF[d]) for d in parts]
            if level < LEVELS - 1:
                order += [(f"x{d}{level}", BANK_OF[d]) for d in ("fbm" if level < 3 else "fb")]
        scan = [(("f", NT), ("b", NT - 1))] + [(("f", r), ("b", NT - 2 - r)) for r in range(NT - 1)] \
            + [(("f", NT - 1),)]
        first, final = {"f": NT, "b": NT - 1}, {"f": NT - 1, "b": 0}
        for steps in scan:
            order += [(f"r{d}{c}", BANK_OF[d]) for d, c in steps if c != first[d]]
            order += [(f"w{d}{c}", BANK_OF[d]) for d, c in steps]
            order += [(f"s{d}{c}", BANK_OF[d]) for d, c in steps if c != final[d]]
        order += [("o", 0), ("ty", 7)]
        bk = Banks(core, order, DH)
        turn_order = ("late PROJ_Q PROJ_K level0 GATES level1 PROJ_V level2 SPLIT_QKV CONV_0 level3 SILU_0 DECAYS CONV_1 "
                      "level4 SILU_1 EXP_B CONV_2 level5 SUMS SILU_2 DECAY_ARG LENGTHS level6 EXP_DECAY scan0 SCALES scan1 "
                      "PROJ_Z0 scan2 PROJ_Z1 scan3 PROJ_Z2 scan4 PROJ_Z3 tail SPLIT_Z").split()

        def run(eng, this, following):
            for part in turn_order:
                if part.isupper():
                    following(part, 0, True)
            with eng.Fori(0, DH - 2) as h:
                for part in turn_order:
                    if part.isupper():
                        following(part, h + 1, False)
                    else:
                        this(part, h)
            for part in turn_order:
                if not part.isupper():
                    this(part, DH - 2)
                elif not part.startswith("SPLIT"):
                    following(part, DH - 1, False)
            for part in turn_order:
                if not part.isupper():
                    this(part, DH - 1)

        def out(name):
            return core.banks[(early if name in early.place else bk).bank(name)]

        def head_of(pair, h):
            return [half[:, h, :] if isinstance(h, int) else
                    half[:, bass.ds(h, 1), :].rearrange("p o n -> p (o n)") for half in pair]

        def by_chunk(ap):
            return ap.rearrange("p (c n) -> p c n", c=NT)

        def over_chunks(ap):
            return ap.unsqueeze(1).broadcast_to([ap.shape[0], NT, ap.shape[-1]])

        def masked(level):
            return 3 * level + 3 if level < 4 else 12 + 2 * (level - 3)

        def wait_xt(eng, d, level, h):
            if level == 0:
                eng.wait_ge(s["x_start"], 3 * h + 3)
            else:
                bk.wait_read(eng, f"z{d}{level}", h)

        def sc(kind, c, d):
            n = rows(c)
            return hs[0:n, kind * NC5 + c, DIRS.index(d):DIRS.index(d) + 1]

        def sc_next(kind, c, d):
            return hs_next[0:rows(c), kind * NC5 + c, DIRS.index(d):DIRS.index(d) + 1]

        with nc.Block() as block:
            @block.sync
            def _(sp):
                sp.dma_start(w_ab[:, :, :], a["w_dn_ab"]).then_inc(s["ab_in"], 16)
                loads = ((upper[:, :], a["upper"]), (lower[:, :], a["lower"]),
                         (masks[:, :, :, :], a["masks"]), (conv_w[:, :, :], a["dn_conv"]),
                         (norm_g[:, :], a["dn_norm_g"]),
                         (dtb[:, :], a["dn_dt_bias"].partition_broadcast(P)),
                         (alog[:, :], a["dn_a_log"].partition_broadcast(P)))
                for dst, src in loads:
                    sp.dma_start(dst, src).then_inc(s["tables_in"], 16)
                for g in range(4):
                    weights.load(sp, g, g, True)
                with sp.Fori(0, DH - 1) as h:
                    for g in range(4):
                        weights.load(sp, h * 4 + (4 + g), g, True)

            @block.tensor
            def _(pe):
                pe.wait_ge(s["ab_in"], 16)
                pe.wait_ge(s["ab_lo"], 1)
                for t in range(NC5):
                    for kc in range(KC):
                        last = pair_matmul(nc, core.banks[0][0:rows(t), 32 * t:32 * t + 32],
                                           view(hT, slice(None), kc, tok_cols(t)),
                                           view(w_ab_pair, slice(None), kc), kc == 0, kc == KC - 1)
                setup_bank.fills("ab", last)
                pe.wait_ge(s["tables_in"], 16 * 7)
                pe.wait_ge(s["g_ready"], 1)
                sums = core.banks[1]
                nc.tensor.matmul(sums[:, 0:32], upper[:, :], g[:, 0:NT, 0:8], start=True, stop=True)
                nc.tensor.matmul(sums[:, 32:64], lower[:, :], g[:, 0:NT, 8:16], start=True, stop=True)
                nc.tensor.matmul(sums[0:META, 64:72], upper[0:META, 0:META], g[0:META, NT, 0:8],
                                 start=True, stop=True)
                nc.tensor.matmul(sums[:, 128:192], ones[:, :], g[:, 0:NT, :], start=True, stop=True)
                setup_bank.fills("sums", nc.tensor.matmul(
                    sums[0:META, 200:208], ones[0:META, 0:META], g[0:META, NT, 0:8], start=True, stop=True))

                setup_bank.wait_read(pe, "sums")

                def project(name, i, hn):
                    weights.wait(pe, 4 * hn + i)
                    early.wait_free(pe, name, hn)
                    for kc in range(KC):
                        left, ends = weights.columns(0, i, kc), dict(start=kc == 0, stop=kc == KC - 1)
                        last = pair_matmul(nc, out(name)[:, :], left,
                                           view(hT, slice(None), kc, slice(META, TOK)), **ends)
                        if kc == KC - 1:
                            early.fills(name, last)
                        last = pair_matmul(nc, out("pm")[:, i * META:(i + 1) * META], left,
                                           view(hT, slice(None), kc, slice(0, META)), **ends)
                    return last

                def following(part, hn, at_start):
                    if part == "PROJ_Q":
                        early.wait_free(pe, "pm", hn)
                        project("q", 0, hn)
                    elif part == "PROJ_K":
                        project("k", 1, hn)
                    elif part == "PROJ_V":
                        early.fills("pm", project("v", 2, hn))
                    elif part.startswith("PROJ_Z"):
                        quarter = int(part[-1])
                        if quarter == 0:
                            weights.wait(pe, 4 * hn + 3)
                            early.wait_free(pe, "z", hn)
                        for kc in range(KC // 4 * quarter, KC // 4 * (quarter + 1)):
                            last = pair_matmul(nc, out("z")[:, :], weights.columns(0, 3, kc),
                                               view(hT, slice(None), kc, slice(META, TOK)), kc == 0, kc == KC - 1)
                        if quarter == 3:
                            early.fills("z", last)
                    elif part == "DECAYS":
                        pe.wait_ge(s["gtri_ready"], 3 * hn + 3)
                        for i, d in enumerate(DIRS):
                            early.wait_free(pe, "b" + d, hn)
                            early.fills("b" + d, nc.tensor.matmul(out("b" + d)[:, :], ones[:, :],
                                                                  gt[:, i, :, :], start=True, stop=True))
                        early.wait_free(pe, "bm", hn)
                        early.fills("bm", nc.tensor.matmul(out("bm")[:, 0:META], ones[:, :], gtm[:, :],
                                                           start=True, stop=True))
                    elif part == "SUMS":
                        pe.wait_ge(s["sq_ready"], 2 * hn + 2)
                        early.wait_free(pe, "ss", hn)
                        for i in range(2):
                            for t in range(NT + i):
                                last = nc.tensor.matmul(out("ss")[0:rows(t), NC5 * i + t:NC5 * i + t + 1],
                                                        sq_meta[:, :] if t == NT else sq[:, i, t, :], ones[:, 0:1], start=True, stop=True)
                        early.fills("ss", last)
                    elif part == "SCALES":
                        pe.wait_ge(s["diag_ready"], hn + 1)
                        for name, right, n in (("nq", gt[:, 0, :, :], SEQ), ("nk", gt[:, 1, :, :], SEQ),
                                               ("nm", gtm[:, :], META)):
                            early.wait_free(pe, name, hn)
                            early.fills(name, nc.tensor.matmul(out(name)[:, 0:n], ones[:, :], right,
                                                               start=True, stop=True))

                def late(h):
                    pe.wait_ge(s["silu_ready"], 3 * h + 3)
                    early.wait_read(pe, "nm", h)
                    early.wait_read(pe, "nk", h)
                    for name, src in (("tv", cv[:, 2, :]), ("tk", qk[:, 1, :])):
                        bk.wait_free(pe, name, h)
                        for t in range(NT):
                            last = nc.tensor.transpose(out(name)[:, t * P:(t + 1) * P], src[:, tok_cols(t)],
                                                       ident[:, :])
                        bk.fills(name, last)
                    bk.wait_free(pe, "tm", h)
                    nc.tensor.transpose(out("tm")[0:META, 0:P], cv[:, 2, 0:META], ident[:, :])
                    bk.fills("tm", nc.tensor.transpose(out("tm")[0:META, P:2 * P], qk[:, 1, 0:META],
                                                       ident[:, :]))
                    early.wait_read(pe, "nq", h)
                    for name, i in (("kk", 1), ("qk", 0)):
                        bk.wait_free(pe, name, h)
                        for t in range(NT):
                            last = nc.tensor.matmul(out(name)[:, t * P:(t + 1) * P], qk[:, 1, tok_cols(t)],
                                                    qk[:, i, tok_cols(t)], start=True, stop=True)
                        bk.fills(name, last)
                    bk.wait_free(pe, "kkm", h)
                    bk.fills("kkm", nc.tensor.matmul(out("kkm")[0:META, 0:META], qk[:, 1, 0:META],
                                                     qk[:, 1, 0:META], start=True, stop=True))

                def grow(level, h):
                    parts = [("f", 0), ("b", 1)] + ([("m", 2)] if level < 4 else [])
                    if level:
                        pe.wait_ge(s["masked_ready"], 18 * h + masked(level))
                        for d, i in parts:
                            bk.wait_read(pe, f"x{d}{level - 1}", h)
                            bk.wait_free(pe, f"y{d}{level}", h)
                            if d == "m":
                                last = nc.tensor.matmul(out("ym1")[:, 0:META], lmm[:, level, :],
                                                        xm[:, 0, 0:META], start=True, stop=True)
                            else:
                                for t in range(NT):
                                    last = nc.tensor.matmul(out(f"y{d}{level}")[:, t * P:(t + 1) * P],
                                                            lm[:, i, level, t, :], x[:, i, t, :],
                                                            start=True, stop=True)
                            bk.fills(f"y{d}{level}", last)
                        for d, i in parts:
                            bk.wait_read(pe, f"y{d}{level}", h)
                            bk.wait_free(pe, f"z{d}{level}", h)
                            if d == "m":
                                last = nc.tensor.matmul(out("ym1")[:, 0:META], xm[:, 2, :],
                                                        xm[:, 1, 0:META], start=True, stop=True)
                            else:
                                for t in range(NT):
                                    last = nc.tensor.matmul(out(f"z{d}{level}")[:, t * P:(t + 1) * P],
                                                            yy[:, i, t, :], xt[:, i, t, :],
                                                            start=True, stop=True)
                            bk.fills(f"z{d}{level}", last)
                    if level < LEVELS - 1:
                        for d, i in parts:
                            if d == "m" and level == 3:
                                continue
                            wait_xt(pe, d, level, h)
                            bk.wait_free(pe, f"x{d}{level}", h)
                            if d == "m":
                                last = nc.tensor.transpose(out("ym1")[:, 0:P], xm[:, 1, :], ident[:, :])
                            else:
                                for t in range(NT):
                                    last = nc.tensor.transpose(out(f"x{d}{level}")[:, t * P:(t + 1) * P],
                                                               xt[:, i, t, :], ident[:, :])
                            bk.fills(f"x{d}{level}", last)

                def scan_round(number, h):
                    steps, opened = scan[number], number > 0
                    if number == 0:
                        pe.wait_ge(s["qd_ready"], 2 * h + 2)
                        pe.wait_ge(s["attn_ready"], 2 * h + 2)
                        for name in ("tv", "tk", "tm"):
                            bk.wait_read(pe, name, h)
                        for d, level in (("f", LEVELS - 1), ("b", LEVELS - 1), ("m", 3)):
                            wait_xt(pe, d, level, h)
                        bk.wait_free(pe, "o", h)
                    for d, c in steps:
                        i, n = DIRS.index(d), rows(c)
                        if c != first[d]:
                            previous = {"f": NT if c == 0 else c - 1, "b": c + 1}[d]
                            bk.wait_read(pe, f"s{d}{previous}", h)
                            bk.wait_free(pe, f"r{d}{c}", h)
                            bk.fills(f"r{d}{c}", nc.tensor.matmul(out(f"r{d}{c}")[0:n, 0:DK],
                                                                  qk[:, 1, tok_cols(c)], state[:, i, :],
                                                                  start=True, stop=True))
                            nc.tensor.matmul(out("o")[:, c * P:(c + 1) * P], qd[:, i, c * P:(c + 1) * P],
                                             state[:, i, :], start=not opened, stop=False,
                                             skip_group_check=True)
                            opened = True
                    for d, c in steps:
                        i, n = DIRS.index(d), rows(c)
                        left = xm[:, 1, :] if c == NT else xt[:, i, c, :]
                        right = v_tok[:, c, :]
                        if c != first[d]:
                            bk.wait_read(pe, f"r{d}{c}", h)
                            right = rhs[:, i, :]
                        bk.wait_free(pe, f"w{d}{c}", h)
                        bk.fills(f"w{d}{c}", nc.tensor.matmul(out(f"w{d}{c}")[:, 0:DK], left, right,
                                                              start=True, stop=True))
                    for d, c in steps:
                        i, n = DIRS.index(d), rows(c)
                        bk.wait_read(pe, f"w{d}{c}", h)
                        if c != final[d]:
                            bk.wait_free(pe, f"s{d}{c}", h)
                            bk.fills(f"s{d}{c}", nc.tensor.matmul(out(f"s{d}{c}")[:, 0:DK],
                                                                  k_tok[0:n, c, :], v2[0:n, i, :],
                                                                  start=True, stop=True))
                        if c != NT:
                            last = nc.tensor.matmul(out("o")[:, c * P:(c + 1) * P], attn[:, i, c, :],
                                                    vn[:, i, :], start=not opened, stop=steps is scan[-1],
                                                    skip_group_check=True)
                            opened = True
                    if steps is scan[-1]:
                        bk.fills("o", last)

                def this(part, h):
                    if part == "late":
                        late(h)
                    elif part.startswith("level"):
                        grow(int(part[-1]), h)
                    elif part.startswith("scan"):
                        scan_round(int(part[-1]), h)
                    elif part == "tail":
                        bk.wait_read(pe, "o", h)
                        bk.wait_free(pe, "ty", h)
                        for t in range(NT):
                            last = nc.tensor.transpose(out("ty")[:, t * P:(t + 1) * P], y[:, t, :], ident[:, :])
                        bk.fills("ty", last)

                run(pe, this, following)

            @block.scalar
            def _(act):
                link = Chain(act, s["act_steps"])
                act.wait_ge(s["ab_in"], 16)
                nc.scalar.activation(w_ab_pair[0][:, :, :], w_ab[:, :, :], ACT.Copy).then_inc(s["ab_hi"], 1)
                for g in range(4):
                    weights.hi(act, g, g, 0)
                act.wait_ge(s["sp_arg"], 1)
                link(nc.scalar.activation(g2[:, :, :], g2[:, :, :], ACT.Exp))
                link(nc.scalar.activation(g2[:, :, :], g2[:, :, :], ACT.Ln, bias=1.0))
                link(nc.scalar.activation(alog[:, :], alog[:, :], ACT.Exp))
                nc.scalar.activation(scal[:, BETA, :, :], raw[:, :, 16:32], ACT.Sigmoid)\
                    .then_inc(s["sp_log"], 1)
                setup_bank.wait_read(act, "sums")
                nc.scalar.activation(scal[:, NEGEXP, :, :], scal[:, NEGB, :, :], ACT.Exp, scale=-1.0)
                nc.scalar.activation(scal[:, BETAEND, :, :], scal[:, BETAEND, :, :], ACT.Exp)
                nc.scalar.activation(scal[:, END, :, :], scal[:, END, :, :], ACT.Exp)\
                    .then_inc(s["exp_ready"], 1)

                def following(part, hn, at_start):
                    if part in ("PROJ_Q", "PROJ_K", "PROJ_V"):
                        if part == "PROJ_V":
                            early.wait_full(act, "pm", hn)
                            early.reads("pm", nc.scalar.activation(
                                pre[:, :, 2:2 + META], out("pm")[:, 0:3 * META].rearrange("p (i n) -> p i n", i=3),
                                ACT.Copy))
                        name = part[-1].lower()
                        early.wait_full(act, name, hn)
                        early.reads(name, nc.scalar.activation(pre[:, "qkv".index(name), 2 + META:2 + TOK],
                                                               out(name)[:, :], ACT.Copy))
                    elif part.startswith("SPLIT"):
                        for i in ((0, 1, 2) if part == "SPLIT_QKV" else (3,)):
                            early.wait_full(act, ("q", "k", "pm", "z")[i], hn)
                            weights.hi(act, 4 * hn + (4 + i), i, 0)
                    elif part.startswith("SILU"):
                        i = int(part[-1])
                        act.wait_ge(s["conv_ready"], 3 * hn + (i + 1))
                        nc.scalar.activation(cv[:, i, :], cv[:, i, :], ACT.Silu).then_inc(s["silu_ready"], 1)
                        if i < 2:
                            act.wait_ge(s["silu_ready"], 3 * hn + (i + 1))
                            if i == 0 and not at_start:
                                act.wait_ge(s["masked_ready"], 18 * hn)
                            if i == 1:
                                nc.scalar.activation(sq_meta[:, :], cv[:, 1, 0:META], ACT.Square)
                            nc.scalar.activation(sq[:, i, :, :], by_chunk(cv[:, i, META:TOK]), ACT.Square)\
                                .then_inc(s["sq_ready"], 1)
                    elif part == "EXP_B":
                        if not at_start:
                            act.wait_ge(s["qd_ready"], 2 * hn)
                        for i, d in enumerate(DIRS):
                            early.wait_full(act, "b" + d, hn)
                            nc.scalar.activation(expb[:, i, :], out("b" + d)[:, :], ACT.Exp)\
                                .then_inc(s["expb_ready"], 1)
                    elif part == "EXP_DECAY":
                        for name in ("bf", "bb", "bm"):
                            early.wait_read(act, name, hn)
                        nc.scalar.activation(dec[:, :, :, :], dec[:, :, :, :], ACT.Exp)\
                            .then_inc(s["dec_ready"], 1)
                        nc.scalar.activation(decm[:, :], decm[:, :], ACT.Exp).then_inc(s["dec_ready"], 1)
                    elif part == "LENGTHS":
                        early.wait_full(act, "ss", hn)
                        nc.scalar.activation(inv_len[:, 0:NT], out("ss")[:, 0:NT], ACT.Sqrt, bias=eps[:, 0:1],
                                             scale=float(DK))
                        nc.scalar.activation(inv_len[0:META, 2 * NC5 - 1:2 * NC5],
                                             out("ss")[0:META, 2 * NC5 - 1:2 * NC5], ACT.Sqrt,
                                             bias=eps[0:META, 1:2])
                        early.reads("ss", nc.scalar.activation(
                            inv_len[:, NC5:NC5 + NT], out("ss")[:, NC5:NC5 + NT], ACT.Sqrt, bias=eps[:, 1:2]))

                def late(h):
                    for name, dst in (("tv", v_tok), ("tk", k_tok)):
                        bk.wait_full(act, name, h)
                        bk.reads(name, nc.scalar.activation(dst[:, 0:NT, :], by_chunk(out(name)[:, :]),
                                                            ACT.Copy))
                    bk.wait_full(act, "tm", h)
                    nc.scalar.activation(v_tok[0:META, NT, :], out("tm")[0:META, 0:P], ACT.Copy)
                    bk.reads("tm", nc.scalar.activation(k_tok[0:META, NT, :], out("tm")[0:META, P:2 * P],
                                                        ACT.Copy))
                    early.wait_full(act, "z", h)
                    early.reads("z", nc.scalar.activation(gz[:, :], out("z")[:, :], ACT.Silu))

                def grow(level, h):
                    parts = [("f", 0), ("b", 1)] + ([("m", 2)] if level < 4 else [])
                    if level:
                        for d, i in parts:
                            bk.wait_full(act, f"y{d}{level}", h)
                            if d == "m":
                                ins = nc.scalar.activation(xm[0:META, 2, 0:META], out("ym1")[0:META, 0:META],
                                                           ACT.Copy)
                            else:
                                ins = nc.scalar.activation(yy[:, i, :, :], by_chunk(out(f"y{d}{level}")[:, :]),
                                                           ACT.Copy)
                            bk.reads(f"y{d}{level}", ins)
                    if level < LEVELS - 1:
                        for d, i in parts:
                            if d == "m" and level == 3:
                                continue
                            bk.wait_full(act, f"x{d}{level}", h)
                            if d == "m":
                                ins = nc.scalar.activation(xm[0:META, 0, 0:META], out("ym1")[0:META, 0:META],
                                                           ACT.Copy)
                            else:
                                ins = nc.scalar.activation(x[:, i, :, :], by_chunk(out(f"x{d}{level}")[:, :]),
                                                           ACT.Copy)
                            bk.reads(f"x{d}{level}", ins)

                def this(part, h):
                    if part == "late":
                        late(h)
                    elif part.startswith("level"):
                        grow(int(part[-1]), h)
                    elif part.startswith("scan"):
                        for d, c in scan[int(part[-1])]:
                            if d == "b":
                                bk.wait_full(act, f"w{d}{c}", h)
                                nc.scalar.activation(vn[:, 1, :], out(f"w{d}{c}")[:, 0:DK], ACT.Copy,
                                                     scale=sc(BETA, c, d))
                                bk.reads(f"w{d}{c}", nc.scalar.activation(v2[:, 1, :], out(f"w{d}{c}")[:, 0:DK],
                                                                          ACT.Copy, scale=sc(BETAEND, c, d)))
                    elif part == "tail":
                        bk.wait_full(act, "o", h)
                        nc.scalar.activation(ysq[:, :, :], by_chunk(out("o")[:, :]), ACT.Square)\
                            .then_inc(s["ysq_ready"], 1)
                        act.wait_ge(s["ms_ready"], h + 1)
                        nc.scalar.activation(rstd[:, :], rstd[:, :], ACT.Sqrt).then_inc(s["std_ready"], 1)
                        bk.wait_read(act, "ty", h)
                        nc.scalar.activation(head_of(yT, h)[0], gz[:, :], ACT.Copy).then_inc(s["y_hi"], 1)
                        act.wait_ge(s["y_lo"], h + 1)

                run(act, this, following)

            @block.gpsimd
            def _(pool):
                for g in range(4):
                    weights.lo(pool, g, g, 0)
                for g in range(3):
                    weights.lo(pool, 4 + g, g, 0)

                def turn(h, weights_left):
                    pool.wait_ge(s["expb_ready"], 2 * h + 2)
                    early.wait_read(pool, "nq", h)
                    for i in range(2):
                        nc.gpsimd.tensor_tensor(qd[:, i, :], expb[:, i, :], qk[:, 0, META:TOK], ALU.mult)\
                            .then_inc(s["qd_ready"], 1)
                    bk.wait_read(pool, "kk", h)
                    bk.wait_read(pool, "kkm", h)
                    for level in range(LEVELS):
                        for i in range(2):
                            nc.gpsimd.tensor_tensor(lm[:, i, level, :, :], lt[:, i, :, :],
                                                    over_chunks(masks[:, i, level, :]), ALU.mult)\
                                .then_inc(s["masked_ready"], 1)
                        if level < 4:
                            nc.gpsimd.tensor_tensor(lmm[0:META, level, 0:META], ltm[:, :], masks[0:META, 0, level, 0:META],
                                                    ALU.mult).then_inc(s["masked_ready"], 1)
                    bk.wait_read(pool, "qk", h)
                    for i, keep in enumerate((upper, lower)):
                        nc.gpsimd.tensor_tensor(attn[:, i, :, :], attn[:, i, :, :],
                                                over_chunks(keep[:, :]), ALU.mult).then_inc(s["attn_ready"], 1)
                    if weights_left != "none":
                        weights.lo(pool, h * 4 + 7, 3, 0)
                    if weights_left == "all":
                        for g in range(3):
                            weights.lo(pool, h * 4 + (8 + g), g, 0)

                with pool.Fori(0, DH - 2) as h:
                    turn(h, "all")
                turn(DH - 2, "z")
                turn(DH - 1, "none")

            @block.vector
            def _(dve):
                link = Chain(dve, s["dve_steps"])
                nc.vector.memset(pre[:, :, :], 0.0)
                nc.vector.memset(raw[:, :, :], 0.0)
                nc.vector.memset(scal[:, :, :, :], 0.0)
                for zeroed in (gtm[:, :], lmm[:, :, :], xm[:, :, :], v_tok[:, NT, :]):
                    nc.vector.memset(zeroed, 0.0)
                nc.vector.memset(eps[:, 0:1], DK * RMS_EPS)
                nc.vector.memset(eps[:, 1:2], RMS_EPS)
                nc.vector.memset(inv_len[:, :], 1.0)
                link(nc.vector.memset(ones[:, :], 1.0))
                dve.wait_ge(s["ab_hi"], 1)
                nc.vector.tensor_tensor(w_ab_pair[1][:, :, :], w_ab[:, :, :], w_ab_pair[0][:, :, :],
                                        ALU.subtract).then_inc(s["ab_lo"], 1)
                setup_bank.wait_full(dve, "ab")
                nc.vector.tensor_copy(raw[:, 0:NT, :],
                                      core.banks[0][:, 0:NT * 32].rearrange("p (t n) -> p t n", t=NT))
                setup_bank.reads("ab", nc.vector.tensor_copy(raw[0:META, NT, :],
                                                             core.banks[0][0:META, NT * 32:NC5 * 32]))
                setup_bank.wait_read(dve, "ab")
                dve.wait_ge(s["tables_in"], 16 * 7)
                z = raw[:, :, 0:16]
                link(nc.vector.tensor_tensor(z, z, dtb[:, :].unsqueeze(1).broadcast_to([P, NC5, 16]), ALU.add))
                link(nc.vector.tensor_scalar(g2[:, :, :], z, -1.0, None, ALU.mult))
                nc.vector.tensor_tensor(g2[:, :, :], g2[:, :, :], z, ALU.min).then_inc(s["sp_arg"], 1)
                dve.wait_ge(s["sp_log"], 1)
                link(nc.vector.tensor_scalar(g[:, :, :], z, 0.0, None, ALU.max))
                link(nc.vector.tensor_tensor(g[:, :, :], g[:, :, :], g2[:, :, :], ALU.add))
                link(nc.vector.tensor_scalar(alog[:, :], alog[:, :], -1.0, None, ALU.mult))
                link(nc.vector.tensor_tensor(g[:, :, :], g[:, :, :],
                                             alog[:, :].unsqueeze(1).broadcast_to([P, NC5, 16]), ALU.mult))
                nc.vector.tensor_copy(scal[:, G, :, :], g[:, :, :]).then_inc(s["g_ready"], 1)
                setup_bank.wait_full(dve, "sums")
                dve.wait_ge(s["g_ready"], 1)
                sums = core.banks[1]
                running = ((scal[:, :, 0:NT, 0:8], sums[:, 0:32].rearrange("p (c n) -> p c n", c=NT),
                            sums[:, 128:192].rearrange("p (c n) -> p c n", c=NT)[:, :, 0:8]),
                           (scal[:, :, 0:NT, 8:16], sums[:, 32:64].rearrange("p (c n) -> p c n", c=NT),
                            sums[:, 128:192].rearrange("p (c n) -> p c n", c=NT)[:, :, 8:16]),
                           (scal[0:META, :, NT:NC5, 0:8], sums[0:META, 64:72].unsqueeze(1),
                            sums[0:META, 200:208].unsqueeze(1)))
                for dst, b, end in running:
                    link(nc.vector.tensor_scalar(dst[:, NEGB], b, -1.0, None, ALU.mult))
                    nc.vector.tensor_copy(dst[:, END], end)
                    ins = nc.vector.tensor_tensor(dst[:, BETAEND], dst[:, NEGB], end, ALU.add)
                setup_bank.reads("sums", ins)
                dve.wait_ge(s["exp_ready"], 1)
                nc.vector.tensor_tensor(scal[:, BETAEND, :, :], scal[:, BETAEND, :, :], scal[:, BETA, :, :],
                                        ALU.mult)
                link(nc.vector.tensor_scalar(scal[:, NEGEXP, :, :], scal[:, NEGEXP, :, :], -1.0, None,
                                             ALU.mult))
                before = link.n

                def following(part, hn, at_start):
                    link = Chain(dve, s["next_steps"], FOLLOWING_DONE[part], hn, FOLLOWING_STEPS) \
                        if part in FOLLOWING_DONE else None
                    if part == "GATES":
                        ds = slice(hn, hn + 1) if isinstance(hn, int) else bass.ds(hn, 1)
                        nc.vector.tensor_copy(hs_next[:, :, :], scal[:, :, :, :].rearrange(
                            "p k c (d h) -> p (k c) d h", d=2)[:, :, :, ds].rearrange("p k d o -> p k (d o)"))
                        link(nc.vector.tensor_copy(cw[:, :], conv_w[:, ds, :].rearrange("p o n -> p (o n)")))
                        for i, (d, tri) in enumerate(zip(DIRS, (upper, lower))):
                            for c in range(NT):
                                ins = nc.vector.tensor_scalar(gt[:, i, c, :], tri[:, :], sc_next(G, c, d), None,
                                                              ALU.mult)
                            ins.then_inc(s["gtri_ready"], 1)
                        nc.vector.tensor_scalar(gtm[0:META, :], upper[0:META, 0:META], sc_next(G, NT, "f"), None,
                                                ALU.mult).then_inc(s["gtri_ready"], 1)
                    elif part.startswith("CONV"):
                        i = int(part[-1])
                        early.wait_read(dve, "pm", hn)
                        early.wait_read(dve, "qkv"[i], hn)
                        link(nc.vector.tensor_scalar(cv[:, i, :], pre[:, i, 0:TOK], cw[:, CW * i:CW * i + 1],
                                                     None, ALU.mult))
                        for j in range(1, CW):
                            ins = nc.vector.scalar_tensor_tensor(
                                out=cv[:, i, :], in0=pre[:, i, j:j + TOK], scalar=cw[:, CW * i + j:CW * i + j + 1],
                                in1=cv[:, i, :], op0=ALU.mult, op1=ALU.add)
                            if j < CW - 1:
                                link(ins)
                        ins.then_inc(s["conv_ready"], 1)
                    elif part == "DECAY_ARG":
                        dve.wait_ge(s["expb_ready"], 2 * hn + 2)
                        for i, d in enumerate(DIRS):
                            for c in range(NT):
                                ins = nc.vector.tensor_scalar(dec[:, i, c, :], out("b" + d)[:, c * P:(c + 1) * P],
                                                              sc_next(NEGB, c, d), 0.0, ALU.add, ALU.min)
                            early.reads("b" + d, ins)
                        early.wait_full(dve, "bm", hn)
                        early.reads("bm", nc.vector.tensor_scalar(decm[:, :], out("bm")[0:META, 0:META],
                                                                  sc_next(NEGB, NT, "f"), 0.0, ALU.add, ALU.min))
                        early.wait_read(dve, "bm", hn)
                        early.wait_read(dve, "bb", hn)
                    elif part == "SCALES":
                        early.wait_read(dve, "ss", hn)
                        link(nc.vector.reciprocal(inv_len[:, :], inv_len[:, :]))
                        for i in range(2):
                            for t in range(NT):
                                nc.vector.tensor_scalar(gt[:, i, t, :], ident[:, :],
                                                        inv_len[:, NC5 * i + t:NC5 * i + t + 1], None, ALU.mult)
                        nc.vector.tensor_scalar(gtm[0:META, :], ident[0:META, 0:META],
                                                inv_len[0:META, 2 * NC5 - 1:2 * NC5], None, ALU.mult)\
                            .then_inc(s["diag_ready"], 1)

                def late(h):
                    link = Chain(dve, s["dve_steps"], before, h, 3)
                    ds = slice(h, h + 1) if isinstance(h, int) else bass.ds(h, 1)
                    link(nc.vector.tensor_copy(hs[:, :, :], scal[:, :, :, :].rearrange(
                        "p k c (d h) -> p (k c) d h", d=2)[:, :, :, ds].rearrange("p k d o -> p k (d o)")))
                    dve.wait_ge(s["silu_ready"], 3 * h + 2)
                    early.wait_full(dve, "nk", h)
                    early.reads("nk", nc.vector.tensor_tensor(qk[:, 1, META:TOK], cv[:, 1, META:TOK],
                                                              out("nk")[:, :], ALU.mult))
                    early.wait_full(dve, "nm", h)
                    early.reads("nm", nc.vector.tensor_tensor(qk[:, 1, 0:META], cv[:, 1, 0:META],
                                                              out("nm")[:, 0:META], ALU.mult))
                    early.reads("nq", nc.vector.tensor_tensor(qk[:, 0, META:TOK], cv[:, 0, META:TOK],
                                                              out("nq")[:, :], ALU.mult))
                    dve.wait_ge(s["dec_ready"], 2 * h + 2)
                    bk.wait_full(dve, "kk", h)
                    for i, d in enumerate(DIRS):
                        for c in range(NT):
                            ins = nc.vector.scalar_tensor_tensor(
                                out=lt[:, i, c, :], in0=out("kk")[:, c * P:(c + 1) * P], scalar=sc(BETA, c, d),
                                in1=dec[:, i, c, :], op0=ALU.mult, op1=ALU.mult)
                    bk.reads("kk", ins)
                    bk.wait_full(dve, "kkm", h)
                    bk.reads("kkm", nc.vector.scalar_tensor_tensor(
                        out=ltm[:, :], in0=out("kkm")[0:META, 0:META], scalar=sc(BETA, NT, "f"),
                        in1=decm[:, :], op0=ALU.mult, op1=ALU.mult))
                    bk.wait_full(dve, "qk", h)
                    for i in range(2):
                        ins = nc.vector.tensor_tensor(attn[:, i, :, :], by_chunk(out("qk")[:, :]),
                                                      dec[:, i, :, :], ALU.mult)
                    bk.reads("qk", ins)
                    bk.wait_read(dve, "qk", h)
                    bk.wait_read(dve, "kkm", h)

                def grow(level, h):
                    if level == 0:
                        dve.wait_ge(s["masked_ready"], 18 * h + masked(0))
                        for i in range(2):
                            nc.vector.tensor_tensor(xt[:, i, :, :], over_chunks(ident[:, :]), lm[:, i, 0, :, :],
                                                    ALU.subtract).then_inc(s["x_start"], 1)
                        nc.vector.tensor_tensor(xm[0:META, 1, 0:META], ident[0:META, 0:META],
                                                lmm[0:META, 0, 0:META], ALU.subtract).then_inc(s["x_start"], 1)
                        return
                    for d, i in [("f", 0), ("b", 1)] + ([("m", 2)] if level < 4 else []):
                        name = f"z{d}{level}"
                        bk.wait_full(dve, name, h)
                        if d == "m":
                            bk.reads(name, nc.vector.tensor_tensor(xm[0:META, 1, 0:META], xm[0:META, 1, 0:META],
                                                                   out("ym1")[0:META, 0:META], ALU.subtract))
                        else:
                            bk.reads(name, nc.vector.tensor_tensor(xt[:, i, :, :], xt[:, i, :, :],
                                                                   by_chunk(out(name)[:, :]), ALU.subtract))

                def scan_round(steps, h):
                    for d, c in steps:
                        if c != first[d]:
                            bk.wait_full(dve, f"r{d}{c}", h)
                            bk.reads(f"r{d}{c}", nc.vector.scalar_tensor_tensor(
                                out=rhs[:, DIRS.index(d), :], in0=out(f"r{d}{c}")[:, 0:DK],
                                scalar=sc(NEGEXP, c, d), in1=v_tok[:, c, :], op0=ALU.mult, op1=ALU.add))
                    for d, c in steps:
                        if d == "f":
                            n, name = rows(c), f"w{d}{c}"
                            bk.wait_full(dve, name, h)
                            nc.vector.tensor_scalar(vn[0:n, 0, :], out(name)[0:n, 0:DK], sc(BETA, c, d),
                                                    None, ALU.mult)
                            bk.reads(name, nc.vector.tensor_scalar(v2[0:n, 0, :], out(name)[0:n, 0:DK],
                                                                   sc(BETAEND, c, d), None, ALU.mult))
                    for d, c in steps:
                        if c != final[d]:
                            i, name = DIRS.index(d), f"s{d}{c}"
                            bk.wait_full(dve, name, h)
                            if c == first[d]:
                                ins = nc.vector.tensor_copy(state[:, i, :], out(name)[:, 0:DK])
                            else:
                                ins = nc.vector.scalar_tensor_tensor(
                                    out=state[:, i, :], in0=state[:, i, :], scalar=sc(END, c, d),
                                    in1=out(name)[:, 0:DK], op0=ALU.mult, op1=ALU.add)
                            bk.reads(name, ins)

                def tail(h):
                    link = Chain(dve, s["dve_steps"], before + 1, h, 3)
                    dve.wait_ge(s["ysq_ready"], h + 1)
                    link(nc.vector.tensor_reduce(rstd[:, :], ysq[:, :, :], AX.X, ALU.add))
                    nc.vector.tensor_scalar(rstd[:, :], rstd[:, :], 1.0 / DK, RMS_EPS, ALU.mult, ALU.add)\
                        .then_inc(s["ms_ready"], 1)
                    dve.wait_ge(s["std_ready"], h + 1)
                    link(nc.vector.reciprocal(rstd[:, :], rstd[:, :]))
                    for c in range(NT):
                        ins = nc.vector.tensor_scalar(y[:, c, :], out("o")[:, c * P:(c + 1) * P],
                                                      rstd[:, c:c + 1], None, ALU.mult)
                    bk.reads("o", ins)
                    bk.wait_full(dve, "ty", h)
                    early.wait_read(dve, "z", h)
                    dst = head_of(yT, h)
                    bk.reads("ty", nc.vector.scalar_tensor_tensor(out=gz[:, :], in0=out("ty")[:, :],
                                                                  scalar=norm_g[:, 0:1], in1=gz[:, :],
                                                                  op0=ALU.mult, op1=ALU.mult))
                    dve.wait_ge(s["y_hi"], h + 1)
                    nc.vector.tensor_tensor(dst[1], gz[:, :], dst[0], ALU.subtract).then_inc(s["y_lo"], 1)

                def this(part, h):
                    if part == "late":
                        late(h)
                    elif part.startswith("level"):
                        grow(int(part[-1]), h)
                    elif part.startswith("scan"):
                        scan_round(scan[int(part[-1])], h)
                    elif part == "tail":
                        tail(h)

                run(dve, this, following)



MIX_FIRST = 4


def mixer_out(core, weights, a, h0, merged, h1T, ident):
    nc = core.nc
    with ExitStack() as ctx:
        mT = sbuf_pair(nc, ctx, "mix_T", [P, KC, SEQ])
        gain = sbuf(nc, ctx, "mix_gain", [P, D])
        bias = sbuf(nc, ctx, "mix_bias", [P, D])
        stats = sbuf(nc, ctx, "mix_stats", [P, NT, 12])
        mv = sbuf(nc, ctx, "mix_mv", [P, NT, 2])
        rstd = sbuf(nc, ctx, "mix_rstd", [P, NT])
        gb_in, steps_done, var_ready, std_ready, row_ready = (
            core.sem("mix_" + n) for n in ("gb_in", "steps", "var_ready", "std_ready", "row_ready"))
        hi_done = {kind: core.sem(f"mix_{kind}_hi") for kind in "mh"}
        order = [(f"m{t}{h}", (2 * t + h) % 8) for t in range(NT) for h in range(2)]
        order += [(f"o{t}{n}", (2 * t + n) % 8) for t in range(NT) for n in range(2)]
        order += [(f"h{t}{h}", (2 * t + h) % 8) for t in range(NT) for h in range(2)]
        bk = Banks(core, order)

        def out(name):
            return core.banks[bk.bank(name)]

        def transposed(pe, kind, src, t):
            for h in range(2):
                name = f"{kind}{t}{h}"
                bk.wait_free(pe, name)
                for c in range(4):
                    last = nc.tensor.transpose(out(name)[:, c * P:(c + 1) * P],
                                               src[:, t, (4 * h + c) * P:(4 * h + c + 1) * P], ident[:, :])
                bk.fills(name, last)

        def part(t, h):
            return slice(None), slice(4 * h, 4 * h + 4), slice(t * P, (t + 1) * P)

        def high_halves(act, kind, dst, t):
            for h in range(2):
                name = f"{kind}{t}{h}"
                bk.wait_full(act, name)
                nc.scalar.activation(dst[0][part(t, h)], out(name)[:, :].rearrange("p (c n) -> p c n", c=4),
                                     ACT.Copy).then_inc(hi_done[kind], 1)

        def low_halves(dve, kind, dst, t):
            for h in range(2):
                name = f"{kind}{t}{h}"
                dve.wait_ge(hi_done[kind], 2 * t + h + 1)
                bk.reads(name, nc.vector.tensor_tensor(
                    dst[1][part(t, h)], out(name)[:, :].rearrange("p (c n) -> p c n", c=4), dst[0][part(t, h)],
                    ALU.subtract))

        with nc.Block() as block:
            @block.sync
            def _(sp):
                sp.dma_start(gain[:, :], a["ln1_g"].partition_broadcast(P)).then_inc(gb_in, 16)
                sp.dma_start(bias[:, :], a["ln1_b"].partition_broadcast(P)).then_inc(gb_in, 16)

            @block.tensor
            def _(pe):
                for t in range(NT):
                    transposed(pe, "m", merged, t)
                for t in range(NT):
                    for h in range(2):
                        bk.wait_read(pe, f"m{t}{h}")
                    for n in range(2):
                        name = f"o{t}{n}"
                        bk.wait_free(pe, name)
                        for kc in range(KC):
                            last = pair_matmul(nc, out(name)[:, :],
                                               view(mT, slice(None), kc, slice(t * P, (t + 1) * P)),
                                               weights.block(MIX_FIRST + n, kc), kc == 0, kc == KC - 1)
                        bk.fills(name, last)
                for t in range(NT):
                    pe.wait_ge(row_ready, t + 1)
                    transposed(pe, "h", h0, t)

            @block.scalar
            def _(act):
                for t in range(NT):
                    high_halves(act, "m", mT, t)
                for t in range(NT):
                    act.wait_ge(var_ready, t + 1)
                    nc.scalar.activation(rstd[:, t:t + 1], mv[:, t, 1:2], ACT.Sqrt).then_inc(std_ready, 1)
                for t in range(NT):
                    high_halves(act, "h", h1T, t)

            @block.vector
            def _(dve):
                link = Chain(dve, steps_done)
                for t in range(NT):
                    low_halves(dve, "m", mT, t)
                dve.wait_ge(gb_in, 32)
                for t in range(NT):
                    for n in range(2):
                        name = f"o{t}{n}"
                        bk.wait_full(dve, name)
                        row = h0[:, t, n * 512:(n + 1) * 512]
                        bk.reads(name, nc.vector.scalar_tensor_tensor(out=row, in0=row, scalar=ALPHA,
                                                                      in1=out(name)[:, :], op0=ALU.mult,
                                                                      op1=ALU.add))
                        bk.wait_read(dve, name)
                    for n in range(2):
                        ins = nc.vector.bn_stats(stats[:, t, 6 * n:6 * n + 6], h0[:, t, n * 512:(n + 1) * 512])
                    link(ins)
                    link(nc.vector.bn_aggr(mv[:, t, :], stats[:, t, :]))
                    nc.vector.tensor_scalar(mv[:, t, 1:2], mv[:, t, 1:2], LN_EPS, None, ALU.add)\
                        .then_inc(var_ready, 1)
                    dve.wait_ge(std_ready, t + 1)
                    link(nc.vector.reciprocal(rstd[:, t:t + 1], rstd[:, t:t + 1]))
                    row = h0[:, t, :]
                    link(nc.vector.tensor_scalar(row, row, mv[:, t, 0:1], rstd[:, t:t + 1],
                                                 ALU.subtract, ALU.mult))
                    link(nc.vector.tensor_tensor(row, row, gain[:, :], ALU.mult))
                    nc.vector.tensor_tensor(row, row, bias[:, :], ALU.add).then_inc(row_ready, 1)
                for t in range(NT):
                    low_halves(dve, "h", h1T, t)


BLOCKS = NK
RING = 4


def over_blocks(eng, first, end, step):
    while first < RING:
        step(first, first)
        first += 1
    if end - first > RING:
        with eng.Fori(0, (end - first) // RING) as turn:
            for j in range(RING):
                step(turn * RING + (first + j), RING + j)
    else:
        for n in range(first, end):
            step(n, RING + n % RING)


def block_of(dram, n):
    if isinstance(n, int):
        return dram[n]
    one = dram[bass.ds(n, 1)]
    return one.rearrange("o p k n -> (o p) k n") if len(dram.shape) == 4 else one.rearrange("o p n -> (o p) n")


class Hidden:

    def __init__(self, core, ctx, a, h1T, hidden_dram):
        nc = self.nc = core.nc
        self.core, self.peer_u, self.xs, self.dram = core, a["peer_u"], h1T, hidden_dram
        self.u32 = sbuf(nc, ctx, "hid_u", [P, RING, KC, P])
        self.us = [sbuf(nc, ctx, f"hid_u_{n}", [P, 2, KC, P], BF16) for n in ("hi", "lo")]
        self.act_out = sbuf(nc, ctx, "hid_gelu", [P, RING, SEQ])
        self.u_in = [core.sem(f"hid_u_in{i}") for i in range(RING)]
        self.stored = [core.sem(f"hid_stored{i}") for i in range(RING)]
        self.u_hi, self.u_lo, self.formed, self.gelu = (
            core.sem("hid_" + n) for n in ("u_hi", "u_lo", "formed", "gelu"))

    def load(self, sp, n, m):
        slot = m % RING
        block = block_of(self.peer_u, n)
        if m >= RING:
            sp.wait_ge(self.u_lo, n - (RING - 1))
        sp.dma_start(self.u32[:, slot, :, :], block).then_inc(self.u_in[slot], 16)

    def store(self, sp, n, m):
        block = block_of(self.dram, n)
        sp.wait_ge(self.gelu, n + 1)
        sp.dma_start(block, self.act_out[:, m % RING, :]).then_inc(self.stored[m % RING], 16)

    def form(self, pe, n, m):
        bank = self.core.banks[4 + m % RING]
        pe.wait_ge(self.u_hi, n + 1)
        pe.wait_ge(self.u_lo, n + 1)
        if m >= RING:
            pe.wait_ge(self.gelu, n - (RING - 1))
        for kc in range(KC):
            last = pair_matmul(self.nc, bank[:, :], view(self.us, slice(None), m % 2, kc),
                               view(self.xs, slice(None), kc), kc == 0, kc == KC - 1)
        last.then_inc(self.formed, 1)

    def split_hi(self, act, n, m):
        act.wait_ge(self.u_in[m % RING], (16 // RING) * (n - m % RING) + 16)
        if m >= 2:
            act.wait_ge(self.formed, n - 1)
        self.nc.scalar.activation(self.us[0][:, m % 2, :, :], self.u32[:, m % RING, :, :],
                                  ACT.Copy).then_inc(self.u_hi, 1)

    def apply_gelu(self, act, n, m):
        act.wait_ge(self.formed, n + 1)
        if m >= RING:
            act.wait_ge(self.stored[m % RING], (16 // RING) * (n - m % RING))
        self.nc.scalar.activation(self.act_out[:, m % RING, :], self.core.banks[4 + m % RING][:, :],
                                  ACT.Gelu).then_inc(self.gelu, 1)

    def split_lo(self, pool, n, m):
        pool.wait_ge(self.u_hi, n + 1)
        if m >= 2:
            pool.wait_ge(self.formed, n - 1)
        self.nc.gpsimd.tensor_tensor(self.us[1][:, m % 2, :, :], self.u32[:, m % RING, :, :],
                                     self.us[0][:, m % 2, :, :], ALU.subtract).then_inc(self.u_lo, 1)



def retrieve(core, weights, a, h1T, picked, hidden, blocks, ident):
    nc = core.nc
    HP = 2 * PH
    share = blocks // NT
    LEAST = -3.0e38
    with ExitStack() as ctx:
        qT = sbuf(nc, ctx, "top_q", [P, HP, SEQ])
        keys = sbuf(nc, ctx, "top_keys", [P, HP, NK])
        iota = sbuf(nc, ctx, "top_iota", [P, TOPK])
        score = sbuf(nc, ctx, "top_score", [P, HP, NK])
        rest = sbuf(nc, ctx, "top_rest", [P, HP, NK])
        best = sbuf(nc, ctx, "top_best", [P, HP, TOPK])
        besti = sbuf(nc, ctx, "top_best_index", [P, HP, TOPK], U32)
        bestf = sbuf(nc, ctx, "top_best_index_f", [P, HP, TOPK])
        pairs = sbuf(nc, ctx, "top_pairs", [P, PH, TOPK, TOPK])
        left = sbuf(nc, ctx, "top_pairs_left", [P, PH, TOPK, TOPK])
        top = sbuf(nc, ctx, "top_of_pairs", [P, PH, TOPK])
        topi = sbuf(nc, ctx, "top_of_pairs_index", [P, PH, TOPK], U32)
        rank = sbuf(nc, ctx, "top_rank", [P, 2, PH, TOPK], U32)
        rankf = sbuf(nc, ctx, "top_rank_f", [P, 2, PH, TOPK])
        total = sbuf(nc, ctx, "top_total", [P, PH])
        after_wait = sbuf(nc, ctx, "top_after_wait", [P, 1])
        chosen = sbuf(nc, ctx, "top_chosen", [P, 3, PH, TOPK])
        keys_in, dve_steps, exp_arg, exp_ready, chosen_ready, turned = (
            core.sem("top_" + n) for n in ("keys_in", "dve_steps", "exp_arg", "exp_ready",
                                           "chosen_ready", "turned"))
        qb = Banks(core, [(f"q{c}", c) for c in range(4)], 4)
        bk = Banks(core, [(f"s{c}", c) for c in range(4)] + [("t", 0)], NT)

        with nc.Block() as block:
            @block.sync
            def _(sp):
                for g in range(8):
                    weights.load(sp, g, g, True)
                sp.dma_start(keys[:, :, :], a["peer_keys"]).then_inc(keys_in, 16)
                sp.dma_start(iota[:, :], a["iota"][:, 0:TOPK]).then_inc(keys_in, 16)
                for n in range(RING):
                    hidden.load(sp, n, n)
                for g in range(8, 16):
                    weights.load(sp, g, g, True)

                def store_and_load(n, m):
                    hidden.store(sp, n, m)
                    hidden.load(sp, n + RING, m + RING)

                over_blocks(sp, 0, blocks, store_and_load)

            @block.tensor
            def _(pe):
                for n in range(4):
                    for c in range(4):
                        weights.wait(pe, 4 * n + c)
                        qb.wait_free(pe, f"q{c}", n)
                        for kc in range(KC):
                            last = pair_matmul(nc, core.banks[c][:, :], weights.columns(n % weights.blocks, c, kc),
                                               view(h1T, slice(None), kc), kc == 0, kc == KC - 1)
                        qb.fills(f"q{c}", last)
                pe.wait_ge(keys_in, 32)
                for c in range(4):
                    qb.wait_read(pe, f"q{c}", 3)

                def scores(t):
                    for c in range(4):
                        bk.wait_free(pe, f"s{c}", t)
                        for j in range(4):
                            hp = 4 * c + j
                            last = nc.tensor.matmul(core.banks[c][:, j * NK:(j + 1) * NK],
                                                    qT[:, hp, t * P:(t + 1) * P], keys[:, hp, :],
                                                    start=True, stop=True)
                        bk.fills(f"s{c}", last)

                for t in range(NT):
                    scores(t)
                    over_blocks(pe, t * share, (t + 1) * share, lambda n, m: hidden.form(pe, n, m))
                    pe.wait_ge(chosen_ready, 3 * t + 3)
                    bk.wait_free(pe, "t", t)
                    for j in range(3):
                        last = nc.tensor.transpose(core.banks[0][:, j * P:(j + 1) * P],
                                                   chosen[:, j, :, :].rearrange("p h k -> p (h k)"), ident[:, :])
                    bk.fills("t", last)

            @block.scalar
            def _(act):
                for g in range(4 * weights.blocks):
                    weights.hi(act, g, g, g // 4)
                for n in range(4):
                    for c in range(4):
                        qb.wait_full(act, f"q{c}", n)
                        qb.reads(f"q{c}", nc.scalar.activation(qT[:, 4 * n + c, :], core.banks[c][:, :], ACT.Copy))
                        if n + weights.blocks < 4:
                            g = 4 * (n + weights.blocks) + c
                            weights.hi(act, g, g, n % weights.blocks)
                hidden.split_hi(act, 0, 0)

                def step(n, m):
                    hidden.split_hi(act, n + 1, m + 1)
                    hidden.apply_gelu(act, n, m)

                for t in range(NT):
                    for c in range(4):
                        bk.wait_full(act, f"s{c}", t)
                        act.wait_ge(exp_arg, t + 1)
                        bk.reads(f"s{c}", nc.scalar.activation(
                            score[:, 4 * c:4 * c + 4, :],
                            core.banks[c][:, :].rearrange("p (j n) -> p j n", j=4), ACT.Copy))
                    over_blocks(act, t * share, (t + 1) * share - RING, step)
                    act.wait_ge(exp_arg, t + 2)
                    nc.scalar.activation(top[:, :, :], top[:, :, :], ACT.Exp).then_inc(exp_ready, 1)
                    over_blocks(act, (t + 1) * share - RING, (t + 1) * share, step)
                    bk.wait_full(act, "t", t)
                    bk.reads("t", nc.scalar.activation(
                        picked[:, :, t * P:(t + 1) * P],
                        core.banks[0][:, 0:3 * P].rearrange("p (j n) -> p j n", j=3), ACT.Copy))

            @block.gpsimd
            def _(pool):
                for g in range(16):
                    weights.lo(pool, g, g, g // 4 % weights.blocks)
                over_blocks(pool, 0, blocks, lambda n, m: hidden.split_lo(pool, n, m))

            @block.vector
            def _(dve):
                nc.vector.memset(total[:, :], 0.0).then_inc(exp_arg, 1)
                dve.wait_ge(exp_arg, 1)
                dve.wait_ge(keys_in, 32)
                with dve.Fori(0, NT) as t:
                    link = Chain(dve, dve_steps, 0, t, 18)

                    def step(ins):
                        link(ins)
                        nc.vector.memset(after_wait[:, :], 0.0)

                    def best_of(values, reduced, n, out, index):
                        for i in range(n):
                            ins = nc.vector.max(out[:, i, 0:8], values[:, i, :])
                        step(ins)
                        for i in range(n):
                            nc.vector.max_index(index[:, i, 0:8], out[:, i, 0:8], values[:, i, :])
                            ins = nc.vector.match_replace(reduced[:, i, :], out[:, i, 0:8], values[:, i, :], LEAST)
                        step(ins)
                        for i in range(n):
                            ins = nc.vector.max(out[:, i, 8:16], reduced[:, i, :])
                        step(ins)
                        for i in range(n):
                            ins = nc.vector.max_index(index[:, i, 8:16], out[:, i, 8:16], reduced[:, i, :])
                        step(ins)

                    for c in range(4):
                        bk.wait_read(dve, f"s{c}", t)
                    nc.vector.memset(after_wait[:, :], 0.0)
                    best_of(score, rest, HP, best, besti)
                    by_head = best[:, :, :].rearrange("p (h s) k -> p h s k", s=2)
                    wide = [P, PH, TOPK, TOPK]
                    nc.vector.tensor_copy(bestf[:, :, :], besti[:, :, :])
                    step(nc.vector.tensor_tensor(pairs[:, :, :, :], by_head[:, :, 0, :].unsqueeze(3).broadcast_to(wide),
                                                 by_head[:, :, 1, :].unsqueeze(2).broadcast_to(wide), ALU.add))
                    best_of(pairs[:, :, :, :].rearrange("p h a b -> p h (a b)"),
                            left[:, :, :, :].rearrange("p h a b -> p h (a b)"), PH, top, topi)
                    nc.vector.tensor_scalar(rank[:, 0, :, :], topi[:, :, :], 4, None, ALU.logical_shift_right)
                    link(nc.vector.tensor_scalar(rank[:, 1, :, :], topi[:, :, :], 15, None, ALU.bitwise_and))
                    link(nc.vector.tensor_copy(rankf[:, :, :, :], rank[:, :, :, :]))
                    link(nc.vector.tensor_copy(total[:, :], top[:, :, 0]))
                    nc.vector.tensor_tensor(top[:, :, :], top[:, :, :],
                                            total[:, :].unsqueeze(2).broadcast_to([P, PH, TOPK]),
                                            ALU.subtract).then_inc(exp_arg, 1)
                    of_rank = bestf[:, :, :].rearrange("p (h s) k -> p h s k", s=2)
                    for side in range(2):
                        link(nc.vector.tensor_tensor(
                            left[:, :, :, :], rankf[:, side, :, :].unsqueeze(3).broadcast_to(wide),
                            iota[:, :].unsqueeze(1).unsqueeze(1).broadcast_to(wide), ALU.is_equal))
                        link(nc.vector.tensor_tensor(
                            left[:, :, :, :], left[:, :, :, :],
                            of_rank[:, :, side, :].unsqueeze(2).broadcast_to(wide), ALU.mult))
                        nc.vector.tensor_reduce(chosen[:, 1 + side, :, :], left[:, :, :, :], AX.X, ALU.add)\
                            .then_inc(chosen_ready, 1)
                        dve.wait_ge(chosen_ready, 3 * t + (side + 1))
                    dve.wait_ge(exp_ready, t + 1)
                    link(nc.vector.tensor_reduce(total[:, :], top[:, :, :], AX.X, ALU.add))
                    link(nc.vector.reciprocal(total[:, :], total[:, :]))
                    nc.vector.tensor_tensor(chosen[:, 0, :, :], top[:, :, :],
                                            total[:, :].unsqueeze(2).broadcast_to([P, PH, TOPK]),
                                            ALU.mult).then_inc(chosen_ready, 1)
                    dve.wait_ge(chosen_ready, 3 * t + 3)
                    link.ends_turn()


def spread(core, a, picked, weights_dram, hidden, blocks):
    nc = core.nc
    G = 4
    SLOTS = 4
    SPAN = 64
    per = SEQ // G // (BLOCKS - blocks)
    with ExitStack() as ctx:
        iota = sbuf(nc, ctx, "spread_iota", [P, NK])
        first = sbuf(nc, ctx, "spread_first", [P, SLOTS, G, NK])
        second = sbuf(nc, ctx, "spread_second", [P, SLOTS, G, NK])
        grid = sbuf(nc, ctx, "spread_grid", [P, 2, NK, SPAN])
        iota_in, first_ready, second_ready = (
            core.sem("spread_" + n) for n in ("iota_in", "first_ready", "second_ready"))
        stored = [core.sem(f"spread_stored{side}") for side in range(2)]
        TURN = SLOTS * G
        bk = Banks(core, [(f"w{u}", u) for u in range(SLOTS)], SEQ // TURN)
        spans = SEQ // SPAN
        span_turns = SPAN // TURN
        span_blocks = (BLOCKS - blocks) // spans
        turn_blocks = SLOTS // per

        with nc.Block() as block:
            @block.sync
            def _(sp):
                sp.dma_start(iota[:, :], a["iota"]).then_inc(iota_in, 16)

                def store_and_load(n, m):
                    hidden.store(sp, n, m)
                    hidden.load(sp, n + RING, m + RING)

                over_blocks(sp, blocks, BLOCKS - RING, store_and_load)
                for n in range(BLOCKS - RING, BLOCKS):
                    hidden.store(sp, n, n)
                for slot in range(RING):
                    sp.wait_ge(hidden.stored[slot], 16 * BLOCKS // RING)
                for side in range(2):
                    sp.wait_ge(stored[side], 16 * spans // 2)

            @block.vector
            def _(dve):
                dve.wait_ge(iota_in, 16)
                with dve.Fori(0, SEQ // TURN) as turn:
                    for u in range(SLOTS):
                        bk.wait_used(dve, f"w{u}", turn)
                        for j in range(G):
                            token = turn * TURN + (u * G + j)
                            ins = nc.vector.tensor_scalar(
                                first[:, u, j, :], iota[:, :],
                                picked[:, 1, bass.ds(token, 1)], picked[:, 0, bass.ds(token, 1)],
                                ALU.is_equal, ALU.mult)
                        ins.then_inc(first_ready, 1)
                        for j in range(G):
                            token = turn * TURN + (u * G + j)
                            ins = nc.vector.tensor_scalar(second[:, u, j, :], iota[:, :],
                                                          picked[:, 2, bass.ds(token, 1)], None,
                                                          ALU.is_equal)
                        ins.then_inc(second_ready, 1)

            @block.tensor
            def _(pe):
                with pe.Fori(0, SEQ // TURN // 2) as two:
                    for j in range(2 * turn_blocks):
                        turn = two * 2 + j // turn_blocks
                        hidden.form(pe, two * (2 * turn_blocks) + (blocks + j), RING + j)
                        for u in range(per * (j % turn_blocks), per * (j % turn_blocks + 1)):
                            pe.wait_ge(first_ready, SLOTS * turn + (u + 1))
                            pe.wait_ge(second_ready, SLOTS * turn + (u + 1))
                            bk.wait_free(pe, f"w{u}", turn)
                            for i in range(G):
                                last = nc.tensor.matmul(core.banks[u][:, i * NK:(i + 1) * NK], first[:, u, i, :],
                                                        second[:, u, i, :], start=True, stop=True)
                            bk.fills(f"w{u}", last)

            @block.scalar
            def _(act):
                def step(n, m, side, turn, in_span, u0, split=True):
                    if split:
                        hidden.split_hi(act, n + 1, m + 1)
                    hidden.apply_gelu(act, n, m)
                    for u in range(u0, u0 + per):
                        bk.wait_full(act, f"w{u}", turn)
                        token = in_span * TURN + u * G
                        cols = slice(token, token + G) if isinstance(token, int) else bass.ds(token, G)
                        bk.reads(f"w{u}", nc.scalar.activation(
                            grid[:, side, :, cols], core.banks[u][:, :].rearrange("p (j n) -> p n j", j=G), ACT.Copy))

                for t in range(spans):
                    if t >= 2:
                        act.wait_ge(stored[t % 2], 16 * (t // 2))
                    final = t == spans - 1
                    loops = span_turns // 2 - (1 if final else 0)
                    with act.Fori(0, loops) as two:
                        for j in range(2 * turn_blocks):
                            in_span = two * 2 + j // turn_blocks
                            step(two * (2 * turn_blocks) + (blocks + t * span_blocks + j), RING + j, t % 2,
                                 in_span + t * span_turns, in_span, per * (j % turn_blocks))
                    if final:
                        for j in range(2 * turn_blocks):
                            in_span = loops * 2 + j // turn_blocks
                            step(blocks + t * span_blocks + loops * 2 * turn_blocks + j, RING + j, t % 2,
                                 in_span + t * span_turns, in_span, per * (j % turn_blocks),
                                 split=j < 2 * turn_blocks - 1)
                    for u in range(SLOTS):
                        bk.wait_read(act, f"w{u}", (t + 1) * span_turns - 1)
                    nc.scalar.dma_start(weights_dram.rearrange("b a t -> a b t")[:, :, t * SPAN:(t + 1) * SPAN],
                                        grid[:, t % 2, :, :]).then_inc(stored[t % 2], 16)

            @block.gpsimd
            def _(pool):
                over_blocks(pool, blocks, BLOCKS, lambda n, m: hidden.split_lo(pool, n, m))



GROUP = 4


def experts(core, a, acc, hidden_dram, weights_dram):
    nc = core.nc
    with ExitStack() as ctx:
        v32 = sbuf(nc, ctx, "ex_v", [P, RING, D])
        wt = sbuf(nc, ctx, "ex_weights", [P, RING, SEQ])
        g32 = sbuf(nc, ctx, "ex_gated", [P, RING, SEQ])
        vs = [sbuf(nc, ctx, f"ex_v_{n}", [P, 2 * GROUP, D], BF16) for n in ("hi", "lo")]
        gs = [sbuf(nc, ctx, f"ex_gated_{n}", [P, 2 * GROUP, SEQ], BF16) for n in ("hi", "lo")]
        v_in = [core.sem(f"ex_v_in{i}") for i in range(RING)]
        wt_in = [core.sem(f"ex_weights_in{i}") for i in range(RING)]
        hid_in = [core.sem(f"ex_hidden_in{i}") for i in range(RING)]
        names = "v_hi v_lo gated gated_hi gated_lo unit added".split()
        s = {n: core.sem("ex_" + n) for n in names}

        def run(eng, step, last_units):
            for j in range(GROUP):
                step(j, j)
            with eng.Fori(0, (BLOCKS - 2 * GROUP) // (2 * GROUP)) as turn:
                for j in range(2 * GROUP):
                    step(turn * (2 * GROUP) + (GROUP + j), GROUP + j)
            for n in range(BLOCKS - GROUP, BLOCKS):
                step(n, n)
            for n in range(BLOCKS, BLOCKS + GROUP):
                last_units(n, n)

        def arrived(n, m):
            return (16 // RING) * (n - m % RING) + 16

        with nc.Block() as block:
            @block.sync
            def _(sp):
                def load(n, m):
                    slot = m % RING
                    hid_block, w_block, v_block = (block_of(dram, n) for dram in (hidden_dram, weights_dram,
                                                                                  a["peer_v"]))
                    if m >= RING:
                        sp.wait_ge(s["gated_lo"], n - (RING - 1))
                    sp.dma_start(g32[:, slot, :], hid_block).then_inc(hid_in[slot], 16)
                    sp.dma_start(wt[:, slot, :], w_block).then_inc(wt_in[slot], 16)
                    if m >= RING:
                        sp.wait_ge(s["v_lo"], n - (RING - 1))
                    sp.dma_start(v32[:, slot, :], v_block).then_inc(v_in[slot], 16)

                over_blocks(sp, 0, BLOCKS, load)

            @block.tensor
            def _(pe):
                def units(n, m):
                    side = (m // GROUP - 1) % 2
                    for u in (2 * (m % GROUP), 2 * (m % GROUP) + 1):
                        half, t = divmod(u, NT)
                        bank = core.banks[4 + t]
                        pe.wait_ge(s["added"], 2 * n + (u - 2 * GROUP - 2 * (m % GROUP) + 1))
                        for j in range(GROUP):
                            slot = GROUP * side + j
                            for i, (l, r) in enumerate(PASSES):
                                last = nc.tensor.matmul(bank[:, :], gs[l][:, slot, t * P:(t + 1) * P],
                                                        vs[r][:, slot, half * 512:(half + 1) * 512],
                                                        start=j == 0 and i == 0,
                                                        stop=j == GROUP - 1 and i == 2)
                        last.then_inc(s["unit"], 1)

                def step(n, m):
                    if m >= GROUP:
                        if m % GROUP == 0:
                            for name in ("gated_hi", "gated_lo", "v_hi", "v_lo"):
                                pe.wait_ge(s[name], n)
                        units(n, m)

                run(pe, step, step)

            @block.scalar
            def _(act):
                def step(n, m):
                    act.wait_ge(v_in[m % RING], arrived(n, m))
                    if m >= GROUP:
                        act.wait_ge(s["added"], 2 * n + (NT - 2 * (m % GROUP) - 2 * GROUP))
                    nc.scalar.activation(vs[0][:, m % 8, :], v32[:, m % RING, :], ACT.Copy).then_inc(s["v_hi"], 1)
                    act.wait_ge(s["gated"], n + 1)
                    nc.scalar.activation(gs[0][:, m % 8, :], g32[:, m % RING, :], ACT.Copy)\
                        .then_inc(s["gated_hi"], 1)

                run(act, step, lambda n, m: None)

            @block.gpsimd
            def _(pool):
                def step(n, m):
                    pool.wait_ge(s["v_hi"], n + 1)
                    nc.gpsimd.tensor_tensor(vs[1][:, m % 8, :], v32[:, m % RING, :], vs[0][:, m % 8, :],
                                            ALU.subtract).then_inc(s["v_lo"], 1)

                run(pool, step, lambda n, m: None)

            @block.vector
            def _(dve):
                def add_units(n, m):
                    for u in (2 * (m % GROUP), 2 * (m % GROUP) + 1):
                        half, t = divmod(u, NT)
                        dve.wait_ge(s["unit"], 2 * n + (u - 2 * GROUP - 2 * (m % GROUP) + 1))
                        part = acc[:, t, half * 512:(half + 1) * 512]
                        nc.vector.tensor_tensor(part, part, core.banks[4 + t][:, :], ALU.add)\
                            .then_inc(s["added"], 1)

                def step(n, m):
                    dve.wait_ge(hid_in[m % RING], arrived(n, m))
                    dve.wait_ge(wt_in[m % RING], arrived(n, m))
                    nc.vector.tensor_tensor(g32[:, m % RING, :], g32[:, m % RING, :], wt[:, m % RING, :], ALU.mult)\
                        .then_inc(s["gated"], 1)
                    dve.wait_ge(s["gated_hi"], n + 1)
                    nc.vector.tensor_tensor(gs[1][:, m % 8, :], g32[:, m % RING, :], gs[0][:, m % 8, :],
                                            ALU.subtract).then_inc(s["gated_lo"], 1)
                    if m >= GROUP:
                        add_units(n, m)

                for t in range(NT):
                    nc.vector.tensor_scalar(acc[:, t, :], acc[:, t, :], ALPHA, None, ALU.mult)\
                        .then_inc(s["added"], 1)
                dve.wait_ge(s["added"], NT)
                run(dve, step, add_units)


def finish(core, a, acc, out):
    nc = core.nc
    with ExitStack() as ctx:
        gain = sbuf(nc, ctx, "fin_gain", [P, D])
        bias = sbuf(nc, ctx, "fin_bias", [P, D])
        stats = sbuf(nc, ctx, "fin_stats", [P, NT, 12])
        mv = sbuf(nc, ctx, "fin_mv", [P, NT, 2])
        rstd = sbuf(nc, ctx, "fin_rstd", [P, NT])
        gb_in, steps_done, var_ready, std_ready, row_ready, stored = (
            core.sem("fin_" + n) for n in ("gb_in", "steps", "var_ready", "std_ready", "row_ready", "stored"))
        with nc.Block() as block:
            @block.sync
            def _(sp):
                sp.dma_start(gain[:, :], a["ln2_g"].partition_broadcast(P)).then_inc(gb_in, 16)
                sp.dma_start(bias[:, :], a["ln2_b"].partition_broadcast(P)).then_inc(gb_in, 16)
                for t in range(NT):
                    sp.wait_ge(row_ready, t + 1)
                    sp.dma_start(out[t * P:(t + 1) * P, :], acc[:, t, :]).then_inc(stored, 16)
                sp.wait_ge(stored, 16 * NT)

            @block.scalar
            def _(act):
                act.wait_ge(var_ready, 1)
                nc.scalar.activation(rstd[:, :], mv[:, :, 1], ACT.Sqrt).then_inc(std_ready, 1)

            @block.vector
            def _(dve):
                link = Chain(dve, steps_done)
                for t in range(NT):
                    for n in range(2):
                        ins = nc.vector.bn_stats(stats[:, t, 6 * n:6 * n + 6], acc[:, t, n * 512:(n + 1) * 512])
                link(ins)
                for t in range(NT):
                    ins = nc.vector.bn_aggr(mv[:, t, :], stats[:, t, :])
                link(ins)
                nc.vector.tensor_scalar(mv[:, :, 1], mv[:, :, 1], LN_EPS, None, ALU.add).then_inc(var_ready, 1)
                dve.wait_ge(std_ready, 1)
                link(nc.vector.reciprocal(rstd[:, :], rstd[:, :]))
                dve.wait_ge(gb_in, 32)
                for t in range(NT):
                    row = acc[:, t, :]
                    link(nc.vector.tensor_scalar(row, row, mv[:, t, 0:1], rstd[:, t:t + 1],
                                                 ALU.subtract, ALU.mult))
                    link(nc.vector.tensor_tensor(row, row, gain[:, :], ALU.mult))
                    nc.vector.tensor_tensor(row, row, bias[:, :], ALU.add).then_inc(row_ready, 1)


def program(nc, a, out):
    with ExitStack() as ctx:
        core = Core(nc, ctx)
        hidden_dram = nc.dram_tensor("expert_hidden", [NK, NK, SEQ], F32).ap()
        weights_dram = nc.dram_tensor("expert_weights", [NK, NK, SEQ], F32).ap()
        ident = sbuf(nc, ctx, "ident", [P, P])
        h0 = sbuf(nc, ctx, "h0", [P, NT, D])
        hT = sbuf_pair(nc, ctx, "hT", [P, KC, TOK])
        weights = Weights(core)
        embed(core, a, h0, hT, ident)
        h1T = view(hT, slice(None), slice(None), slice(META, TOK))
        with ExitStack() as mixer:
            merged = sbuf(nc, mixer, "merged", [P, NT, D])
            with ExitStack() as part:
                yT = sbuf_pair(nc, part, "ret_yT", [P, 4 * RH, SEQ])
                weights.open(part, "ret", 3, a["w_ret"])
                retention(core, weights, a, hT, yT, merged, ident)
                weights.close(12 * RH)
                weights.dram = a["w_ret_out"]
                branch_out(core, weights, "ret_out", hT, yT, 4 * RH, 3, merged, False)
                weights.close(24)
            with ExitStack() as part:
                yT = sbuf_pair(nc, part, "dn_yT", [P, DH, SEQ])
                with ExitStack() as heads:
                    weights.open(heads, "dn", 1, a["w_dn"])
                    delta_net(core, weights, a, hT, yT, ident)
                    weights.close(4 * DH)
                weights.open(part, "dn_out", 6, a["w_dn_out"])
                branch_out(core, weights, "dn_out", hT, yT, DH, 0, merged, True, extra=2)
                mixer_out(core, weights, a, h0, merged, h1T, ident)
                weights.close(24)
        with ExitStack() as part:
            picked = sbuf(nc, part, "picked", [P, 3, SEQ])
            hidden = Hidden(core, part, a, h1T, hidden_dram)
            with ExitStack() as queries:
                weights.open(queries, "top", 2, a["w_query"])
                retrieve(core, weights, a, h1T, picked, hidden, BLOCKS // 2, ident)
            spread(core, a, picked, weights_dram, hidden, BLOCKS // 2)
        experts(core, a, h0, hidden_dram, weights_dram)
        finish(core, a, h0, out)


def shape_constants():
    pos = np.arange(TOK, dtype=np.float32)
    inv = (1.0 / (np.float32(10000.0) ** (np.arange(0, RDK, 2, dtype=np.float32) / np.float32(RDK)))).astype(np.float32)
    ang = inv[:, None] * pos[None, :]
    delta = np.arange(STRIP)[None, :] - (NT - 1) * P - np.arange(P)[:, None]
    return {
        "ident": np.eye(P, dtype=np.float32),
        "cos": np.cos(ang).astype(np.float32),
        "sin": np.sin(ang).astype(np.float32),
        "ahead": np.maximum(delta, 0).astype(np.float32),
        "behind": np.maximum(-delta, 0).astype(np.float32),
        "upper": np.triu(np.ones((P, P), np.float32)),
        "lower": np.tril(np.ones((P, P), np.float32)),
        "masks": level_masks(),
        "iota": np.tile(np.arange(NK, dtype=np.float32), (P, 1)),
    }


def level_masks():
    j, i = np.arange(P)[:, None], np.arange(P)[None, :]
    out = np.zeros((P, 2, LEVELS, P), np.float32)
    for level in range(LEVELS):
        n = 2 ** level
        same = i // (2 * n) == j // (2 * n)
        out[:, 0, level] = same & (i // n > j // n)
        out[:, 1, level] = same & (i // n < j // n)
    return out


def laid_out(x, meta_tokens, emb_ln_g, emb_ln_b, w_in, ret_decay_logit, dn_conv, dn_a_log, dn_dt_bias,
             dn_norm_g, p_ret, p_dn, w_out, ln1_g, ln1_b, peer_wq, peer_keys, peer_u, peer_v, ln2_g, ln2_b):
    c = np.ascontiguousarray

    def rows_in_chunks(w):
        return w.reshape(-1, P, w.shape[-1]).transpose(1, 0, 2)

    def slices(parts):
        w = np.concatenate(parts, 1)
        return c(w.reshape(KC, P, -1, P).transpose(2, 1, 0, 3))

    ends = np.cumsum([1024, 1024, 2048, 2048, 1024, 1024, 1024, 1024, 16, 16, 1024, 1024])
    rq, rk, rv, rg, dq, dk, dv, dz, da, db, ga, gb = np.split(w_in[0], ends[:-1], axis=1)
    ret_out, ret_out_rest = ([ga[:, n:n + 512], p_ret[0][:D, n:n + 512], p_ret[0][D:, n:n + 512]]
                             for n in (0, 512))
    return {
        "x": c(x[0]), "meta": c(meta_tokens), "emb_g": c(emb_ln_g), "emb_b": c(emb_ln_b),
        "ret_logit": c(ret_decay_logit[0].reshape(-1)),
        "w_ret": slices([m[:, h * n:(h + 1) * n] for h in range(RH)
                         for m, n in ((rq, RDK), (rk, RDK), (rv, RDV), (rg, RDV))] + ret_out),
        "w_ret_out": slices(ret_out + ret_out_rest),
        "w_dn": slices([m[:, h * DK:(h + 1) * DK] for h in range(DH) for m in (dq, dk, dv, dz)]),
        "w_dn_out": slices([gb[:, :512], p_dn[0][:, :512], gb[:, 512:], p_dn[0][:, 512:],
                            w_out[0][:, :512], w_out[0][:, 512:]]),
        "w_query": slices([peer_wq[0]]),
        "w_dn_ab": c(rows_in_chunks(np.concatenate([da, db], 1))),
        "dn_conv": c(dn_conv[0].reshape(CW, 3, DH, P).transpose(3, 2, 1, 0).reshape(P, DH, 3 * CW)),
        "dn_norm_g": c(dn_norm_g[0][:, None]), "dn_dt_bias": c(dn_dt_bias[0].reshape(-1)),
        "dn_a_log": c(dn_a_log[0].reshape(-1)),
        "ln1_g": c(ln1_g[0]), "ln1_b": c(ln1_b[0]),
        "peer_keys": c(peer_keys[0].transpose(3, 0, 1, 2).reshape(P, 2 * PH, NK)),
        "peer_u": c(peer_u[0].reshape(NK, NK, KC, P).transpose(1, 3, 2, 0)),
        "peer_v": c(peer_v[0].reshape(NK, NK, D).transpose(1, 0, 2)),
        "ln2_g": c(ln2_g[0]), "ln2_b": c(ln2_b[0]),
        **shape_constants(),
    }


def kernel(**inputs):
    import concourse.bacc as bacc
    from concourse.bass_utils import run_bass_kernel_spmd as run

    nc = bacc.Bacc("TRN2", target_bir_lowering=False, num_devices=1)
    arrays, a = {}, {}
    for name, array in laid_out(**{n: np.asarray(v) for n, v in inputs.items()}).items():
        arrays[f"in_{name}"] = array
        a[name] = nc.dram_tensor(f"in_{name}", array.shape, mybir.dt.from_np(array.dtype),
                                 kind="ExternalInput").ap()
    out = nc.dram_tensor("out_0", (SEQ, D), F32, kind="ExternalOutput").ap()
    program(nc, a, out)
    result = run(nc, [arrays], core_ids=[0])
    return result.results[0]["out_0"].reshape(1, SEQ, D)
```

```python
from contextlib import ExitStack

import numpy as np

import concourse.bass as bass
from concourse import mybir
from concourse.alu_op_type import AluOpType as ALU

ACT = mybir.ActivationFunctionType
AX = mybir.AxisListType
F32 = mybir.dt.float32
BF16 = mybir.dt.bfloat16
U32 = mybir.dt.uint32

P = 128
D = 1024
KC = D // P
SEQ = 512
META = 16
TOK = SEQ + META
NT = SEQ // P
RH, RDK, RDV = 4, 256, 512
DH, DK = 8, 128
CW = 5
PH, NK, TOPK = 8, 128, 16
ALPHA = 2.0 ** 0.25
LN_EPS, RMS_EPS = 1e-5, 1e-6
STRIP = SEQ + (NT - 1) * P + META
LEVELS = 7


def tok_cols(t):
    return slice(0, META) if t == NT else slice(META + t * P, META + (t + 1) * P)


def rows(t):
    return META if t == NT else P


class Banks:

    def __init__(self, core, order, turns=1):
        self.uses, self.place = {}, {}
        self.full, self.free, self.base = core.full, core.free, list(core.products)
        for name, b in order:
            k = self.uses.get(b, 0)
            self.place[name] = (b, k)
            self.uses[b] = k + 1
        for b, n in self.uses.items():
            core.products[b] += n * turns

    def bank(self, name):
        return self.place[name][0]

    def count(self, name, turn, done):
        b, k = self.place[name]
        return turn * self.uses[b] + (self.base[b] + k + (1 if done else 0))

    def wait_free(self, eng, name, turn=0):
        eng.wait_ge(self.free[self.bank(name)], self.count(name, turn, False))

    def wait_full(self, eng, name, turn=0):
        eng.wait_ge(self.full[self.bank(name)], self.count(name, turn, True))

    def wait_used(self, eng, name, turn=0):
        eng.wait_ge(self.full[self.bank(name)], self.count(name, turn, False))

    def wait_read(self, eng, name, turn=0):
        eng.wait_ge(self.free[self.bank(name)], self.count(name, turn, True))

    def fills(self, name, ins):
        ins.then_inc(self.full[self.bank(name)], 1)

    def reads(self, name, ins):
        ins.then_inc(self.free[self.bank(name)], 1)


class Chain:

    def __init__(self, eng, sem, base=0, turn=0, per_turn=0):
        self.eng, self.sem, self.base, self.turn, self.per_turn, self.n = eng, sem, base, turn, per_turn, 0

    def __call__(self, ins):
        ins.then_inc(self.sem, 1)
        self.n += 1
        self.eng.wait_ge(self.sem, self.turn * self.per_turn + (self.base + self.n))

    def ends_turn(self):
        assert self.n == self.per_turn, self.n


class Core:

    def __init__(self, nc, ctx):
        self.nc, self.ctx = nc, ctx
        self.banks = [ctx.enter_context(nc.psum_tensor(f"bank{b}", [P, 512], F32)) for b in range(8)]
        self.full = [self.sem(f"bank{b}_full") for b in range(8)]
        self.free = [self.sem(f"bank{b}_free") for b in range(8)]
        self.products = [0] * 8

    def sem(self, name):
        return self.ctx.enter_context(self.nc.semaphore(name))


def sbuf(nc, ctx, name, shape, dtype=F32):
    return ctx.enter_context(nc.sbuf_tensor(name, shape, dtype))


def sbuf_pair(nc, ctx, name, shape):
    return [sbuf(nc, ctx, f"{name}_{half}", shape, BF16) for half in ("hi", "lo")]



PASSES = ((0, 0), (0, 1), (1, 0))


def pair_matmul(nc, out, left, right, start, stop):
    for i, (l, r) in enumerate(PASSES):
        last = nc.tensor.matmul(out, left[l], right[r], start=start and i == 0,
                                stop=stop and i == len(PASSES) - 1)
    return last


def view(pair, *at):
    return [half[at] for half in pair]


class Weights:

    RING = 4

    def __init__(self, core):
        self.core, self.nc, self.first = core, core.nc, 0
        self.arrived = [core.sem(f"w_slice_in{i}") for i in range(self.RING)]
        self.hi_done, self.lo_done = core.sem("w_hi_done"), core.sem("w_lo_done")

    def open(self, ctx, name, blocks, dram):
        self.raw = sbuf(self.nc, ctx, f"{name}_w_raw", [P, self.RING, KC, P])
        self.pairs, self.dram = [], dram
        self.extend(ctx, name, blocks)

    def extend(self, ctx, name, blocks):
        self.pairs += [sbuf_pair(self.nc, ctx, f"{name}_w{b}", [P, 4, KC, P]) for b in range(blocks)]
        self.blocks = len(self.pairs)

    def close(self, slices):
        self.first += slices

    def load(self, sp, g, m, waits):
        source = self.dram[g] if isinstance(g, int) else \
            self.dram[bass.ds(g, 1)].rearrange("o p k n -> (o p) k n")
        if waits:
            sp.wait_ge(self.lo_done, g + (self.first - self.RING + 1))
        sp.dma_start(self.raw[:, m % self.RING, :, :], source).then_inc(self.arrived[m % self.RING], 16)

    def hi(self, act, g, m, slot):
        act.wait_ge(self.arrived[m % self.RING],
                    (16 // self.RING) * (g - m % self.RING) + ((16 // self.RING) * self.first + 16))
        self.nc.scalar.activation(self.pairs[slot][0][:, m % 4, :, :], self.raw[:, m % self.RING, :, :],
                                  ACT.Copy).then_inc(self.hi_done, 1)

    def lo(self, pool, g, m, slot):
        pool.wait_ge(self.hi_done, g + (self.first + 1))
        self.nc.gpsimd.tensor_tensor(self.pairs[slot][1][:, m % 4, :, :], self.raw[:, m % self.RING, :, :],
                                     self.pairs[slot][0][:, m % 4, :, :], ALU.subtract).then_inc(self.lo_done, 1)

    def wait(self, pe, g):
        pe.wait_ge(self.lo_done, g + (self.first + 1))

    def columns(self, slot, c, kc):
        return view(self.pairs[slot], slice(None), c, kc)

    def block(self, slot, kc):
        return view(self.pairs[slot], slice(None), slice(None), kc)



def norm_stats(nc, link, src, n, width, stats, mv, eps):
    step = 512
    for j in range(width // step):
        link(nc.vector.bn_stats(stats[0:n, 6 * j:6 * j + 6], src[:, j * step:(j + 1) * step]))
    link(nc.vector.bn_aggr(mv[0:n, 0:2], stats[0:n, 0:6 * (width // step)]))
    link(nc.vector.tensor_scalar(mv[0:n, 1:2], mv[0:n, 1:2], eps, None, ALU.add))


def embed(core, weights, ready, a, h0, hT, ident):
    nc = core.nc
    with ExitStack() as ctx:
        hm = sbuf(nc, ctx, "embed_meta", [META, D])
        gain = sbuf(nc, ctx, "embed_gain", [P, D])
        bias = sbuf(nc, ctx, "embed_bias", [P, D])
        stats = sbuf(nc, ctx, "embed_stats", [P, NT + 1, 12])
        mv = sbuf(nc, ctx, "embed_mv", [P, NT + 1, 2])
        rstd = sbuf(nc, ctx, "embed_rstd", [P, NT + 1, 1])
        shift = sbuf(nc, ctx, "embed_shift", [P, NT + 1])
        x_in = [core.sem(f"embed_x_in{t}") for t in range(NT + 1)]
        gb_in, shift_ready, normed = core.sem("embed_gb_in"), core.sem("embed_shift"), core.sem("embed_normed")
        id_in, hi_ready = core.sem("ident_in"), core.sem("embed_hi_ready")
        chain, var_ok, std_ok, row_ok = (core.sem(f"embed_{n}") for n in ("chain", "var", "std", "row"))
        order = [(f"t{t}h{h}", (2 * t + h) % 8) for t in range(NT + 1) for h in range(2)]
        bk = Banks(core, order)

        def tile(t):
            return hm[:, :] if t == NT else h0[:, t, :]

        with nc.Block() as block:
            @block.sync
            def _(sp):
                for t in range(NT):
                    sp.dma_start(h0[:, t, :], a["x"][t * P:(t + 1) * P, :]).then_inc(x_in[t], 16)
                sp.dma_start(hm[:, :], a["meta"]).then_inc(x_in[NT], 16)
                sp.dma_start(gain[:, :], a["emb_g"].partition_broadcast(P)).then_inc(gb_in, 16)
                sp.dma_start(bias[:, :], a["emb_b"].partition_broadcast(P)).then_inc(gb_in, 16)
                sp.dma_start(ident[:, :], a["ident"]).then_inc(id_in, 16)
                for g in range(ready):
                    weights.load(sp, g, g, g >= weights.RING)

            @block.gpsimd
            def _(pool):
                for g in range(ready):
                    weights.lo(pool, g, g, g // 4)

            @block.vector
            def _(dve):
                link = Chain(dve, chain)

                def low_halves(dve, t):
                    for h in range(2):
                        name, cols = f"t{t}h{h}", tok_cols(t)
                        dve.wait_ge(hi_ready, 2 * t + h + 1)
                        src = core.banks[bk.bank(name)][:, :].rearrange("p (k n) -> p k n", k=4)[:, :, 0:rows(t)]
                        bk.reads(name, nc.vector.tensor_tensor(hT[1][:, 4 * h:4 * h + 4, cols], src,
                                                               hT[0][:, 4 * h:4 * h + 4, cols], ALU.subtract))

                for t in range(NT + 1):
                    n = rows(t)
                    dve.wait_ge(x_in[t], 16)
                    norm_stats(nc, link, tile(t), n, D, stats[:, t, :], mv[:, t, :], LN_EPS)
                nc.vector.tensor_copy(rstd[0:1, 0, :], mv[0:1, 0, 1:2]).then_inc(var_ok, 1)
                dve.wait_ge(std_ok, 2)
                link(nc.vector.reciprocal(rstd[:, 0:NT, 0], rstd[:, 0:NT, 0]))
                link(nc.vector.reciprocal(rstd[0:META, NT, :], rstd[0:META, NT, :]))
                nc.vector.tensor_tensor(shift[:, 0:NT], mv[:, 0:NT, 0], rstd[:, 0:NT, 0], ALU.mult)
                link(nc.vector.tensor_tensor(shift[0:META, NT:NT + 1], mv[0:META, NT, 0:1], rstd[0:META, NT, :],
                                             ALU.mult))
                nc.vector.tensor_scalar(shift[:, 0:NT], shift[:, 0:NT], -1.0, None, ALU.mult)
                nc.vector.tensor_scalar(shift[0:META, NT:NT + 1], shift[0:META, NT:NT + 1], -1.0, None, ALU.mult)\
                    .then_inc(shift_ready, 1)
                dve.wait_ge(gb_in, 32)
                for t in range(NT + 1):
                    n, row = rows(t), tile(t)
                    dve.wait_ge(normed, t + 1)
                    link(nc.vector.tensor_tensor(row, row, gain[0:n, :], ALU.mult))
                    nc.vector.tensor_tensor(row, row, bias[0:n, :], ALU.add).then_inc(row_ok, 1)
                    if t:
                        low_halves(dve, t - 1)
                low_halves(dve, NT)

            @block.scalar
            def _(act):
                act.wait_ge(var_ok, 1)
                nc.scalar.activation(rstd[:, 0:NT, 0], mv[:, 0:NT, 1], ACT.Sqrt).then_inc(std_ok, 1)
                nc.scalar.activation(rstd[0:META, NT, :], mv[0:META, NT, 1:2], ACT.Sqrt).then_inc(std_ok, 1)
                act.wait_ge(shift_ready, 1)
                for t in range(NT + 1):
                    n = rows(t)
                    nc.scalar.activation(tile(t), tile(t), ACT.Identity, bias=shift[0:n, t:t + 1],
                                         scale=rstd[0:n, t, :]).then_inc(normed, 1)
                for t in range(NT + 1):
                    n = rows(t)
                    for h in range(2):
                        name = f"t{t}h{h}"
                        b = bk.bank(name)
                        bk.wait_full(act, name)
                        src = core.banks[b][:, :].rearrange("p (k n) -> p k n", k=4)[:, :, 0:n]
                        nc.scalar.activation(hT[0][:, 4 * h:4 * h + 4, tok_cols(t)], src,
                                             ACT.Copy).then_inc(hi_ready, 1)
                    for g in range(ready * t // (NT + 1), ready * (t + 1) // (NT + 1)):
                        weights.hi(act, g, g, g // 4)

            @block.tensor
            def _(pe):
                pe.wait_ge(id_in, 16)
                for t in range(NT + 1):
                    n = rows(t)
                    pe.wait_ge(row_ok, t + 1)
                    for h in range(2):
                        name = f"t{t}h{h}"
                        b = bk.bank(name)
                        bk.wait_free(pe, name)
                        for k in range(4):
                            c = 4 * h + k
                            last = nc.tensor.transpose(core.banks[b][:, k * P:k * P + n],
                                                       tile(t)[:, c * P:(c + 1) * P], ident[0:n, 0:n])
                        last.then_inc(bk.full[b], 1)



def retention(core, weights, ready, a, hT, yT, work, ident):
    nc = core.nc
    with ExitStack() as ctx:
        cos = sbuf(nc, ctx, "ret_cos", [P, TOK])
        sin = sbuf(nc, ctx, "ret_sin", [P, TOK])
        ahead = sbuf(nc, ctx, "ret_ahead", [P, STRIP])
        behind = sbuf(nc, ctx, "ret_behind", [P, STRIP])
        ld = sbuf(nc, ctx, "ret_logdec", [P, 2, RH])
        lw = sbuf(nc, ctx, "ret_logdec_work", [P, 2, RH])
        ldh = sbuf(nc, ctx, "ret_logdec_head", [P, 2])
        strip = sbuf(nc, ctx, "ret_strip", [P, STRIP])
        q = sbuf(nc, ctx, "ret_q", [P, 2, SEQ])
        k = sbuf(nc, ctx, "ret_k", [P, 2, TOK])
        tmp = sbuf(nc, ctx, "ret_tmp", [P, 2, SEQ])
        v = sbuf(nc, ctx, "ret_v", [P, NT, RDV])
        vm = sbuf(nc, ctx, "ret_v_meta", [META, RDV])
        y, gate = work[:, :, 0:RDV], work[:, :, RDV:2 * RDV]
        sd = sbuf(nc, ctx, "ret_scores", [P, NT + 1, SEQ])
        stats = sbuf(nc, ctx, "ret_stats", [P, NT, 6])
        mv = sbuf(nc, ctx, "ret_mv", [P, NT, 2])
        rstd = sbuf(nc, ctx, "ret_rstd", [P, NT, 1])
        after_wait = sbuf(nc, ctx, "ret_after_wait", [P, 1])
        tables_in, logit_in, y_hi = (core.sem("ret_" + n) for n in ("tables_in", "logit_in", "y_hi"))
        rstd_ready = core.sem("ret_rstd_ready")
        act_steps, dve_steps, logit_ready, strip_arg, strip_ready, q_ready, k_ready, var_ready, std_ready, y_ready = (
            core.sem("ret_" + n) for n in ("act_steps", "dve_steps", "logit_ready", "strip_arg", "strip_ready",
                                           "q_ready", "k_ready", "var_ready", "std_ready", "y_ready"))
        order = ([("q0", 0), ("q1", 1), ("k0", 2), ("k1", 3), ("km", 4)]
                 + [("v0", 5), ("v1", 6), ("v2", 7), ("v3", 0), ("v4", 1)]
                 + [("g0", 2), ("g1", 3), ("g2", 4), ("g3", 5)]
                 + [("s0", 6), ("s1", 7), ("s2", 0), ("s3", 1), ("s4", 2)]
                 + [("o0", 3), ("o1", 4), ("o2", 5), ("o3", 6)]
                 + [("y0", 7), ("y1", 0), ("y2", 1), ("y3", 2)])
        bk = Banks(core, order, RH)

        def out(name):
            return core.banks[bk.bank(name)]

        blocks = (("qk", "km"), ("v", "v4"), ("g", "g3"))
        B = len(blocks)

        with nc.Block() as block:
            @block.sync
            def _(sp):
                sp.dma_start(ld[:, :, :].rearrange("p a b -> p (a b)"),
                             a["ret_logit"].partition_broadcast(P)).then_inc(logit_in, 16)
                for table, name in ((cos, "cos"), (sin, "sin"), (ahead, "ahead"), (behind, "behind")):
                    sp.dma_start(table[:, :], a[name]).then_inc(tables_in, 16)
                for g in range(ready, 4 * B):
                    weights.load(sp, g, g, True)
                with sp.Fori(0, RH) as h:
                    for g in range(4 * B):
                        weights.load(sp, h * (4 * B) + (4 * B + g), g, True)

            @block.gpsimd
            def _(pool):
                for g in range(ready, 4 * B):
                    weights.lo(pool, g, g, g // 4)
                with pool.Fori(0, RH) as h:
                    for g in range(4 * B):
                        weights.lo(pool, h * (4 * B) + (4 * B + g), g, g // 4)

            @block.tensor
            def _(pe):
                with pe.Fori(0, RH) as h:
                    for c, name in enumerate(("q0", "q1", "k0", "k1")):
                        weights.wait(pe, h * (4 * B) + c)
                        bk.wait_free(pe, name, h)
                        if name == "k0":
                            bk.wait_free(pe, "km", h)
                        for kc in range(KC):
                            left, ends = weights.columns(0, c, kc), dict(start=kc == 0, stop=kc == KC - 1)
                            last = pair_matmul(nc, out(name)[:, :], left,
                                               view(hT, slice(None), kc, slice(META, TOK)), **ends)
                            if kc == KC - 1:
                                bk.fills(name, last)
                            if c >= 2:
                                last = pair_matmul(nc, out("km")[:, (c - 2) * META:(c - 1) * META], left,
                                                   view(hT, slice(None), kc, slice(0, META)), **ends)
                    bk.fills("km", last)
                    for b, kind, tiles in ((1, "v", NT + 1), (2, "g", NT)):
                        weights.wait(pe, h * (4 * B) + (4 * b + 3))
                        for t in range(tiles):
                            name = f"{kind}{t}"
                            bk.wait_free(pe, name, h)
                            for kc in range(KC):
                                last = pair_matmul(nc, out(name)[0:rows(t), :],
                                                   view(hT, slice(None), kc, tok_cols(t)),
                                                   weights.block(b, kc), kc == 0, kc == KC - 1)
                            bk.fills(name, last)
                    pe.wait_ge(q_ready, h + 1)
                    pe.wait_ge(k_ready, 2 * h + 2)
                    for t in range(NT + 1):
                        bk.wait_free(pe, f"s{t}", h)
                        for c in range(2):
                            last = nc.tensor.matmul(out(f"s{t}")[0:rows(t), :], k[:, c, tok_cols(t)],
                                                    q[:, c, :], start=c == 0, stop=c == 1)
                        bk.fills(f"s{t}", last)
                    for t in range(NT + 1):
                        bk.wait_read(pe, f"v{t}", h)
                        bk.wait_read(pe, f"s{t}", h)
                    for i in range(NT):
                        bk.wait_free(pe, f"o{i}", h)
                        for t in range(NT + 1):
                            n = rows(t)
                            value = vm[:, :] if t == NT else v[:, t, :]
                            last = nc.tensor.matmul(out(f"o{i}")[:, :], sd[0:n, t, i * P:(i + 1) * P],
                                                    value, start=t == 0, stop=t == NT)
                        bk.fills(f"o{i}", last)
                    for i in range(NT):
                        pe.wait_ge(y_ready, NT * h + (i + 1))
                        bk.wait_free(pe, f"y{i}", h)
                        for c in range(4):
                            last = nc.tensor.transpose(out(f"y{i}")[:, c * P:(c + 1) * P],
                                                       y[:, i, c * P:(c + 1) * P], ident[:, :])
                        bk.fills(f"y{i}", last)

            @block.scalar
            def _(act):
                act.wait_ge(logit_ready, 1)
                link = Chain(act, act_steps)
                link(nc.scalar.activation(lw[:, :, :], lw[:, :, :], ACT.Exp, scale=-1.0))
                link(nc.scalar.activation(lw[:, :, :], lw[:, :, :], ACT.Ln, bias=1.0))

                def following(b, h):
                    bk.wait_full(act, blocks[b][1], h)
                    for c in range(4):
                        weights.hi(act, h * (4 * B) + (4 * B + 4 * b + c), 4 * b + c, b)

                for g in range(ready, 4 * B):
                    weights.hi(act, g, g, g // 4)
                with act.Fori(0, RH) as h:
                    act.wait_ge(strip_arg, h + 1)
                    nc.scalar.activation(strip[:, :], strip[:, :], ACT.Exp).then_inc(strip_ready, 1)
                    for t in range(NT + 1):
                        bk.wait_full(act, f"v{t}", h)
                        dst = vm[:, :] if t == NT else v[:, t, :]
                        bk.reads(f"v{t}", nc.scalar.activation(dst, out(f"v{t}")[0:rows(t), :], ACT.Copy))
                    following(0, h)
                    for t in range(NT):
                        bk.wait_full(act, f"g{t}", h)
                        bk.reads(f"g{t}", nc.scalar.activation(gate[:, t, :], out(f"g{t}")[:, :], ACT.Silu))
                    following(1, h)
                    following(2, h)
                    act.wait_ge(var_ready, NT * h + NT)
                    nc.scalar.activation(rstd[:, :, 0], mv[:, :, 1], ACT.Sqrt).then_inc(std_ready, 1)
                    for i in range(NT):
                        bk.wait_full(act, f"y{i}", h)
                        nc.scalar.activation(yT[0][:, bass.ds(4 * h, 4), i * P:(i + 1) * P],
                                             out(f"y{i}")[:, :].rearrange("p (c n) -> p c n", c=4),
                                             ACT.Copy).then_inc(y_hi, 1)

            @block.vector
            def _(dve):
                link = Chain(dve, dve_steps)
                dve.wait_ge(logit_in, 16)
                link(nc.vector.tensor_scalar(lw[:, :, :], ld[:, :, :], -1.0, None, ALU.mult))
                nc.vector.tensor_tensor(lw[:, :, :], lw[:, :, :], ld[:, :, :], ALU.max).then_inc(logit_ready, 1)
                link(nc.vector.tensor_scalar(ld[:, :, :], ld[:, :, :], -1.0, 0.0, ALU.mult, ALU.max))
                dve.wait_ge(act_steps, 2)
                link(nc.vector.tensor_tensor(ld[:, :, :], ld[:, :, :], lw[:, :, :], ALU.add))
                link(nc.vector.tensor_scalar(ld[:, :, :], ld[:, :, :], -1.0, None, ALU.mult))
                dve.wait_ge(tables_in, 64)
                before = link.n
                with dve.Fori(0, RH) as h:
                    link = Chain(dve, dve_steps, before, h, 16)
                    link(nc.vector.tensor_copy(ldh[:, :], ld[:, :, bass.ds(h, 1)].rearrange("p a o -> p (a o)")))
                    link(nc.vector.tensor_scalar(strip[:, :], ahead[:, :], ldh[:, 0:1], None, ALU.mult))
                    nc.vector.scalar_tensor_tensor(out=strip[:, :], in0=behind[:, :], scalar=ldh[:, 1:2],
                                                   in1=strip[:, :], op0=ALU.mult, op1=ALU.add)\
                        .then_inc(strip_arg, 1)
                    for names, dst, col, at, n in ((("q0", "q1"), q, 0, META, SEQ), (("k0", "k1"), k, META, META, SEQ),
                                                   (("km",), k, 0, 0, META)):
                        for name in names:
                            bk.wait_full(dve, name, h)
                        if len(names) == 2:
                            x1, x2 = out(names[0])[:, :], out(names[1])[:, :]
                        else:
                            x1, x2 = out("km")[:, 0:META], out("km")[:, META:2 * META]
                        cs, sn = cos[:, at:at + n], sin[:, at:at + n]
                        nc.vector.tensor_tensor(tmp[:, 0, 0:n], x1, cs, ALU.mult)
                        link(nc.vector.tensor_tensor(tmp[:, 1, 0:n], x2, sn, ALU.mult))
                        link(nc.vector.tensor_tensor(dst[:, 0, col:col + n], tmp[:, 0, 0:n], tmp[:, 1, 0:n],
                                                     ALU.subtract))
                        ins = nc.vector.tensor_tensor(tmp[:, 0, 0:n], x1, sn, ALU.mult)
                        if len(names) == 2:
                            bk.reads(names[0], ins)
                        bk.reads(names[-1], nc.vector.tensor_tensor(tmp[:, 1, 0:n], x2, cs, ALU.mult))
                        bk.wait_read(dve, names[-1], h)
                        nc.vector.tensor_tensor(dst[:, 1, col:col + n], tmp[:, 0, 0:n], tmp[:, 1, 0:n],
                                                ALU.add).then_inc(q_ready if dst is q else k_ready, 1)
                        if dst is q:
                            dve.wait_ge(q_ready, h + 1)
                        else:
                            dve.wait_ge(k_ready, 2 * h + (1 if len(names) == 2 else 2))
                    dve.wait_ge(strip_ready, h + 1)
                    for t in range(NT + 1):
                        n = rows(t)
                        bk.wait_full(dve, f"s{t}", h)
                        x0 = (NT - 1) * P + META if t == NT else (NT - 1 - t) * P
                        bk.reads(f"s{t}", nc.vector.scalar_tensor_tensor(
                            out=sd[0:n, t, :], in0=out(f"s{t}")[0:n, :], scalar=RDK ** -0.5,
                            in1=strip[0:n, x0:x0 + SEQ], op0=ALU.mult, op1=ALU.mult))
                    for i in range(NT):
                        bk.wait_full(dve, f"o{i}", h)
                        link(nc.vector.bn_stats(stats[:, i, :], out(f"o{i}")[:, :]))
                        nc.vector.memset(after_wait[:, :], 0.0)
                        link(nc.vector.bn_aggr(mv[:, i, :], stats[:, i, :]))
                        nc.vector.tensor_scalar(mv[:, i, 1:2], mv[:, i, 1:2], LN_EPS, None, ALU.add)\
                            .then_inc(var_ready, 1)
                    dve.wait_ge(std_ready, h + 1)
                    for t in range(NT):
                        bk.wait_read(dve, f"g{t}", h)
                    nc.vector.reciprocal(rstd[:, :, 0], rstd[:, :, 0]).then_inc(rstd_ready, 1)
                    dve.wait_ge(rstd_ready, h + 1)
                    for i in range(NT):
                        bk.reads(f"o{i}", nc.vector.tensor_scalar(
                            y[:, i, :], out(f"o{i}")[:, :], mv[:, i, 0:1], rstd[:, i, :],
                            ALU.subtract, ALU.mult))
                        bk.wait_read(dve, f"o{i}", h)
                        nc.vector.tensor_tensor(y[:, i, :], y[:, i, :], gate[:, i, :], ALU.mult)\
                            .then_inc(y_ready, 1)
                    for i in range(NT):
                        dve.wait_ge(y_hi, NT * h + (i + 1))
                        part = (slice(None), bass.ds(4 * h, 4), slice(i * P, (i + 1) * P))
                        bk.reads(f"y{i}", nc.vector.tensor_tensor(
                            yT[1][part], out(f"y{i}")[:, :].rearrange("p (c n) -> p c n", c=4), yT[0][part],
                            ALU.subtract))
                    link.ends_turn()



def branch_out(core, weights, phase, hT, yT, chunks, started, merged, adds, extra=0):
    nc = core.nc
    with ExitStack() as ctx:
        gate = sbuf(nc, ctx, phase + "_gate", [P, NT, 512])
        gated = core.sem(f"{phase}_gated")
        halves = D // 512
        bk = Banks(core, [(f"g{t}", t) for t in range(NT)] + [(f"p{t}", NT + t) for t in range(NT)], halves)
        per_half = 1 + chunks // KC
        total = halves * per_half + extra

        def out(name):
            return core.banks[bk.bank(name)]

        def slot(b):
            return b % weights.blocks

        with nc.Block() as block:
            @block.sync
            def _(sp):
                for g in range(4 * started, 4 * total):
                    weights.load(sp, g, g, weights.first + g >= weights.RING)

            @block.gpsimd
            def _(pool):
                for g in range(4 * started, 4 * total):
                    weights.lo(pool, g, g, slot(g // 4))

            @block.tensor
            def _(pe):
                for n in range(halves):
                    for kind, left, b0, depth in (("g", hT, 0, KC), ("p", yT, 1, chunks)):
                        for t in range(NT):
                            name = f"{kind}{t}"
                            cols = tok_cols(t) if kind == "g" else slice(t * P, (t + 1) * P)
                            bk.wait_free(pe, name, n)
                            for c in range(depth):
                                b = per_half * n + b0 + c // KC
                                if t == 0 and c % KC == 0:
                                    weights.wait(pe, 4 * b + 3)
                                last = pair_matmul(nc, out(name)[:, :], view(left, slice(None), c, cols),
                                                   weights.block(slot(b), c % KC), c == 0, c == depth - 1)
                            bk.fills(name, last)

            @block.scalar
            def _(act):
                def split(blocks):
                    for b in blocks:
                        if b >= weights.blocks:
                            n, place = divmod(b - weights.blocks, per_half)
                            bk.wait_full(act, f"g{NT - 1}" if place == 0 else f"p{NT - 1}", n)
                        for c in range(4):
                            weights.hi(act, 4 * b + c, 4 * b + c, slot(b))

                def sigmoids(n):
                    for t in range(NT):
                        bk.wait_full(act, f"g{t}", n)
                        act.wait_ge(gated, NT * n + 1)
                        bk.reads(f"g{t}", nc.scalar.activation(gate[:, t, :], out(f"g{t}")[:, :], ACT.Sigmoid))

                split(range(started, per_half))
                sigmoids(0)
                split(range(max(started, per_half), halves * per_half))
                sigmoids(1)
                split(range(halves * per_half, total))

            @block.vector
            def _(dve):
                nc.vector.memset(gate[0:1, 0, 0:1], 0.0).then_inc(gated, 1)
                with dve.Fori(0, halves) as n:
                    for t in range(NT):
                        bk.wait_full(dve, f"p{t}", n)
                        bk.wait_read(dve, f"g{t}", n)
                        dst = merged[:, t, bass.ds(512 * n, 512)]
                        if adds:
                            bk.reads(f"p{t}", nc.vector.tensor_tensor(gate[:, t, :], out(f"p{t}")[:, :],
                                                                      gate[:, t, :], ALU.mult))
                            bk.wait_read(dve, f"p{t}", n)
                            nc.vector.tensor_tensor(dst, dst, gate[:, t, :], ALU.add).then_inc(gated, 1)
                        else:
                            bk.reads(f"p{t}", nc.vector.tensor_tensor(dst, out(f"p{t}")[:, :],
                                                                      gate[:, t, :], ALU.mult))
                            bk.wait_read(dve, f"p{t}", n)
                            nc.vector.tensor_copy(gate[0:1, t, 0:1], gate[0:1, t, 1:2]).then_inc(gated, 1)



DIRS = ("f", "b")
BANK_OF = {"f": 1, "b": 4, "m": 7}
FOLLOWING_DONE = {"GATES": 0, "CONV_0": 1, "CONV_1": 1 + (CW - 1), "CONV_2": 1 + 2 * (CW - 1),
                  "SCALES": 1 + 3 * (CW - 1), "MATRICES": 2 + 3 * (CW - 1)}
FOLLOWING_STEPS = 1 + 3 * (CW - 1) + 2


def delta_net(core, weights, a, hT, yT, ident):
    nc = core.nc
    NC5 = NT + 1
    with ExitStack() as ctx:
        w_ab = sbuf(nc, ctx, "dn_w_ab", [P, KC, 32])
        w_ab_pair = sbuf_pair(nc, ctx, "dn_w_ab", [P, KC, 32])
        upper = sbuf(nc, ctx, "dn_upper", [P, P])
        lower = sbuf(nc, ctx, "dn_lower", [P, P])
        ones = sbuf(nc, ctx, "dn_ones", [P, P])
        masks = sbuf(nc, ctx, "dn_masks", [P, 2, LEVELS, P])
        conv_w = sbuf(nc, ctx, "dn_conv_w", [P, DH, 3 * CW])
        cw = sbuf(nc, ctx, "dn_conv_head", [P, 3 * CW])
        norm_g = sbuf(nc, ctx, "dn_norm_g", [P, 1])
        dtb = sbuf(nc, ctx, "dn_dt_bias", [P, 16])
        alog = sbuf(nc, ctx, "dn_a_log", [P, 16])
        raw = sbuf(nc, ctx, "dn_raw", [P, NC5, 32])
        g = sbuf(nc, ctx, "dn_g", [P, NC5, 16])
        g2 = sbuf(nc, ctx, "dn_g_work", [P, NC5, 16])
        NEGB, BETA, NEGEXP, BETAEND, END, G = range(6)
        scal = sbuf(nc, ctx, "dn_scal", [P, 6, NC5, 16])
        hs = sbuf(nc, ctx, "dn_scal_head", [P, 6 * NC5, 2])
        hs_next = sbuf(nc, ctx, "dn_scal_next_head", [P, 6 * NC5, 2])
        eps = sbuf(nc, ctx, "dn_eps", [P, 2])
        pre = sbuf(nc, ctx, "dn_conv_in", [P, 3, TOK + CW - 1])
        cv = sbuf(nc, ctx, "dn_conv_out", [P, 3, TOK])
        qk = sbuf(nc, ctx, "dn_q_k", [P, 2, TOK])
        expb = sbuf(nc, ctx, "dn_exp_b", [P, 2, SEQ])
        sq_meta = sbuf(nc, ctx, "dn_squares_meta", [P, META])
        v_tok = sbuf(nc, ctx, "dn_v_tok", [P, NC5, DK])
        k_tok = sbuf(nc, ctx, "dn_k_tok", [P, NC5, DK])
        inv_len = sbuf(nc, ctx, "dn_inverse_lengths", [P, 2 * NC5])
        gz = sbuf(nc, ctx, "dn_gate_z", [P, SEQ])
        gt = sbuf(nc, ctx, "dn_g_tri", [P, 2, NT, P])
        gtm = sbuf(nc, ctx, "dn_g_tri_meta", [P, META])
        dec = sbuf(nc, ctx, "dn_decay", [P, 2, NT, P])
        decm = sbuf(nc, ctx, "dn_decay_meta", [META, META])
        qd = sbuf(nc, ctx, "dn_q_decayed", [P, 2, SEQ])
        attn = sbuf(nc, ctx, "dn_attn", [P, 2, NT, P])
        lt = sbuf(nc, ctx, "dn_l", [P, 2, NT, P])
        sq = lt[:, :, :, :]
        ltm = sbuf(nc, ctx, "dn_l_meta", [META, META])
        lm = sbuf(nc, ctx, "dn_l_levels", [P, 2, LEVELS, NT, P])
        lmm = sbuf(nc, ctx, "dn_l_levels_meta", [P, 4, P])
        x = sbuf(nc, ctx, "dn_x", [P, 2, NT, P])
        xt = sbuf(nc, ctx, "dn_xt", [P, 2, NT, P])
        yy = sbuf(nc, ctx, "dn_lx", [P, 2, NT, P])
        xm = sbuf(nc, ctx, "dn_x_meta", [P, 3, P])
        state = sbuf(nc, ctx, "dn_state", [P, 2, DK])
        rhs = sbuf(nc, ctx, "dn_rhs", [P, 2, DK])
        vn = sbuf(nc, ctx, "dn_v_new", [P, 2, DK])
        v2 = sbuf(nc, ctx, "dn_v_end", [P, 2, DK])
        ysq, y = gt[:, 0, :, :], gt[:, 1, :, :]
        rstd = sbuf(nc, ctx, "dn_rstd", [P, NT])
        names = ("ab_in ab_hi ab_lo y_hi y_lo tables_in act_steps dve_steps sp_arg sp_log g_ready exp_ready conv_ready "
                 "silu_ready sq_ready diag_ready gtri_ready expb_ready dec_ready qd_ready "
                 "attn_ready masked_ready x_start next_steps ysq_ready ms_ready std_ready").split()
        s = {n: core.sem("dn_" + n) for n in names}
        setup_bank = Banks(core, [("ab", 0), ("sums", 1)])
        early = Banks(core, [("q", 2), ("pm0", 3), ("k", 3), ("pm1", 5), ("v", 5), ("pm2", 2), ("bf", 2),
                             ("bb", 3), ("bm", 5), ("ss", 2), ("nq", 2), ("nk", 3), ("nm", 5), ("z", 6)], DH)
        order = [("tv", 1), ("tk", 4), ("tm", 7), ("kk", 1), ("qk", 4), ("kkm", 7)]
        for level in range(LEVELS):
            parts = "fbm" if level < 4 else "fb"
            if level:
                order += [(f"y{d}{level}", BANK_OF[d]) for d in parts]
                order += [(f"z{d}{level}", BANK_OF[d]) for d in parts]
            if level < LEVELS - 1:
                order += [(f"x{d}{level}", BANK_OF[d]) for d in ("fbm" if level < 3 else "fb")]
        scan = [(("f", NT), ("b", NT - 1))] + [(("f", r), ("b", NT - 2 - r)) for r in range(NT - 1)] \
            + [(("f", NT - 1),)]
        first, final = {"f": NT, "b": NT - 1}, {"f": NT - 1, "b": 0}
        for steps in scan:
            order += [(f"r{d}{c}", BANK_OF[d]) for d, c in steps if c != first[d]]
            order += [(f"w{d}{c}", BANK_OF[d]) for d, c in steps]
            order += [(f"s{d}{c}", BANK_OF[d]) for d, c in steps if c != final[d]]
        order += [("o", 0), ("ty", 0)]
        bk = Banks(core, order, DH)
        turn_order = ("PROJ_Q PROJ_K grow0 turn0 GATES CONV_0 SPLIT_Q SPLIT_K SILU_0 PROJ_V CONV_1 SILU_1 grow1 "
                      "CONV_2 DECAYS turn1 SPLIT_V grow2 SILU_2 turn2 EXP_B DECAY_ARG grow3 SUMS turn3 "
                      "EXP_DECAY grow4 LENGTHS turn4 SCALES grow5 turn5 grow6 scan0 scan1 PROJ_Z0 scan2 scan3 "
                      "scan4 PROJ_Z1 UNIT tail0 PROJ_Z2 tail1 UNIT_COPY PROJ_Z3 MATRICES tail2 GATE_Z SPLIT_Z").split()

        ahead = ("PROJ_Q", "PROJ_K", "PROJ_V")

        def run(eng, this, following, done=()):
            for part in turn_order:
                if part.isupper() and part not in done:
                    following(part, 0, True)
            with eng.Fori(0, DH - 1) as h:
                for part in turn_order:
                    if part.isupper():
                        following(part, h + 1, False)
                    else:
                        this(part, h)
            for part in turn_order:
                if not part.isupper():
                    this(part, DH - 1)

        def out(name):
            return core.banks[(early if name in early.place else bk).bank(name)]

        def head_of(pair, h):
            return [half[:, h, :] if isinstance(h, int) else
                    half[:, bass.ds(h, 1), :].rearrange("p o n -> p (o n)") for half in pair]

        def by_chunk(ap):
            return ap.rearrange("p (c n) -> p c n", c=NT)

        def over_chunks(ap):
            return ap.unsqueeze(1).broadcast_to([ap.shape[0], NT, ap.shape[-1]])

        def masked(level):
            return 3 * level + 3 if level < 4 else 12 + 2 * (level - 3)

        def wait_xt(eng, d, level, h):
            if level == 0:
                eng.wait_ge(s["x_start"], 3 * h + 3)
            else:
                bk.wait_read(eng, f"z{d}{level}", h)

        def sc(kind, c, d):
            n = rows(c)
            return hs[0:n, kind * NC5 + c, DIRS.index(d):DIRS.index(d) + 1]

        def sc_next(kind, c, d):
            return hs_next[0:rows(c), kind * NC5 + c, DIRS.index(d):DIRS.index(d) + 1]

        with nc.Block() as block:
            @block.sync
            def _(sp):
                sp.dma_start(w_ab[:, :, :], a["w_dn_ab"]).then_inc(s["ab_in"], 16)
                loads = ((upper[:, :], a["upper"]), (lower[:, :], a["lower"]),
                         (masks[:, :, :, :], a["masks"]), (conv_w[:, :, :], a["dn_conv"]),
                         (norm_g[:, :], a["dn_norm_g"]),
                         (dtb[:, :], a["dn_dt_bias"].partition_broadcast(P)),
                         (alog[:, :], a["dn_a_log"].partition_broadcast(P)))
                for dst, src in loads:
                    sp.dma_start(dst, src).then_inc(s["tables_in"], 16)
                for g in range(4):
                    weights.load(sp, g, g, True)
                with sp.Fori(0, DH) as h:
                    for g in range(4):
                        weights.load(sp, h * 4 + (4 + g), g, True)

            @block.tensor
            def _(pe):
                pe.wait_ge(s["ab_in"], 16)
                pe.wait_ge(s["ab_lo"], 1)
                for t in range(NC5):
                    for kc in range(KC):
                        last = pair_matmul(nc, core.banks[0][0:rows(t), 32 * t:32 * t + 32],
                                           view(hT, slice(None), kc, tok_cols(t)),
                                           view(w_ab_pair, slice(None), kc), kc == 0, kc == KC - 1)
                setup_bank.fills("ab", last)
                def sum_decays():
                    pe.wait_ge(s["tables_in"], 16 * 7)
                    pe.wait_ge(s["g_ready"], 1)
                    sums = core.banks[1]
                    nc.tensor.matmul(sums[:, 0:32], upper[:, :], g[:, 0:NT, 0:8], start=True, stop=True)
                    nc.tensor.matmul(sums[:, 32:64], lower[:, :], g[:, 0:NT, 8:16], start=True, stop=True)
                    nc.tensor.matmul(sums[0:META, 64:72], upper[0:META, 0:META], g[0:META, NT, 0:8],
                                     start=True, stop=True)
                    nc.tensor.matmul(sums[:, 128:192], ones[:, :], g[:, 0:NT, :], start=True, stop=True)
                    setup_bank.fills("sums", nc.tensor.matmul(
                        sums[0:META, 200:208], ones[0:META, 0:META], g[0:META, NT, 0:8], start=True, stop=True))

                def project(name, i, hn):
                    weights.wait(pe, 4 * hn + i)
                    early.wait_free(pe, f"pm{i}", hn)
                    early.wait_free(pe, name, hn)
                    for kc in range(KC):
                        left, ends = weights.columns(0, i, kc), dict(start=kc == 0, stop=kc == KC - 1)
                        last = pair_matmul(nc, out(name)[:, :], left,
                                           view(hT, slice(None), kc, slice(META, TOK)), **ends)
                        if kc == KC - 1:
                            early.fills(name, last)
                        last = pair_matmul(nc, out(f"pm{i}")[:, i * META:(i + 1) * META], left,
                                           view(hT, slice(None), kc, slice(0, META)), **ends)
                    early.fills(f"pm{i}", last)

                def unit(h):
                    pe.wait_ge(s["silu_ready"], 3 * h + 3)
                    early.wait_read(pe, "nm", h)
                    early.wait_read(pe, "nk", h)
                    for name, src in (("tv", cv[:, 2, :]), ("tk", qk[:, 1, :])):
                        bk.wait_free(pe, name, h)
                        for t in range(NT):
                            last = nc.tensor.transpose(out(name)[:, t * P:(t + 1) * P], src[:, tok_cols(t)],
                                                       ident[:, :])
                        bk.fills(name, last)
                    bk.wait_free(pe, "tm", h)
                    nc.tensor.transpose(out("tm")[0:META, 0:P], cv[:, 2, 0:META], ident[:, :])
                    bk.fills("tm", nc.tensor.transpose(out("tm")[0:META, P:2 * P], qk[:, 1, 0:META],
                                                       ident[:, :]))
                    early.wait_read(pe, "nq", h)
                    for name, i in (("kk", 1), ("qk", 0)):
                        bk.wait_free(pe, name, h)
                        for t in range(NT):
                            last = nc.tensor.matmul(out(name)[:, t * P:(t + 1) * P], qk[:, 1, tok_cols(t)],
                                                    qk[:, i, tok_cols(t)], start=True, stop=True)
                        bk.fills(name, last)
                    bk.wait_free(pe, "kkm", h)
                    bk.fills("kkm", nc.tensor.matmul(out("kkm")[0:META, 0:META], qk[:, 1, 0:META],
                                                     qk[:, 1, 0:META], start=True, stop=True))

                def following(part, hn, at_start):
                    if part == "PROJ_Q":
                        project("q", 0, hn)
                    elif part == "UNIT":
                        unit(hn)
                    elif part == "PROJ_K":
                        project("k", 1, hn)
                    elif part == "PROJ_V":
                        project("v", 2, hn)
                    elif part.startswith("PROJ_Z"):
                        quarter = int(part[-1])
                        if quarter == 0:
                            weights.wait(pe, 4 * hn + 3)
                            early.wait_free(pe, "z", hn)
                        for kc in range(KC // 4 * quarter, KC // 4 * (quarter + 1)):
                            last = pair_matmul(nc, out("z")[:, :], weights.columns(0, 3, kc),
                                               view(hT, slice(None), kc, slice(META, TOK)), kc == 0, kc == KC - 1)
                        if quarter == 3:
                            early.fills("z", last)
                    elif part == "DECAYS":
                        pe.wait_ge(s["gtri_ready"], 3 * hn + 3)
                        for i, d in enumerate(DIRS):
                            early.wait_free(pe, "b" + d, hn)
                            early.fills("b" + d, nc.tensor.matmul(out("b" + d)[:, :], ones[:, :],
                                                                  gt[:, i, :, :], start=True, stop=True))
                        early.wait_free(pe, "bm", hn)
                        early.fills("bm", nc.tensor.matmul(out("bm")[:, 0:META], ones[:, :], gtm[:, :],
                                                           start=True, stop=True))
                    elif part == "SUMS":
                        pe.wait_ge(s["sq_ready"], 2 * hn + 2)
                        early.wait_free(pe, "ss", hn)
                        for i in range(2):
                            for t in range(NT + i):
                                last = nc.tensor.matmul(out("ss")[0:rows(t), NC5 * i + t:NC5 * i + t + 1],
                                                        sq_meta[:, :] if t == NT else sq[:, i, t, :],
                                                        ones[:, 0:1], start=True, stop=True)
                        early.fills("ss", last)
                    elif part == "SCALES":
                        pe.wait_ge(s["diag_ready"], hn + 1)
                        for name, right, n in (("nq", gt[:, 0, :, :], SEQ), ("nk", gt[:, 1, :, :], SEQ),
                                               ("nm", gtm[:, :], META)):
                            early.wait_free(pe, name, hn)
                            early.fills(name, nc.tensor.matmul(out(name)[:, 0:n], ones[:, :], right,
                                                               start=True, stop=True))

                def grow(level, h):
                    parts = [("f", 0), ("b", 1)] + ([("m", 2)] if level < 4 else [])
                    if level:
                        pe.wait_ge(s["masked_ready"], 18 * h + masked(level))
                        for d, i in parts:
                            bk.wait_read(pe, f"x{d}{level - 1}", h)
                            bk.wait_free(pe, f"y{d}{level}", h)
                            if d == "m":
                                last = nc.tensor.matmul(out("ym1")[:, 0:META], lmm[:, level, :],
                                                        xm[:, 0, 0:META], start=True, stop=True)
                            else:
                                for t in range(NT):
                                    last = nc.tensor.matmul(out(f"y{d}{level}")[:, t * P:(t + 1) * P],
                                                            lm[:, i, level, t, :], x[:, i, t, :],
                                                            start=True, stop=True)
                            bk.fills(f"y{d}{level}", last)
                        for d, i in parts:
                            bk.wait_read(pe, f"y{d}{level}", h)
                            bk.wait_free(pe, f"z{d}{level}", h)
                            if d == "m":
                                last = nc.tensor.matmul(out("ym1")[:, 0:META], xm[:, 2, :],
                                                        xm[:, 1, 0:META], start=True, stop=True)
                            else:
                                for t in range(NT):
                                    last = nc.tensor.matmul(out(f"z{d}{level}")[:, t * P:(t + 1) * P],
                                                            yy[:, i, t, :], xt[:, i, t, :],
                                                            start=True, stop=True)
                            bk.fills(f"z{d}{level}", last)

                def turned(level, h):
                    parts = [("f", 0), ("b", 1)] + ([("m", 2)] if level < 4 else [])
                    if level < LEVELS - 1:
                        for d, i in parts:
                            if d == "m" and level == 3:
                                continue
                            wait_xt(pe, d, level, h)
                            bk.wait_free(pe, f"x{d}{level}", h)
                            if d == "m":
                                last = nc.tensor.transpose(out("ym1")[:, 0:P], xm[:, 1, :], ident[:, :])
                            else:
                                for t in range(NT):
                                    last = nc.tensor.transpose(out(f"x{d}{level}")[:, t * P:(t + 1) * P],
                                                               xt[:, i, t, :], ident[:, :])
                            bk.fills(f"x{d}{level}", last)

                def scan_round(number, h):
                    steps, opened = scan[number], number > 0
                    if number == 0:
                        pe.wait_ge(s["qd_ready"], 2 * h + 2)
                        pe.wait_ge(s["attn_ready"], 2 * h + 2)
                        for name in ("tv", "tk", "tm"):
                            bk.wait_read(pe, name, h)
                        for d, level in (("f", LEVELS - 1), ("b", LEVELS - 1), ("m", 3)):
                            wait_xt(pe, d, level, h)
                        bk.wait_free(pe, "o", h)
                    for d, c in steps:
                        i, n = DIRS.index(d), rows(c)
                        if c != first[d]:
                            previous = {"f": NT if c == 0 else c - 1, "b": c + 1}[d]
                            bk.wait_read(pe, f"s{d}{previous}", h)
                            bk.wait_free(pe, f"r{d}{c}", h)
                            bk.fills(f"r{d}{c}", nc.tensor.matmul(out(f"r{d}{c}")[0:n, 0:DK],
                                                                  qk[:, 1, tok_cols(c)], state[:, i, :],
                                                                  start=True, stop=True))
                            nc.tensor.matmul(out("o")[:, c * P:(c + 1) * P], qd[:, i, c * P:(c + 1) * P],
                                             state[:, i, :], start=not opened, stop=False,
                                             skip_group_check=True)
                            opened = True
                    for d, c in steps:
                        i, n = DIRS.index(d), rows(c)
                        left = xm[:, 1, :] if c == NT else xt[:, i, c, :]
                        right = v_tok[:, c, :]
                        if c != first[d]:
                            bk.wait_read(pe, f"r{d}{c}", h)
                            right = rhs[:, i, :]
                        bk.wait_free(pe, f"w{d}{c}", h)
                        bk.fills(f"w{d}{c}", nc.tensor.matmul(out(f"w{d}{c}")[:, 0:DK], left, right,
                                                              start=True, stop=True))
                    for d, c in steps:
                        i, n = DIRS.index(d), rows(c)
                        bk.wait_read(pe, f"w{d}{c}", h)
                        if c != final[d]:
                            bk.wait_free(pe, f"s{d}{c}", h)
                            bk.fills(f"s{d}{c}", nc.tensor.matmul(out(f"s{d}{c}")[:, 0:DK],
                                                                  k_tok[0:n, c, :], v2[0:n, i, :],
                                                                  start=True, stop=True))
                        if c != NT:
                            last = nc.tensor.matmul(out("o")[:, c * P:(c + 1) * P], attn[:, i, c, :],
                                                    vn[:, i, :], start=not opened, stop=steps is scan[-1],
                                                    skip_group_check=True)
                            opened = True
                    if steps is scan[-1]:
                        bk.fills("o", last)

                def this(part, h):
                    if part.startswith("grow"):
                        grow(int(part[-1]), h)
                    elif part.startswith("turn"):
                        turned(int(part[-1]), h)
                    elif part.startswith("scan"):
                        scan_round(int(part[-1]), h)
                    elif part == "tail1":
                        bk.wait_read(pe, "o", h)
                        bk.wait_free(pe, "ty", h)
                        for t in range(NT):
                            last = nc.tensor.transpose(out("ty")[:, t * P:(t + 1) * P], y[:, t, :], ident[:, :])
                        bk.fills("ty", last)

                for part in ahead:
                    following(part, 0, True)
                sum_decays()
                setup_bank.wait_read(pe, "sums")
                run(pe, this, following, done=ahead)

            @block.scalar
            def _(act):
                link = Chain(act, s["act_steps"])
                act.wait_ge(s["ab_in"], 16)
                nc.scalar.activation(w_ab_pair[0][:, :, :], w_ab[:, :, :], ACT.Copy).then_inc(s["ab_hi"], 1)
                for g in range(4):
                    weights.hi(act, g, g, 0)
                act.wait_ge(s["sp_arg"], 1)
                link(nc.scalar.activation(g2[:, :, :], g2[:, :, :], ACT.Exp))
                link(nc.scalar.activation(g2[:, :, :], g2[:, :, :], ACT.Ln, bias=1.0))
                link(nc.scalar.activation(alog[:, :], alog[:, :], ACT.Exp))
                nc.scalar.activation(scal[:, BETA, :, :], raw[:, :, 16:32], ACT.Sigmoid)\
                    .then_inc(s["sp_log"], 1)
                def following(part, hn, at_start):
                    if part in ("PROJ_Q", "PROJ_K", "PROJ_V"):
                        name = part[-1].lower()
                        i = "qkv".index(name)
                        early.wait_full(act, name, hn)
                        early.reads(name, nc.scalar.activation(pre[:, i, 2 + META:2 + TOK], out(name)[:, :],
                                                               ACT.Copy))
                        early.wait_full(act, f"pm{i}", hn)
                        early.reads(f"pm{i}", nc.scalar.activation(
                            pre[:, i, 2:2 + META], out(f"pm{i}")[:, i * META:(i + 1) * META], ACT.Copy))
                    elif part.startswith("SPLIT"):
                        i = "QKVZ".index(part[-1])
                        early.wait_full(act, ("pm0", "pm1", "pm2", "z")[i], hn)
                        weights.hi(act, 4 * hn + (4 + i), i, 0)
                    elif part.startswith("SILU"):
                        i = int(part[-1])
                        act.wait_ge(s["conv_ready"], 3 * hn + (i + 1))
                        nc.scalar.activation(cv[:, i, :], cv[:, i, :], ACT.Silu).then_inc(s["silu_ready"], 1)
                    elif part == "EXP_B":
                        if not at_start:
                            act.wait_ge(s["qd_ready"], 2 * hn)
                        for i, d in enumerate(DIRS):
                            early.wait_full(act, "b" + d, hn)
                            nc.scalar.activation(expb[:, i, :], out("b" + d)[:, :], ACT.Exp)\
                                .then_inc(s["expb_ready"], 1)
                    elif part == "EXP_DECAY":
                        for name in ("bf", "bb", "bm"):
                            early.wait_read(act, name, hn)
                        nc.scalar.activation(dec[:, :, :, :], dec[:, :, :, :], ACT.Exp)\
                            .then_inc(s["dec_ready"], 1)
                        nc.scalar.activation(decm[:, :], decm[:, :], ACT.Exp).then_inc(s["dec_ready"], 1)
                    elif part == "UNIT_COPY":
                        for name, dst in (("tv", v_tok), ("tk", k_tok)):
                            bk.wait_full(act, name, hn)
                            bk.reads(name, nc.scalar.activation(dst[:, 0:NT, :], by_chunk(out(name)[:, :]),
                                                                ACT.Copy))
                        bk.wait_full(act, "tm", hn)
                        nc.scalar.activation(v_tok[0:META, NT, :], out("tm")[0:META, 0:P], ACT.Copy)
                        bk.reads("tm", nc.scalar.activation(k_tok[0:META, NT, :], out("tm")[0:META, P:2 * P],
                                                            ACT.Copy))
                    elif part == "GATE_Z":
                        early.wait_full(act, "z", hn)
                        early.reads("z", nc.scalar.activation(gz[:, :], out("z")[:, :], ACT.Silu))
                    elif part == "LENGTHS":
                        early.wait_full(act, "ss", hn)
                        nc.scalar.activation(inv_len[:, 0:NT], out("ss")[:, 0:NT], ACT.Sqrt, bias=eps[:, 0:1],
                                             scale=float(DK))
                        nc.scalar.activation(inv_len[0:META, 2 * NC5 - 1:2 * NC5],
                                             out("ss")[0:META, 2 * NC5 - 1:2 * NC5], ACT.Sqrt,
                                             bias=eps[0:META, 1:2])
                        early.reads("ss", nc.scalar.activation(
                            inv_len[:, NC5:NC5 + NT], out("ss")[:, NC5:NC5 + NT], ACT.Sqrt, bias=eps[:, 1:2]))

                def grow(level, h):
                    parts = [("f", 0), ("b", 1)] + ([("m", 2)] if level < 4 else [])
                    if level:
                        for d, i in parts:
                            bk.wait_full(act, f"y{d}{level}", h)
                            if d == "m":
                                ins = nc.scalar.activation(xm[0:META, 2, 0:META], out("ym1")[0:META, 0:META],
                                                           ACT.Copy)
                            else:
                                ins = nc.scalar.activation(yy[:, i, :, :], by_chunk(out(f"y{d}{level}")[:, :]),
                                                           ACT.Copy)
                            bk.reads(f"y{d}{level}", ins)

                def turned(level, h):
                    parts = [("f", 0), ("b", 1)] + ([("m", 2)] if level < 4 else [])
                    if level < LEVELS - 1:
                        for d, i in parts:
                            if d == "m" and level == 3:
                                continue
                            bk.wait_full(act, f"x{d}{level}", h)
                            if d == "m":
                                ins = nc.scalar.activation(xm[0:META, 0, 0:META], out("ym1")[0:META, 0:META],
                                                           ACT.Copy)
                            else:
                                ins = nc.scalar.activation(x[:, i, :, :], by_chunk(out(f"x{d}{level}")[:, :]),
                                                           ACT.Copy)
                            bk.reads(f"x{d}{level}", ins)

                def this(part, h):
                    if part.startswith("grow"):
                        grow(int(part[-1]), h)
                    elif part.startswith("turn"):
                        turned(int(part[-1]), h)
                    elif part.startswith("scan"):
                        for d, c in scan[int(part[-1])]:
                            if d == "b":
                                bk.wait_full(act, f"w{d}{c}", h)
                                nc.scalar.activation(vn[:, 1, :], out(f"w{d}{c}")[:, 0:DK], ACT.Copy,
                                                     scale=sc(BETA, c, d))
                                bk.reads(f"w{d}{c}", nc.scalar.activation(v2[:, 1, :], out(f"w{d}{c}")[:, 0:DK],
                                                                          ACT.Copy, scale=sc(BETAEND, c, d)))
                    elif part == "tail0":
                        bk.wait_full(act, "o", h)
                        nc.scalar.activation(ysq[:, :, :], by_chunk(out("o")[:, :]), ACT.Square)\
                            .then_inc(s["ysq_ready"], 1)
                    elif part == "tail1":
                        act.wait_ge(s["ms_ready"], h + 1)
                        nc.scalar.activation(rstd[:, :], rstd[:, :], ACT.Sqrt).then_inc(s["std_ready"], 1)
                    elif part == "tail2":
                        bk.wait_read(act, "ty", h)
                        nc.scalar.activation(head_of(yT, h)[0], gz[:, :], ACT.Copy).then_inc(s["y_hi"], 1)
                        act.wait_ge(s["y_lo"], h + 1)

                for part in ahead:
                    following(part, 0, True)
                setup_bank.wait_read(act, "sums")
                nc.scalar.activation(scal[:, NEGEXP, :, :], scal[:, NEGB, :, :], ACT.Exp, scale=-1.0)
                nc.scalar.activation(scal[:, BETAEND, :, :], scal[:, BETAEND, :, :], ACT.Exp)
                nc.scalar.activation(scal[:, END, :, :], scal[:, END, :, :], ACT.Exp)\
                    .then_inc(s["exp_ready"], 1)
                run(act, this, following, done=ahead)

            @block.gpsimd
            def _(pool):
                for g in range(4):
                    weights.lo(pool, g, g, 0)
                for g in range(3):
                    weights.lo(pool, 4 + g, g, 0)

                def squares(hn):
                    if not isinstance(hn, int) or hn:
                        pool.wait_ge(s["masked_ready"], 18 * hn)
                    pool.wait_ge(s["silu_ready"], 3 * hn + 1)
                    nc.gpsimd.tensor_tensor(sq[:, 0, :, :], by_chunk(cv[:, 0, META:TOK]),
                                            by_chunk(cv[:, 0, META:TOK]), ALU.mult).then_inc(s["sq_ready"], 1)
                    pool.wait_ge(s["silu_ready"], 3 * hn + 2)
                    nc.gpsimd.tensor_tensor(sq_meta[:, :], cv[:, 1, 0:META], cv[:, 1, 0:META], ALU.mult)
                    nc.gpsimd.tensor_tensor(sq[:, 1, :, :], by_chunk(cv[:, 1, META:TOK]),
                                            by_chunk(cv[:, 1, META:TOK]), ALU.mult).then_inc(s["sq_ready"], 1)

                squares(0)

                def turn(h, more):
                    pool.wait_ge(s["expb_ready"], 2 * h + 2)
                    early.wait_read(pool, "nq", h)
                    for i in range(2):
                        nc.gpsimd.tensor_tensor(qd[:, i, :], expb[:, i, :], qk[:, 0, META:TOK], ALU.mult)\
                            .then_inc(s["qd_ready"], 1)
                    bk.wait_read(pool, "kk", h)
                    bk.wait_read(pool, "kkm", h)
                    for level in range(LEVELS):
                        for i in range(2):
                            nc.gpsimd.tensor_tensor(lm[:, i, level, :, :], lt[:, i, :, :],
                                                    over_chunks(masks[:, i, level, :]), ALU.mult)\
                                .then_inc(s["masked_ready"], 1)
                        if level < 4:
                            nc.gpsimd.tensor_tensor(lmm[0:META, level, 0:META], ltm[:, :], masks[0:META, 0, level, 0:META],
                                                    ALU.mult).then_inc(s["masked_ready"], 1)
                    bk.wait_read(pool, "qk", h)
                    for i, keep in enumerate((upper, lower)):
                        nc.gpsimd.tensor_tensor(attn[:, i, :, :], attn[:, i, :, :],
                                                over_chunks(keep[:, :]), ALU.mult).then_inc(s["attn_ready"], 1)
                    weights.lo(pool, h * 4 + 7, 3, 0)
                    if more:
                        squares(h + 1)
                        for g in range(3):
                            weights.lo(pool, h * 4 + (8 + g), g, 0)

                with pool.Fori(0, DH - 1) as h:
                    turn(h, True)
                turn(DH - 1, False)

            @block.vector
            def _(dve):
                link = Chain(dve, s["dve_steps"])
                nc.vector.memset(pre[:, :, :], 0.0)
                nc.vector.memset(raw[:, :, :], 0.0)
                nc.vector.memset(scal[:, :, :, :], 0.0)
                for zeroed in (gtm[:, :], lmm[:, :, :], xm[:, :, :], v_tok[:, NT, :]):
                    nc.vector.memset(zeroed, 0.0)
                nc.vector.memset(eps[:, 0:1], DK * RMS_EPS)
                nc.vector.memset(eps[:, 1:2], RMS_EPS)
                nc.vector.memset(inv_len[:, :], 1.0)
                link(nc.vector.memset(ones[:, :], 1.0))
                dve.wait_ge(s["ab_hi"], 1)
                nc.vector.tensor_tensor(w_ab_pair[1][:, :, :], w_ab[:, :, :], w_ab_pair[0][:, :, :],
                                        ALU.subtract).then_inc(s["ab_lo"], 1)
                setup_bank.wait_full(dve, "ab")
                nc.vector.tensor_copy(raw[:, 0:NT, :],
                                      core.banks[0][:, 0:NT * 32].rearrange("p (t n) -> p t n", t=NT))
                setup_bank.reads("ab", nc.vector.tensor_copy(raw[0:META, NT, :],
                                                             core.banks[0][0:META, NT * 32:NC5 * 32]))
                setup_bank.wait_read(dve, "ab")
                dve.wait_ge(s["tables_in"], 16 * 7)
                z = raw[:, :, 0:16]
                link(nc.vector.tensor_tensor(z, z, dtb[:, :].unsqueeze(1).broadcast_to([P, NC5, 16]), ALU.add))
                link(nc.vector.tensor_scalar(g2[:, :, :], z, -1.0, None, ALU.mult))
                nc.vector.tensor_tensor(g2[:, :, :], g2[:, :, :], z, ALU.min).then_inc(s["sp_arg"], 1)
                dve.wait_ge(s["sp_log"], 1)
                link(nc.vector.tensor_scalar(g[:, :, :], z, 0.0, None, ALU.max))
                link(nc.vector.tensor_tensor(g[:, :, :], g[:, :, :], g2[:, :, :], ALU.add))
                link(nc.vector.tensor_scalar(alog[:, :], alog[:, :], -1.0, None, ALU.mult))
                link(nc.vector.tensor_tensor(g[:, :, :], g[:, :, :],
                                             alog[:, :].unsqueeze(1).broadcast_to([P, NC5, 16]), ALU.mult))
                nc.vector.tensor_copy(scal[:, G, :, :], g[:, :, :]).then_inc(s["g_ready"], 1)
                setup_bank.wait_full(dve, "sums")
                dve.wait_ge(s["g_ready"], 1)
                sums = core.banks[1]
                running = ((scal[:, :, 0:NT, 0:8], sums[:, 0:32].rearrange("p (c n) -> p c n", c=NT),
                            sums[:, 128:192].rearrange("p (c n) -> p c n", c=NT)[:, :, 0:8]),
                           (scal[:, :, 0:NT, 8:16], sums[:, 32:64].rearrange("p (c n) -> p c n", c=NT),
                            sums[:, 128:192].rearrange("p (c n) -> p c n", c=NT)[:, :, 8:16]),
                           (scal[0:META, :, NT:NC5, 0:8], sums[0:META, 64:72].unsqueeze(1),
                            sums[0:META, 200:208].unsqueeze(1)))
                for dst, b, end in running:
                    link(nc.vector.tensor_scalar(dst[:, NEGB], b, -1.0, None, ALU.mult))
                    nc.vector.tensor_copy(dst[:, END], end)
                    ins = nc.vector.tensor_tensor(dst[:, BETAEND], dst[:, NEGB], end, ALU.add)
                setup_bank.reads("sums", ins)
                dve.wait_ge(s["exp_ready"], 1)
                nc.vector.tensor_tensor(scal[:, BETAEND, :, :], scal[:, BETAEND, :, :], scal[:, BETA, :, :],
                                        ALU.mult)
                link(nc.vector.tensor_scalar(scal[:, NEGEXP, :, :], scal[:, NEGEXP, :, :], -1.0, None,
                                             ALU.mult))
                before = link.n

                def unit(h):
                    dve.wait_ge(s["silu_ready"], 3 * h + 2)
                    early.wait_full(dve, "nk", h)
                    early.reads("nk", nc.vector.tensor_tensor(qk[:, 1, META:TOK], cv[:, 1, META:TOK],
                                                              out("nk")[:, :], ALU.mult))
                    early.wait_full(dve, "nm", h)
                    early.reads("nm", nc.vector.tensor_tensor(qk[:, 1, 0:META], cv[:, 1, 0:META],
                                                              out("nm")[:, 0:META], ALU.mult))
                    early.reads("nq", nc.vector.tensor_tensor(qk[:, 0, META:TOK], cv[:, 0, META:TOK],
                                                              out("nq")[:, :], ALU.mult))
                def matrices(h, link):
                    ds = slice(h, h + 1) if isinstance(h, int) else bass.ds(h, 1)
                    link(nc.vector.tensor_copy(hs[:, :, :], scal[:, :, :, :].rearrange(
                        "p k c (d h) -> p (k c) d h", d=2)[:, :, :, ds].rearrange("p k d o -> p k (d o)")))
                    dve.wait_ge(s["dec_ready"], 2 * h + 2)
                    bk.wait_full(dve, "kk", h)
                    for i, d in enumerate(DIRS):
                        for c in range(NT):
                            ins = nc.vector.scalar_tensor_tensor(
                                out=lt[:, i, c, :], in0=out("kk")[:, c * P:(c + 1) * P], scalar=sc(BETA, c, d),
                                in1=dec[:, i, c, :], op0=ALU.mult, op1=ALU.mult)
                    bk.reads("kk", ins)
                    bk.wait_full(dve, "kkm", h)
                    bk.reads("kkm", nc.vector.scalar_tensor_tensor(
                        out=ltm[:, :], in0=out("kkm")[0:META, 0:META], scalar=sc(BETA, NT, "f"),
                        in1=decm[:, :], op0=ALU.mult, op1=ALU.mult))
                    bk.wait_full(dve, "qk", h)
                    for i in range(2):
                        ins = nc.vector.tensor_tensor(attn[:, i, :, :], by_chunk(out("qk")[:, :]),
                                                      dec[:, i, :, :], ALU.mult)
                    bk.reads("qk", ins)
                    bk.wait_read(dve, "qk", h)
                    bk.wait_read(dve, "kkm", h)

                def following(part, hn, at_start):
                    link = Chain(dve, s["next_steps"], FOLLOWING_DONE[part], hn, FOLLOWING_STEPS) \
                        if part in FOLLOWING_DONE else None
                    if part == "GATES":
                        ds = slice(hn, hn + 1) if isinstance(hn, int) else bass.ds(hn, 1)
                        nc.vector.tensor_copy(hs_next[:, :, :], scal[:, :, :, :].rearrange(
                            "p k c (d h) -> p (k c) d h", d=2)[:, :, :, ds].rearrange("p k d o -> p k (d o)"))
                        link(nc.vector.tensor_copy(cw[:, :], conv_w[:, ds, :].rearrange("p o n -> p (o n)")))
                        for i, (d, tri) in enumerate(zip(DIRS, (upper, lower))):
                            for c in range(NT):
                                ins = nc.vector.tensor_scalar(gt[:, i, c, :], tri[:, :], sc_next(G, c, d), None,
                                                              ALU.mult)
                            ins.then_inc(s["gtri_ready"], 1)
                        nc.vector.tensor_scalar(gtm[0:META, :], upper[0:META, 0:META], sc_next(G, NT, "f"), None,
                                                ALU.mult).then_inc(s["gtri_ready"], 1)
                    elif part.startswith("CONV"):
                        i = int(part[-1])
                        early.wait_read(dve, "qkv"[i], hn)
                        early.wait_read(dve, f"pm{i}", hn)
                        link(nc.vector.tensor_scalar(cv[:, i, :], pre[:, i, 0:TOK], cw[:, CW * i:CW * i + 1],
                                                     None, ALU.mult))
                        for j in range(1, CW):
                            ins = nc.vector.scalar_tensor_tensor(
                                out=cv[:, i, :], in0=pre[:, i, j:j + TOK], scalar=cw[:, CW * i + j:CW * i + j + 1],
                                in1=cv[:, i, :], op0=ALU.mult, op1=ALU.add)
                            if j < CW - 1:
                                link(ins)
                        ins.then_inc(s["conv_ready"], 1)
                    elif part == "DECAY_ARG":
                        dve.wait_ge(s["expb_ready"], 2 * hn + 2)
                        for i, d in enumerate(DIRS):
                            for c in range(NT):
                                ins = nc.vector.tensor_scalar(dec[:, i, c, :], out("b" + d)[:, c * P:(c + 1) * P],
                                                              sc_next(NEGB, c, d), 0.0, ALU.add, ALU.min)
                            early.reads("b" + d, ins)
                        early.wait_full(dve, "bm", hn)
                        early.reads("bm", nc.vector.tensor_scalar(decm[:, :], out("bm")[0:META, 0:META],
                                                                  sc_next(NEGB, NT, "f"), 0.0, ALU.add, ALU.min))
                        early.wait_read(dve, "bm", hn)
                        early.wait_read(dve, "bb", hn)
                    elif part == "UNIT":
                        unit(hn)
                    elif part == "MATRICES":
                        matrices(hn, link)
                    elif part == "SCALES":
                        early.wait_read(dve, "ss", hn)
                        link(nc.vector.reciprocal(inv_len[:, :], inv_len[:, :]))
                        for i in range(2):
                            for t in range(NT):
                                nc.vector.tensor_scalar(gt[:, i, t, :], ident[:, :],
                                                        inv_len[:, NC5 * i + t:NC5 * i + t + 1], None, ALU.mult)
                        nc.vector.tensor_scalar(gtm[0:META, :], ident[0:META, 0:META],
                                                inv_len[0:META, 2 * NC5 - 1:2 * NC5], None, ALU.mult)\
                            .then_inc(s["diag_ready"], 1)

                def grow(level, h):
                    if level == 0:
                        dve.wait_ge(s["masked_ready"], 18 * h + masked(0))
                        for i in range(2):
                            nc.vector.tensor_tensor(xt[:, i, :, :], over_chunks(ident[:, :]), lm[:, i, 0, :, :],
                                                    ALU.subtract).then_inc(s["x_start"], 1)
                        nc.vector.tensor_tensor(xm[0:META, 1, 0:META], ident[0:META, 0:META],
                                                lmm[0:META, 0, 0:META], ALU.subtract).then_inc(s["x_start"], 1)
                        return
                    for d, i in [("f", 0), ("b", 1)] + ([("m", 2)] if level < 4 else []):
                        name = f"z{d}{level}"
                        bk.wait_full(dve, name, h)
                        if d == "m":
                            bk.reads(name, nc.vector.tensor_tensor(xm[0:META, 1, 0:META], xm[0:META, 1, 0:META],
                                                                   out("ym1")[0:META, 0:META], ALU.subtract))
                        else:
                            bk.reads(name, nc.vector.tensor_tensor(xt[:, i, :, :], xt[:, i, :, :],
                                                                   by_chunk(out(name)[:, :]), ALU.subtract))

                def scan_round(steps, h):
                    for d, c in steps:
                        if c != first[d]:
                            bk.wait_full(dve, f"r{d}{c}", h)
                            bk.reads(f"r{d}{c}", nc.vector.scalar_tensor_tensor(
                                out=rhs[:, DIRS.index(d), :], in0=out(f"r{d}{c}")[:, 0:DK],
                                scalar=sc(NEGEXP, c, d), in1=v_tok[:, c, :], op0=ALU.mult, op1=ALU.add))
                    for d, c in steps:
                        if d == "f":
                            n, name = rows(c), f"w{d}{c}"
                            bk.wait_full(dve, name, h)
                            nc.vector.tensor_scalar(vn[0:n, 0, :], out(name)[0:n, 0:DK], sc(BETA, c, d),
                                                    None, ALU.mult)
                            bk.reads(name, nc.vector.tensor_scalar(v2[0:n, 0, :], out(name)[0:n, 0:DK],
                                                                   sc(BETAEND, c, d), None, ALU.mult))
                    for d, c in steps:
                        if c != final[d]:
                            i, name = DIRS.index(d), f"s{d}{c}"
                            bk.wait_full(dve, name, h)
                            if c == first[d]:
                                ins = nc.vector.tensor_copy(state[:, i, :], out(name)[:, 0:DK])
                            else:
                                ins = nc.vector.scalar_tensor_tensor(
                                    out=state[:, i, :], in0=state[:, i, :], scalar=sc(END, c, d),
                                    in1=out(name)[:, 0:DK], op0=ALU.mult, op1=ALU.add)
                            bk.reads(name, ins)

                def this(part, h):
                    if part.startswith("grow"):
                        grow(int(part[-1]), h)
                    elif part.startswith("scan"):
                        scan_round(scan[int(part[-1])], h)
                    elif part == "tail0":
                        dve.wait_ge(s["ysq_ready"], h + 1)
                        Chain(dve, s["dve_steps"], before, h, 2)(
                            nc.vector.tensor_reduce(rstd[:, :], ysq[:, :, :], AX.X, ALU.add))
                        nc.vector.tensor_scalar(rstd[:, :], rstd[:, :], 1.0 / DK, RMS_EPS, ALU.mult, ALU.add)\
                            .then_inc(s["ms_ready"], 1)
                    elif part == "tail1":
                        dve.wait_ge(s["std_ready"], h + 1)
                        Chain(dve, s["dve_steps"], before + 1, h, 2)(nc.vector.reciprocal(rstd[:, :], rstd[:, :]))
                        for c in range(NT):
                            ins = nc.vector.tensor_scalar(y[:, c, :], out("o")[:, c * P:(c + 1) * P],
                                                          rstd[:, c:c + 1], None, ALU.mult)
                        bk.reads("o", ins)
                    elif part == "tail2":
                        bk.wait_full(dve, "ty", h)
                        dst = head_of(yT, h)
                        bk.reads("ty", nc.vector.scalar_tensor_tensor(out=gz[:, :], in0=out("ty")[:, :],
                                                                      scalar=norm_g[:, 0:1], in1=gz[:, :],
                                                                      op0=ALU.mult, op1=ALU.mult))
                        dve.wait_ge(s["y_hi"], h + 1)
                        nc.vector.tensor_tensor(dst[1], gz[:, :], dst[0], ALU.subtract).then_inc(s["y_lo"], 1)

                run(dve, this, following)



MIX_FIRST = 4


def mixer_out(core, weights, a, h0, merged, h1T, ident):
    nc = core.nc
    with ExitStack() as ctx:
        mT = sbuf_pair(nc, ctx, "mix_T", [P, KC, SEQ])
        gain = sbuf(nc, ctx, "mix_gain", [P, D])
        bias = sbuf(nc, ctx, "mix_bias", [P, D])
        stats = sbuf(nc, ctx, "mix_stats", [P, NT, 12])
        mv = sbuf(nc, ctx, "mix_mv", [P, NT, 2])
        rstd = sbuf(nc, ctx, "mix_rstd", [P, NT])
        gb_in, steps_done, var_ready, std_ready, row_ready = (
            core.sem("mix_" + n) for n in ("gb_in", "steps", "var_ready", "std_ready", "row_ready"))
        hi_done = {kind: core.sem(f"mix_{kind}_hi") for kind in "mh"}
        order = [(f"m{t}{h}", (2 * t + h) % 8) for t in range(NT) for h in range(2)]
        order += [(f"o{t}{n}", (2 * t + n) % 8) for t in range(NT) for n in range(2)]
        order += [(f"h{t}{h}", (2 * t + h) % 8) for t in range(NT) for h in range(2)]
        bk = Banks(core, order)

        def out(name):
            return core.banks[bk.bank(name)]

        def transposed(pe, kind, src, t):
            for h in range(2):
                name = f"{kind}{t}{h}"
                bk.wait_free(pe, name)
                for c in range(4):
                    last = nc.tensor.transpose(out(name)[:, c * P:(c + 1) * P],
                                               src[:, t, (4 * h + c) * P:(4 * h + c + 1) * P], ident[:, :])
                bk.fills(name, last)

        def part(t, h):
            return slice(None), slice(4 * h, 4 * h + 4), slice(t * P, (t + 1) * P)

        def high_halves(act, kind, dst, t):
            for h in range(2):
                name = f"{kind}{t}{h}"
                bk.wait_full(act, name)
                nc.scalar.activation(dst[0][part(t, h)], out(name)[:, :].rearrange("p (c n) -> p c n", c=4),
                                     ACT.Copy).then_inc(hi_done[kind], 1)

        def low_halves(dve, kind, dst, t):
            for h in range(2):
                name = f"{kind}{t}{h}"
                dve.wait_ge(hi_done[kind], 2 * t + h + 1)
                bk.reads(name, nc.vector.tensor_tensor(
                    dst[1][part(t, h)], out(name)[:, :].rearrange("p (c n) -> p c n", c=4), dst[0][part(t, h)],
                    ALU.subtract))

        with nc.Block() as block:
            @block.sync
            def _(sp):
                sp.dma_start(gain[:, :], a["ln1_g"].partition_broadcast(P)).then_inc(gb_in, 16)
                sp.dma_start(bias[:, :], a["ln1_b"].partition_broadcast(P)).then_inc(gb_in, 16)

            @block.tensor
            def _(pe):
                for t in range(NT):
                    transposed(pe, "m", merged, t)
                for t in range(NT):
                    for h in range(2):
                        bk.wait_read(pe, f"m{t}{h}")
                    for n in range(2):
                        name = f"o{t}{n}"
                        bk.wait_free(pe, name)
                        for kc in range(KC):
                            last = pair_matmul(nc, out(name)[:, :],
                                               view(mT, slice(None), kc, slice(t * P, (t + 1) * P)),
                                               weights.block(MIX_FIRST + n, kc), kc == 0, kc == KC - 1)
                        bk.fills(name, last)
                for t in range(NT):
                    pe.wait_ge(row_ready, t + 1)
                    transposed(pe, "h", h0, t)

            @block.scalar
            def _(act):
                for t in range(NT):
                    high_halves(act, "m", mT, t)
                for t in range(NT):
                    act.wait_ge(var_ready, t + 1)
                    nc.scalar.activation(rstd[:, t:t + 1], mv[:, t, 1:2], ACT.Sqrt).then_inc(std_ready, 1)
                for t in range(NT):
                    high_halves(act, "h", h1T, t)

            @block.vector
            def _(dve):
                link = Chain(dve, steps_done)
                for t in range(NT):
                    low_halves(dve, "m", mT, t)
                dve.wait_ge(gb_in, 32)
                for t in range(NT):
                    for n in range(2):
                        name = f"o{t}{n}"
                        bk.wait_full(dve, name)
                        row = h0[:, t, n * 512:(n + 1) * 512]
                        bk.reads(name, nc.vector.scalar_tensor_tensor(out=row, in0=row, scalar=ALPHA,
                                                                      in1=out(name)[:, :], op0=ALU.mult,
                                                                      op1=ALU.add))
                        bk.wait_read(dve, name)
                    for n in range(2):
                        ins = nc.vector.bn_stats(stats[:, t, 6 * n:6 * n + 6], h0[:, t, n * 512:(n + 1) * 512])
                    link(ins)
                    link(nc.vector.bn_aggr(mv[:, t, :], stats[:, t, :]))
                    nc.vector.tensor_scalar(mv[:, t, 1:2], mv[:, t, 1:2], LN_EPS, None, ALU.add)\
                        .then_inc(var_ready, 1)
                    dve.wait_ge(std_ready, t + 1)
                    link(nc.vector.reciprocal(rstd[:, t:t + 1], rstd[:, t:t + 1]))
                    row = h0[:, t, :]
                    link(nc.vector.tensor_scalar(row, row, mv[:, t, 0:1], rstd[:, t:t + 1],
                                                 ALU.subtract, ALU.mult))
                    link(nc.vector.tensor_tensor(row, row, gain[:, :], ALU.mult))
                    nc.vector.tensor_tensor(row, row, bias[:, :], ALU.add).then_inc(row_ready, 1)
                for t in range(NT):
                    low_halves(dve, "h", h1T, t)


BLOCKS = NK
RING = 4


def over_blocks(eng, first, end, step):
    while first < RING:
        step(first, first)
        first += 1
    if end - first > RING:
        with eng.Fori(0, (end - first) // RING) as turn:
            for j in range(RING):
                step(turn * RING + (first + j), RING + j)
    else:
        for n in range(first, end):
            step(n, RING + n % RING)


def block_of(dram, n):
    if isinstance(n, int):
        return dram[n]
    one = dram[bass.ds(n, 1)]
    return one.rearrange("o p k n -> (o p) k n") if len(dram.shape) == 4 else one.rearrange("o p n -> (o p) n")


class Hidden:

    def __init__(self, core, ctx, a, h1T, hidden_dram):
        nc = self.nc = core.nc
        self.core, self.peer_u, self.xs, self.dram = core, a["peer_u"], h1T, hidden_dram
        self.u32 = sbuf(nc, ctx, "hid_u", [P, RING, KC, P])
        self.us = [sbuf(nc, ctx, f"hid_u_{n}", [P, 2, KC, P], BF16) for n in ("hi", "lo")]
        self.act_out = sbuf(nc, ctx, "hid_gelu", [P, RING, SEQ])
        self.u_in = [core.sem(f"hid_u_in{i}") for i in range(RING)]
        self.stored = [core.sem(f"hid_stored{i}") for i in range(RING)]
        self.u_hi, self.u_lo, self.formed, self.gelu = (
            core.sem("hid_" + n) for n in ("u_hi", "u_lo", "formed", "gelu"))

    def load(self, sp, n, m):
        slot = m % RING
        block = block_of(self.peer_u, n)
        if m >= RING:
            sp.wait_ge(self.u_lo, n - (RING - 1))
        sp.dma_start(self.u32[:, slot, :, :], block).then_inc(self.u_in[slot], 16)

    def store(self, sp, n, m):
        block = block_of(self.dram, n)
        sp.wait_ge(self.gelu, n + 1)
        sp.dma_start(block, self.act_out[:, m % RING, :]).then_inc(self.stored[m % RING], 16)

    def form(self, pe, n, m):
        bank = self.core.banks[4 + m % RING]
        pe.wait_ge(self.u_hi, n + 1)
        pe.wait_ge(self.u_lo, n + 1)
        if m >= RING:
            pe.wait_ge(self.gelu, n - (RING - 1))
        for kc in range(KC):
            last = pair_matmul(self.nc, bank[:, :], view(self.us, slice(None), m % 2, kc),
                               view(self.xs, slice(None), kc), kc == 0, kc == KC - 1)
        last.then_inc(self.formed, 1)

    def split_hi(self, act, n, m):
        act.wait_ge(self.u_in[m % RING], (16 // RING) * (n - m % RING) + 16)
        if m >= 2:
            act.wait_ge(self.formed, n - 1)
        self.nc.scalar.activation(self.us[0][:, m % 2, :, :], self.u32[:, m % RING, :, :],
                                  ACT.Copy).then_inc(self.u_hi, 1)

    def apply_gelu(self, act, n, m):
        act.wait_ge(self.formed, n + 1)
        if m >= RING:
            act.wait_ge(self.stored[m % RING], (16 // RING) * (n - m % RING))
        self.nc.scalar.activation(self.act_out[:, m % RING, :], self.core.banks[4 + m % RING][:, :],
                                  ACT.Gelu).then_inc(self.gelu, 1)

    def split_lo(self, pool, n, m):
        pool.wait_ge(self.u_hi, n + 1)
        if m >= 2:
            pool.wait_ge(self.formed, n - 1)
        self.nc.gpsimd.tensor_tensor(self.us[1][:, m % 2, :, :], self.u32[:, m % RING, :, :],
                                     self.us[0][:, m % 2, :, :], ALU.subtract).then_inc(self.u_lo, 1)



def retrieve(core, weights, a, h1T, picked, hidden, blocks, ident):
    nc = core.nc
    HP = 2 * PH
    share = blocks // NT
    LEAST = -3.0e38
    with ExitStack() as ctx:
        qT = sbuf(nc, ctx, "top_q", [P, HP, SEQ])
        keys = sbuf(nc, ctx, "top_keys", [P, HP, NK])
        iota = sbuf(nc, ctx, "top_iota", [P, TOPK])
        score = sbuf(nc, ctx, "top_score", [P, HP, NK])
        work = sbuf(nc, ctx, "top_work", [P, HP * NK])
        rest = work[:, :].rearrange("p (n k) -> p n k", n=HP)
        best = sbuf(nc, ctx, "top_best", [P, HP, TOPK])
        besti = sbuf(nc, ctx, "top_best_index", [P, HP, TOPK], U32)
        bestf = sbuf(nc, ctx, "top_best_index_f", [P, HP, TOPK])
        pairs = sbuf(nc, ctx, "top_pairs", [P, PH, TOPK, TOPK])
        left = work[:, :].rearrange("p (h a b) -> p h a b", h=PH, a=TOPK)
        top = sbuf(nc, ctx, "top_of_pairs", [P, PH, TOPK])
        topi = sbuf(nc, ctx, "top_of_pairs_index", [P, PH, TOPK], U32)
        rank = sbuf(nc, ctx, "top_rank", [P, 2, PH, TOPK], U32)
        rankf = sbuf(nc, ctx, "top_rank_f", [P, 2, PH, TOPK])
        total = sbuf(nc, ctx, "top_total", [P, PH])
        after_wait = sbuf(nc, ctx, "top_after_wait", [P, 1])
        chosen = sbuf(nc, ctx, "top_chosen", [P, 3, PH, TOPK])
        keys_in, dve_steps, exp_arg, exp_ready, chosen_ready, turned = (
            core.sem("top_" + n) for n in ("keys_in", "dve_steps", "exp_arg", "exp_ready",
                                           "chosen_ready", "turned"))
        qb = Banks(core, [(f"q{c}", c) for c in range(4)], 4)
        bk = Banks(core, [(f"s{c}", c) for c in range(4)] + [("t", 0)], NT)

        with nc.Block() as block:
            @block.sync
            def _(sp):
                for g in range(8):
                    weights.load(sp, g, g, True)
                sp.dma_start(keys[:, :, :], a["peer_keys"]).then_inc(keys_in, 16)
                sp.dma_start(iota[:, :], a["iota"][:, 0:TOPK]).then_inc(keys_in, 16)
                for n in range(RING):
                    hidden.load(sp, n, n)
                for g in range(8, 16):
                    weights.load(sp, g, g, True)

                def store_and_load(n, m):
                    hidden.store(sp, n, m)
                    hidden.load(sp, n + RING, m + RING)

                over_blocks(sp, 0, blocks, store_and_load)

            @block.tensor
            def _(pe):
                for n in range(4):
                    for c in range(4):
                        weights.wait(pe, 4 * n + c)
                        qb.wait_free(pe, f"q{c}", n)
                        for kc in range(KC):
                            last = pair_matmul(nc, core.banks[c][:, :], weights.columns(n % weights.blocks, c, kc),
                                               view(h1T, slice(None), kc), kc == 0, kc == KC - 1)
                        qb.fills(f"q{c}", last)
                pe.wait_ge(keys_in, 32)
                for c in range(4):
                    qb.wait_read(pe, f"q{c}", 3)

                def scores(t):
                    for c in range(4):
                        bk.wait_free(pe, f"s{c}", t)
                        for j in range(4):
                            hp = 4 * c + j
                            last = nc.tensor.matmul(core.banks[c][:, j * NK:(j + 1) * NK],
                                                    qT[:, hp, t * P:(t + 1) * P], keys[:, hp, :],
                                                    start=True, stop=True)
                        bk.fills(f"s{c}", last)

                for t in range(NT):
                    scores(t)
                    over_blocks(pe, t * share, (t + 1) * share, lambda n, m: hidden.form(pe, n, m))
                    pe.wait_ge(chosen_ready, 3 * t + 3)
                    bk.wait_free(pe, "t", t)
                    for j in range(3):
                        last = nc.tensor.transpose(core.banks[0][:, j * P:(j + 1) * P],
                                                   chosen[:, j, :, :].rearrange("p h k -> p (h k)"), ident[:, :])
                    bk.fills("t", last)

            @block.scalar
            def _(act):
                for g in range(4 * weights.blocks):
                    weights.hi(act, g, g, g // 4)
                for n in range(4):
                    for c in range(4):
                        qb.wait_full(act, f"q{c}", n)
                        qb.reads(f"q{c}", nc.scalar.activation(qT[:, 4 * n + c, :], core.banks[c][:, :], ACT.Copy))
                        if n + weights.blocks < 4:
                            g = 4 * (n + weights.blocks) + c
                            weights.hi(act, g, g, n % weights.blocks)
                hidden.split_hi(act, 0, 0)

                def step(n, m):
                    hidden.split_hi(act, n + 1, m + 1)
                    hidden.apply_gelu(act, n, m)

                for t in range(NT):
                    for c in range(4):
                        bk.wait_full(act, f"s{c}", t)
                        act.wait_ge(exp_arg, t + 1)
                        bk.reads(f"s{c}", nc.scalar.activation(
                            score[:, 4 * c:4 * c + 4, :],
                            core.banks[c][:, :].rearrange("p (j n) -> p j n", j=4), ACT.Copy))
                    over_blocks(act, t * share, (t + 1) * share - RING, step)
                    act.wait_ge(exp_arg, t + 2)
                    nc.scalar.activation(top[:, :, :], top[:, :, :], ACT.Exp).then_inc(exp_ready, 1)
                    over_blocks(act, (t + 1) * share - RING, (t + 1) * share, step)
                    bk.wait_full(act, "t", t)
                    bk.reads("t", nc.scalar.activation(
                        picked[:, :, t * P:(t + 1) * P],
                        core.banks[0][:, 0:3 * P].rearrange("p (j n) -> p j n", j=3), ACT.Copy))

            @block.gpsimd
            def _(pool):
                for g in range(16):
                    weights.lo(pool, g, g, g // 4 % weights.blocks)
                over_blocks(pool, 0, blocks, lambda n, m: hidden.split_lo(pool, n, m))

            @block.vector
            def _(dve):
                nc.vector.memset(total[:, :], 0.0).then_inc(exp_arg, 1)
                dve.wait_ge(exp_arg, 1)
                dve.wait_ge(keys_in, 32)
                with dve.Fori(0, NT) as t:
                    link = Chain(dve, dve_steps, 0, t, 18)

                    def step(ins):
                        link(ins)
                        nc.vector.memset(after_wait[:, :], 0.0)

                    def best_of(values, reduced, n, out, index):
                        for i in range(n):
                            ins = nc.vector.max(out[:, i, 0:8], values[:, i, :])
                        step(ins)
                        for i in range(n):
                            nc.vector.max_index(index[:, i, 0:8], out[:, i, 0:8], values[:, i, :])
                            ins = nc.vector.match_replace(reduced[:, i, :], out[:, i, 0:8], values[:, i, :], LEAST)
                        step(ins)
                        for i in range(n):
                            ins = nc.vector.max(out[:, i, 8:16], reduced[:, i, :])
                        step(ins)
                        for i in range(n):
                            ins = nc.vector.max_index(index[:, i, 8:16], out[:, i, 8:16], reduced[:, i, :])
                        step(ins)

                    for c in range(4):
                        bk.wait_read(dve, f"s{c}", t)
                    nc.vector.memset(after_wait[:, :], 0.0)
                    best_of(score, rest, HP, best, besti)
                    by_head = best[:, :, :].rearrange("p (h s) k -> p h s k", s=2)
                    wide = [P, PH, TOPK, TOPK]
                    nc.vector.tensor_copy(bestf[:, :, :], besti[:, :, :])
                    step(nc.vector.tensor_tensor(pairs[:, :, :, :], by_head[:, :, 0, :].unsqueeze(3).broadcast_to(wide),
                                                 by_head[:, :, 1, :].unsqueeze(2).broadcast_to(wide), ALU.add))
                    best_of(pairs[:, :, :, :].rearrange("p h a b -> p h (a b)"),
                            left[:, :, :, :].rearrange("p h a b -> p h (a b)"), PH, top, topi)
                    nc.vector.tensor_scalar(rank[:, 0, :, :], topi[:, :, :], 4, None, ALU.logical_shift_right)
                    link(nc.vector.tensor_scalar(rank[:, 1, :, :], topi[:, :, :], 15, None, ALU.bitwise_and))
                    link(nc.vector.tensor_copy(rankf[:, :, :, :], rank[:, :, :, :]))
                    link(nc.vector.tensor_copy(total[:, :], top[:, :, 0]))
                    nc.vector.tensor_tensor(top[:, :, :], top[:, :, :],
                                            total[:, :].unsqueeze(2).broadcast_to([P, PH, TOPK]),
                                            ALU.subtract).then_inc(exp_arg, 1)
                    of_rank = bestf[:, :, :].rearrange("p (h s) k -> p h s k", s=2)
                    for side in range(2):
                        link(nc.vector.tensor_tensor(
                            left[:, :, :, :], rankf[:, side, :, :].unsqueeze(3).broadcast_to(wide),
                            iota[:, :].unsqueeze(1).unsqueeze(1).broadcast_to(wide), ALU.is_equal))
                        link(nc.vector.tensor_tensor(
                            left[:, :, :, :], left[:, :, :, :],
                            of_rank[:, :, side, :].unsqueeze(2).broadcast_to(wide), ALU.mult))
                        nc.vector.tensor_reduce(chosen[:, 1 + side, :, :], left[:, :, :, :], AX.X, ALU.add)\
                            .then_inc(chosen_ready, 1)
                        dve.wait_ge(chosen_ready, 3 * t + (side + 1))
                    dve.wait_ge(exp_ready, t + 1)
                    link(nc.vector.tensor_reduce(total[:, :], top[:, :, :], AX.X, ALU.add))
                    link(nc.vector.reciprocal(total[:, :], total[:, :]))
                    nc.vector.tensor_tensor(chosen[:, 0, :, :], top[:, :, :],
                                            total[:, :].unsqueeze(2).broadcast_to([P, PH, TOPK]),
                                            ALU.mult).then_inc(chosen_ready, 1)
                    dve.wait_ge(chosen_ready, 3 * t + 3)
                    link.ends_turn()


def spread(core, a, picked, weights_dram, hidden, blocks, incoming):
    nc = core.nc
    G = 4
    SLOTS = 4
    SPAN = 64
    CHUNKS = 8
    per = 2
    busy = SEQ // G // per
    with ExitStack() as ctx:
        iota = sbuf(nc, ctx, "spread_iota", [P, NK])
        first = sbuf_pair(nc, ctx, "spread_first", [P, SLOTS, G, NK])
        second = sbuf(nc, ctx, "spread_second", [P, SLOTS, G, NK], BF16)
        rounded = sbuf(nc, ctx, "spread_rounded", [P, SEQ], BF16)
        weight = sbuf(nc, ctx, "spread_weight", [P, 2, SEQ])
        grid = sbuf(nc, ctx, "spread_grid", [P, 2, NK, SPAN])
        iota_in, dve_steps, first_ready, second_ready = (
            core.sem("spread_" + n) for n in ("iota_in", "dve_steps", "first_ready", "second_ready"))
        stored = [core.sem(f"spread_stored{side}") for side in range(2)]
        TURN = SLOTS * G
        bk = Banks(core, [(f"w{u}", u) for u in range(SLOTS)], SEQ // TURN)
        spans = SEQ // SPAN
        span_turns = SPAN // TURN
        span_blocks = busy // spans
        turn_blocks = SLOTS // per

        with nc.Block() as block:
            @block.sync
            def _(sp):
                sp.dma_start(iota[:, :], a["iota"]).then_inc(iota_in, 16)

                def store_and_load(n, m):
                    hidden.store(sp, n, m)
                    hidden.load(sp, n + RING, m + RING)

                over_blocks(sp, blocks, BLOCKS - RING, store_and_load)
                for n in range(BLOCKS - RING, BLOCKS):
                    hidden.store(sp, n, n)
                    incoming.load_values(sp, n - (BLOCKS - RING), n - (BLOCKS - RING))
                for side in range(2):
                    sp.wait_ge(stored[side], 16 * CHUNKS * spans // 2)
                for n in range(RING):
                    sp.wait_ge(hidden.stored[n], 16 * BLOCKS // RING)
                    incoming.load_scores(sp, n, n)

            @block.vector
            def _(dve):
                link = Chain(dve, dve_steps)
                link(nc.vector.tensor_copy(rounded[:, :], picked[:, 0, :]))
                link(nc.vector.tensor_copy(weight[:, 0, :], rounded[:, :]))
                link(nc.vector.tensor_tensor(weight[:, 1, :], picked[:, 0, :], weight[:, 0, :], ALU.subtract))
                dve.wait_ge(iota_in, 16)
                with dve.Fori(0, SEQ // TURN) as turn:
                    for u in range(SLOTS):
                        bk.wait_used(dve, f"w{u}", turn)
                        for j in range(G):
                            token = turn * TURN + (u * G + j)
                            for half in range(2):
                                ins = nc.vector.tensor_scalar(
                                    first[half][:, u, j, :], iota[:, :],
                                    picked[:, 1, bass.ds(token, 1)], weight[:, half, bass.ds(token, 1)],
                                    ALU.is_equal, ALU.mult)
                        ins.then_inc(first_ready, 1)
                        for j in range(G):
                            token = turn * TURN + (u * G + j)
                            ins = nc.vector.tensor_scalar(second[:, u, j, :], iota[:, :],
                                                          picked[:, 2, bass.ds(token, 1)], None,
                                                          ALU.is_equal)
                        ins.then_inc(second_ready, 1)

            @block.tensor
            def _(pe):
                with pe.Fori(0, SEQ // TURN // 2) as two:
                    for j in range(2 * turn_blocks):
                        turn = two * 2 + j // turn_blocks
                        hidden.form(pe, two * (2 * turn_blocks) + (blocks + j), RING + j)
                        for u in range(per * (j % turn_blocks), per * (j % turn_blocks + 1)):
                            pe.wait_ge(first_ready, SLOTS * turn + (u + 1))
                            pe.wait_ge(second_ready, SLOTS * turn + (u + 1))
                            bk.wait_free(pe, f"w{u}", turn)
                            for i in range(G):
                                for half in range(2):
                                    last = nc.tensor.matmul(core.banks[u][:, i * NK:(i + 1) * NK],
                                                            first[half][:, u, i, :], second[:, u, i, :],
                                                            start=half == 0, stop=half == 1)
                            bk.fills(f"w{u}", last)
                over_blocks(pe, blocks + busy, BLOCKS, lambda n, m: hidden.form(pe, n, m))

            @block.scalar
            def _(act):
                def step(n, m, side, turn, in_span, u0):
                    hidden.split_hi(act, n + 1, m + 1)
                    hidden.apply_gelu(act, n, m)
                    for u in range(u0, u0 + per):
                        bk.wait_full(act, f"w{u}", turn)
                        token = in_span * TURN + u * G
                        bk.reads(f"w{u}", nc.scalar.activation(
                            grid[:, side, :, token:token + G],
                            core.banks[u][:, :].rearrange("p (j n) -> p n j", j=G), ACT.Copy))

                def store(side, span, chunk):
                    keys = slice(NK // CHUNKS * chunk, NK // CHUNKS * (chunk + 1))
                    cols = slice(span * SPAN, (span + 1) * SPAN) if isinstance(span, int) \
                        else bass.ds(span * SPAN, SPAN)
                    nc.scalar.dma_start(weights_dram.rearrange("b a t -> a b t")[:, keys, cols],
                                        grid[:, side, keys, :]).then_inc(stored[side], 16)

                def span_steps(t, side, peeled):
                    if not peeled:
                        act.wait_ge(stored[side], t * (16 * CHUNKS // 2) - side * (16 * CHUNKS // 2))
                    for j in range(span_blocks):
                        in_span = j // turn_blocks
                        step(t * span_blocks + (blocks + j), RING + j, side, t * span_turns + in_span, in_span,
                             per * (j % turn_blocks))
                        if j < span_blocks // 2 and not (peeled and side == 0):
                            for chunk in range(2 * j, 2 * j + 2):
                                store(1 - side, t - 1, chunk)
                    for u in range(SLOTS):
                        bk.wait_read(act, f"w{u}", t * span_turns + (span_turns - 1))

                for side in range(2):
                    span_steps(side, side, True)
                with act.Fori(0, spans // 2 - 1) as pair:
                    for side in range(2):
                        span_steps(pair * 2 + (2 + side), side, False)

                def plain(n, m):
                    if not (isinstance(n, int) and n == BLOCKS - 1):
                        hidden.split_hi(act, n + 1, m + 1)
                    hidden.apply_gelu(act, n, m)

                for n in range(blocks + busy, BLOCKS):
                    plain(n, RING + n % RING)
                    if n < blocks + busy + CHUNKS // 2:
                        for chunk in range(2 * (n - blocks - busy), 2 * (n - blocks - busy) + 2):
                            store(1, spans - 1, chunk)

            @block.gpsimd
            def _(pool):
                over_blocks(pool, blocks, BLOCKS, lambda n, m: hidden.split_lo(pool, n, m))



GROUP = 4


class Incoming:

    def __init__(self, core, ctx, a, hidden_dram, weights_dram):
        nc = core.nc
        self.dram = {"v": a["peer_v"], "hidden": hidden_dram, "weights": weights_dram}
        self.v = sbuf(nc, ctx, "ex_v", [P, RING, D])
        self.weights = sbuf(nc, ctx, "ex_weights", [P, RING, SEQ])
        self.gated = sbuf(nc, ctx, "ex_gated", [P, RING, SEQ])
        self.arrived = {name: [core.sem(f"ex_{name}_in{i}") for i in range(RING)] for name in self.dram}

    def load_values(self, sp, n, m):
        block = block_of(self.dram["v"], n)
        sp.dma_start(self.v[:, m % RING, :], block).then_inc(self.arrived["v"][m % RING], 16)

    def load_scores(self, sp, n, m):
        for name, dst in (("hidden", self.gated), ("weights", self.weights)):
            block = block_of(self.dram[name], n)
            sp.dma_start(dst[:, m % RING, :], block).then_inc(self.arrived[name][m % RING], 16)


def experts(core, incoming, acc):
    nc = core.nc
    with ExitStack() as ctx:
        v32, wt, g32 = incoming.v, incoming.weights, incoming.gated
        v_in, wt_in, hid_in = (incoming.arrived[name] for name in ("v", "weights", "hidden"))
        vs = [sbuf(nc, ctx, f"ex_v_{n}", [P, 2 * GROUP, D], BF16) for n in ("hi", "lo")]
        gs = [sbuf(nc, ctx, f"ex_gated_{n}", [P, 2 * GROUP, SEQ], BF16) for n in ("hi", "lo")]
        names = "v_hi v_lo gated gated_hi gated_lo unit added".split()
        s = {n: core.sem("ex_" + n) for n in names}

        def run(eng, step, last_units):
            for j in range(GROUP):
                step(j, j)
            with eng.Fori(0, (BLOCKS - 2 * GROUP) // (2 * GROUP)) as turn:
                for j in range(2 * GROUP):
                    step(turn * (2 * GROUP) + (GROUP + j), GROUP + j)
            for n in range(BLOCKS - GROUP, BLOCKS):
                step(n, n)
            for n in range(BLOCKS, BLOCKS + GROUP):
                last_units(n, n)

        def arrived(n, m):
            return (16 // RING) * (n - m % RING) + 16

        with nc.Block() as block:
            @block.sync
            def _(sp):
                def load(n, m):
                    sp.wait_ge(s["gated_lo"], n - (RING - 1))
                    incoming.load_scores(sp, n, m)
                    sp.wait_ge(s["v_lo"], n - (RING - 1))
                    incoming.load_values(sp, n, m)

                over_blocks(sp, RING, BLOCKS, load)

            @block.tensor
            def _(pe):
                def units(n, m):
                    side = (m // GROUP - 1) % 2
                    for u in (2 * (m % GROUP), 2 * (m % GROUP) + 1):
                        half, t = divmod(u, NT)
                        bank = core.banks[4 + t]
                        pe.wait_ge(s["added"], 2 * n + (u - 2 * GROUP - 2 * (m % GROUP) + 1))
                        for j in range(GROUP):
                            slot = GROUP * side + j
                            for i, (l, r) in enumerate(PASSES):
                                last = nc.tensor.matmul(bank[:, :], gs[l][:, slot, t * P:(t + 1) * P],
                                                        vs[r][:, slot, half * 512:(half + 1) * 512],
                                                        start=j == 0 and i == 0,
                                                        stop=j == GROUP - 1 and i == 2)
                        last.then_inc(s["unit"], 1)

                def step(n, m):
                    if m >= GROUP:
                        if m % GROUP == 0:
                            for name in ("gated_hi", "gated_lo", "v_hi", "v_lo"):
                                pe.wait_ge(s[name], n)
                        units(n, m)

                run(pe, step, step)

            @block.scalar
            def _(act):
                def step(n, m):
                    act.wait_ge(v_in[m % RING], arrived(n, m))
                    if m >= GROUP:
                        act.wait_ge(s["added"], 2 * n + (NT - 2 * (m % GROUP) - 2 * GROUP))
                    nc.scalar.activation(vs[0][:, m % 8, :], v32[:, m % RING, :], ACT.Copy).then_inc(s["v_hi"], 1)
                    act.wait_ge(s["gated"], n + 1)
                    nc.scalar.activation(gs[0][:, m % 8, :], g32[:, m % RING, :], ACT.Copy)\
                        .then_inc(s["gated_hi"], 1)

                run(act, step, lambda n, m: None)

            @block.gpsimd
            def _(pool):
                def step(n, m):
                    pool.wait_ge(s["v_hi"], n + 1)
                    nc.gpsimd.tensor_tensor(vs[1][:, m % 8, :], v32[:, m % RING, :], vs[0][:, m % 8, :],
                                            ALU.subtract).then_inc(s["v_lo"], 1)

                run(pool, step, lambda n, m: None)

            @block.vector
            def _(dve):
                def add_units(n, m):
                    for u in (2 * (m % GROUP), 2 * (m % GROUP) + 1):
                        half, t = divmod(u, NT)
                        dve.wait_ge(s["unit"], 2 * n + (u - 2 * GROUP - 2 * (m % GROUP) + 1))
                        part = acc[:, t, half * 512:(half + 1) * 512]
                        nc.vector.tensor_tensor(part, part, core.banks[4 + t][:, :], ALU.add)\
                            .then_inc(s["added"], 1)

                def step(n, m):
                    dve.wait_ge(hid_in[m % RING], arrived(n, m))
                    dve.wait_ge(wt_in[m % RING], arrived(n, m))
                    nc.vector.tensor_tensor(g32[:, m % RING, :], g32[:, m % RING, :], wt[:, m % RING, :], ALU.mult)\
                        .then_inc(s["gated"], 1)
                    dve.wait_ge(s["gated_hi"], n + 1)
                    nc.vector.tensor_tensor(gs[1][:, m % 8, :], g32[:, m % RING, :], gs[0][:, m % 8, :],
                                            ALU.subtract).then_inc(s["gated_lo"], 1)
                    if m >= GROUP:
                        add_units(n, m)

                for t in range(NT):
                    nc.vector.tensor_scalar(acc[:, t, :], acc[:, t, :], ALPHA, None, ALU.mult)\
                        .then_inc(s["added"], 1)
                dve.wait_ge(s["added"], NT)
                run(dve, step, add_units)


def finish(core, a, acc, out):
    nc = core.nc
    with ExitStack() as ctx:
        gain = sbuf(nc, ctx, "fin_gain", [P, D])
        bias = sbuf(nc, ctx, "fin_bias", [P, D])
        stats = sbuf(nc, ctx, "fin_stats", [P, NT, 12])
        mv = sbuf(nc, ctx, "fin_mv", [P, NT, 2])
        rstd = sbuf(nc, ctx, "fin_rstd", [P, NT])
        shift = sbuf(nc, ctx, "fin_shift", [P, NT])
        gb_in, steps_done, var_ready, std_ready, shift_ready, normed, gained, row_ready, stored = (
            core.sem("fin_" + n) for n in ("gb_in", "steps", "var_ready", "std_ready", "shift_ready", "normed",
                                           "gained", "row_ready", "stored"))
        with nc.Block() as block:
            @block.sync
            def _(sp):
                sp.dma_start(gain[:, :], a["ln2_g"].partition_broadcast(P)).then_inc(gb_in, 16)
                sp.dma_start(bias[:, :], a["ln2_b"].partition_broadcast(P)).then_inc(gb_in, 16)
                for t in range(NT):
                    sp.wait_ge(row_ready, t + 1)
                    sp.dma_start(out[t * P:(t + 1) * P, :], acc[:, t, :]).then_inc(stored, 16)
                sp.wait_ge(stored, 16 * NT)

            @block.scalar
            def _(act):
                act.wait_ge(var_ready, 1)
                nc.scalar.activation(rstd[:, :], mv[:, :, 1], ACT.Sqrt).then_inc(std_ready, 1)
                act.wait_ge(shift_ready, 1)
                for t in range(NT):
                    nc.scalar.activation(acc[:, t, :], acc[:, t, :], ACT.Identity, bias=shift[:, t:t + 1],
                                         scale=rstd[:, t:t + 1]).then_inc(normed, 1)

            @block.gpsimd
            def _(pool):
                for t in range(NT):
                    pool.wait_ge(gained, t + 1)
                    nc.gpsimd.tensor_tensor(acc[:, t, :], acc[:, t, :], bias[:, :], ALU.add)\
                        .then_inc(row_ready, 1)

            @block.vector
            def _(dve):
                link = Chain(dve, steps_done)
                for t in range(NT):
                    for n in range(2):
                        ins = nc.vector.bn_stats(stats[:, t, 6 * n:6 * n + 6], acc[:, t, n * 512:(n + 1) * 512])
                link(ins)
                for t in range(NT):
                    ins = nc.vector.bn_aggr(mv[:, t, :], stats[:, t, :])
                link(ins)
                nc.vector.tensor_scalar(mv[:, :, 1], mv[:, :, 1], LN_EPS, None, ALU.add).then_inc(var_ready, 1)
                dve.wait_ge(std_ready, 1)
                link(nc.vector.reciprocal(rstd[:, :], rstd[:, :]))
                link(nc.vector.tensor_tensor(shift[:, :], mv[:, :, 0], rstd[:, :], ALU.mult))
                nc.vector.tensor_scalar(shift[:, :], shift[:, :], -1.0, None, ALU.mult).then_inc(shift_ready, 1)
                dve.wait_ge(gb_in, 32)
                for t in range(NT):
                    dve.wait_ge(normed, t + 1)
                    nc.vector.tensor_tensor(acc[:, t, :], acc[:, t, :], gain[:, :], ALU.mult).then_inc(gained, 1)


def program(nc, a, out):
    with ExitStack() as ctx:
        core = Core(nc, ctx)
        hidden_dram = nc.dram_tensor("expert_hidden", [NK, NK, SEQ], F32).ap()
        weights_dram = nc.dram_tensor("expert_weights", [NK, NK, SEQ], F32).ap()
        ident = sbuf(nc, ctx, "ident", [P, P])
        h0 = sbuf(nc, ctx, "h0", [P, NT, D])
        hT = sbuf_pair(nc, ctx, "hT", [P, KC, TOK])
        weights = Weights(core)
        h1T = view(hT, slice(None), slice(None), slice(META, TOK))
        with ExitStack() as mixer:
            merged = sbuf(nc, mixer, "merged", [P, NT, D])
            with ExitStack() as part:
                yT = sbuf_pair(nc, part, "ret_yT", [P, 4 * RH, SEQ])
                weights.open(part, "ret", 3, a["w_ret"])
                ready = 4
                embed(core, weights, ready, a, h0, hT, ident)
                retention(core, weights, ready, a, hT, yT, merged, ident)
                weights.close(12 * RH)
                weights.dram = a["w_ret_out"]
                branch_out(core, weights, "ret_out", hT, yT, 4 * RH, 3, merged, False)
                weights.close(24)
            with ExitStack() as part:
                yT = sbuf_pair(nc, part, "dn_yT", [P, DH, SEQ])
                weights.open(part, "dn", 1, a["w_dn"])
                delta_net(core, weights, a, hT, yT, ident)
                weights.close(4 * DH)
                weights.dram = a["w_dn_out"]
                weights.extend(part, "dn_out", 5)
                branch_out(core, weights, "dn_out", hT, yT, DH, 1, merged, True, extra=2)
                mixer_out(core, weights, a, h0, merged, h1T, ident)
                weights.close(24)
        with ExitStack() as last:
            incoming = Incoming(core, last, a, hidden_dram, weights_dram)
            with ExitStack() as part:
                picked = sbuf(nc, part, "picked", [P, 3, SEQ])
                hidden = Hidden(core, part, a, h1T, hidden_dram)
                beside_retrieval = 48
                with ExitStack() as queries:
                    weights.open(queries, "top", 1, a["w_query"])
                    retrieve(core, weights, a, h1T, picked, hidden, beside_retrieval, ident)
                spread(core, a, picked, weights_dram, hidden, beside_retrieval, incoming)
            experts(core, incoming, h0)
        finish(core, a, h0, out)


def shape_constants():
    pos = np.arange(TOK, dtype=np.float32)
    inv = (1.0 / (np.float32(10000.0) ** (np.arange(0, RDK, 2, dtype=np.float32) / np.float32(RDK)))).astype(np.float32)
    ang = inv[:, None] * pos[None, :]
    delta = np.arange(STRIP)[None, :] - (NT - 1) * P - np.arange(P)[:, None]
    return {
        "ident": np.eye(P, dtype=np.float32),
        "cos": np.cos(ang).astype(np.float32),
        "sin": np.sin(ang).astype(np.float32),
        "ahead": np.maximum(delta, 0).astype(np.float32),
        "behind": np.maximum(-delta, 0).astype(np.float32),
        "upper": np.triu(np.ones((P, P), np.float32)),
        "lower": np.tril(np.ones((P, P), np.float32)),
        "masks": level_masks(),
        "iota": np.tile(np.arange(NK, dtype=np.float32), (P, 1)),
    }


def level_masks():
    j, i = np.arange(P)[:, None], np.arange(P)[None, :]
    out = np.zeros((P, 2, LEVELS, P), np.float32)
    for level in range(LEVELS):
        n = 2 ** level
        same = i // (2 * n) == j // (2 * n)
        out[:, 0, level] = same & (i // n > j // n)
        out[:, 1, level] = same & (i // n < j // n)
    return out


def laid_out(x, meta_tokens, emb_ln_g, emb_ln_b, w_in, ret_decay_logit, dn_conv, dn_a_log, dn_dt_bias,
             dn_norm_g, p_ret, p_dn, w_out, ln1_g, ln1_b, peer_wq, peer_keys, peer_u, peer_v, ln2_g, ln2_b):
    c = np.ascontiguousarray

    def rows_in_chunks(w):
        return w.reshape(-1, P, w.shape[-1]).transpose(1, 0, 2)

    def slices(parts):
        w = np.concatenate(parts, 1)
        return c(w.reshape(KC, P, -1, P).transpose(2, 1, 0, 3))

    ends = np.cumsum([1024, 1024, 2048, 2048, 1024, 1024, 1024, 1024, 16, 16, 1024, 1024])
    rq, rk, rv, rg, dq, dk, dv, dz, da, db, ga, gb = np.split(w_in[0], ends[:-1], axis=1)
    ret_out, ret_out_rest = ([ga[:, n:n + 512], p_ret[0][:D, n:n + 512], p_ret[0][D:, n:n + 512]]
                             for n in (0, 512))
    return {
        "x": c(x[0]), "meta": c(meta_tokens), "emb_g": c(emb_ln_g), "emb_b": c(emb_ln_b),
        "ret_logit": c(ret_decay_logit[0].reshape(-1)),
        "w_ret": slices([m[:, h * n:(h + 1) * n] for h in range(RH)
                         for m, n in ((rq, RDK), (rk, RDK), (rv, RDV), (rg, RDV))] + ret_out),
        "w_ret_out": slices(ret_out + ret_out_rest),
        "w_dn": slices([m[:, h * DK:(h + 1) * DK] for h in range(DH) for m in (dq, dk, dv, dz)] + [gb[:, :512]]),
        "w_dn_out": slices([gb[:, :512], p_dn[0][:, :512], gb[:, 512:], p_dn[0][:, 512:],
                            w_out[0][:, :512], w_out[0][:, 512:]]),
        "w_query": slices([peer_wq[0]]),
        "w_dn_ab": c(rows_in_chunks(np.concatenate([da, db], 1))),
        "dn_conv": c(dn_conv[0].reshape(CW, 3, DH, P).transpose(3, 2, 1, 0).reshape(P, DH, 3 * CW)),
        "dn_norm_g": c(dn_norm_g[0][:, None]), "dn_dt_bias": c(dn_dt_bias[0].reshape(-1)),
        "dn_a_log": c(dn_a_log[0].reshape(-1)),
        "ln1_g": c(ln1_g[0]), "ln1_b": c(ln1_b[0]),
        "peer_keys": c(peer_keys[0].transpose(3, 0, 1, 2).reshape(P, 2 * PH, NK)),
        "peer_u": c(peer_u[0].reshape(NK, NK, KC, P).transpose(1, 3, 2, 0)),
        "peer_v": c(peer_v[0].reshape(NK, NK, D).transpose(1, 0, 2)),
        "ln2_g": c(ln2_g[0]), "ln2_b": c(ln2_b[0]),
        **shape_constants(),
    }


def kernel(**inputs):
    import concourse.bacc as bacc
    from concourse.bass_utils import run_bass_kernel_spmd as run

    nc = bacc.Bacc("TRN2", target_bir_lowering=False, num_devices=1)
    arrays, a = {}, {}
    for name, array in laid_out(**{n: np.asarray(v) for n, v in inputs.items()}).items():
        arrays[f"in_{name}"] = array
        a[name] = nc.dram_tensor(f"in_{name}", array.shape, mybir.dt.from_np(array.dtype),
                                 kind="ExternalInput").ap()
    out = nc.dram_tensor("out_0", (SEQ, D), F32, kind="ExternalOutput").ap()
    program(nc, a, out)
    result = run(nc, [arrays], core_ids=[0])
    return result.results[0]["out_0"].reshape(1, SEQ, D)
```
